# Optimizing a Trainium2 kernel written in Bass

```python
import math
import jax, jax.numpy as jnp
from jax import lax
import numpy as np

D_MODEL = 1024
BATCH = 1
SEQ = 512
DEPTH = 1

MEM_LEN = 256
HEAD_DIM = 64
N_DIFF_HEADS = 4
DIFF_V_DIM = 2 * HEAD_DIM
N_FOX_HEADS = 8
N_MEM_HEADS = 4
MEM_HEAD_DIM = D_MODEL // N_MEM_HEADS
D_FF = 4 * D_MODEL
N_BUCKETS = 32
MAX_DISTANCE = 128
Q_BLOCK = 128
EPS = 1e-6

DIFF_QK_W = N_DIFF_HEADS * 2 * HEAD_DIM
DIFF_V_W = N_DIFF_HEADS * DIFF_V_DIM
FOX_W = N_FOX_HEADS * HEAD_DIM
IN_SPLITS = [DIFF_QK_W, DIFF_QK_W, DIFF_V_W, FOX_W, FOX_W, FOX_W, N_FOX_HEADS, D_MODEL, D_MODEL]
IN_COLS = int(sum(IN_SPLITS))
IN_OFFSETS = [int(v) for v in np.cumsum(IN_SPLITS)[:-1]]


def _rmsnorm(x, g):
    xf = x.astype(jnp.float32)
    y = xf * lax.rsqrt(jnp.mean(xf * xf, axis=-1, keepdims=True) + EPS)
    return (y * g.astype(jnp.float32)).astype(x.dtype)

def _split_heads(t, n_heads):
    b, s, _ = t.shape
    return t.reshape(b, s, n_heads, -1).transpose(0, 2, 1, 3)

def _merge_blocks(o):
    nb, b, h, qb, d = o.shape
    return o.transpose(1, 0, 3, 2, 4).reshape(b, nb * qb, h, d)

def _t5_bucket(dist):
    dist = jnp.maximum(dist, 0)
    max_exact = N_BUCKETS // 2
    d = jnp.maximum(dist, 1).astype(jnp.float32)
    large = max_exact + (jnp.log(d / max_exact) / math.log(MAX_DISTANCE / max_exact)
                         * (N_BUCKETS - max_exact)).astype(jnp.int32)
    large = jnp.minimum(large, N_BUCKETS - 1)
    return jnp.where(dist < max_exact, dist, large)

def _hybrid_mixer(h, w_in, b_forget, lq1, lk1, lq2, lk2, g_subln, rel_bias,
                  w_diff_out, w_fox_out, w_o, lambda_init):
    b, s, _ = h.shape
    proj = h @ w_in
    qa, ka, va, qb, kb, vb, fl, ga, gb = jnp.split(proj, IN_OFFSETS, axis=-1)

    qa = _split_heads(qa, 2 * N_DIFF_HEADS).reshape(b, N_DIFF_HEADS, 2, s, HEAD_DIM)
    ka = _split_heads(ka, 2 * N_DIFF_HEADS).reshape(b, N_DIFF_HEADS, 2, s, HEAD_DIM)
    qa1, qa2 = qa[:, :, 0], qa[:, :, 1]
    ka1, ka2 = ka[:, :, 0], ka[:, :, 1]
    va = _split_heads(va, N_DIFF_HEADS)
    lam = (jnp.exp(jnp.sum(lq1.astype(jnp.float32) * lk1.astype(jnp.float32)))
           - jnp.exp(jnp.sum(lq2.astype(jnp.float32) * lk2.astype(jnp.float32)))
           + lambda_init)

    qb = _split_heads(qb, N_FOX_HEADS)
    kb = _split_heads(kb, N_FOX_HEADS)
    vb = _split_heads(vb, N_FOX_HEADS)
    log_f = jax.nn.log_sigmoid(fl.astype(jnp.float32) + b_forget.astype(jnp.float32))
    cum = jnp.cumsum(log_f, axis=1).transpose(0, 2, 1)

    scale = HEAD_DIM ** -0.5
    table = rel_bias.astype(jnp.float32)
    k_pos = jnp.arange(s)

    def block(i):
        q0 = i * Q_BLOCK
        q_pos = q0 + jnp.arange(Q_BLOCK)
        dist = q_pos[:, None] - k_pos[None, :]
        causal = dist >= 0
        rel = jnp.transpose(table[_t5_bucket(dist)], (2, 0, 1))
        sl = lambda t: lax.dynamic_slice_in_dim(t, q0, Q_BLOCK, axis=2)
        s1 = jnp.einsum('bhqd,bhkd->bhqk', sl(qa1), ka1).astype(jnp.float32) * scale + rel
        s2 = jnp.einsum('bhqd,bhkd->bhqk', sl(qa2), ka2).astype(jnp.float32) * scale + rel
        a1 = jax.nn.softmax(jnp.where(causal, s1, -jnp.inf), axis=-1)
        a2 = jax.nn.softmax(jnp.where(causal, s2, -jnp.inf), axis=-1)
        oa = jnp.einsum('bhqk,bhkd->bhqd', (a1 - lam * a2).astype(va.dtype), va)
        c_q = lax.dynamic_slice_in_dim(cum, q0, Q_BLOCK, axis=2)
        sb = (jnp.einsum('bhqd,bhkd->bhqk', sl(qb), kb).astype(jnp.float32) * scale
              + (c_q[..., None] - cum[:, :, None, :]))
        pb = jax.nn.softmax(jnp.where(causal, sb, -jnp.inf), axis=-1)
        ob = jnp.einsum('bhqk,bhkd->bhqd', pb.astype(vb.dtype), vb)
        return oa, ob

    oa, ob = lax.map(block, jnp.arange(s // Q_BLOCK))
    ya = _rmsnorm(_merge_blocks(oa), g_subln) * (1.0 - lambda_init)
    ya = ya.reshape(b, s, DIFF_V_W)
    yb = _merge_blocks(ob).reshape(b, s, FOX_W)
    merged = jax.nn.sigmoid(ga) * (ya @ w_diff_out) + jax.nn.sigmoid(gb) * (yb @ w_fox_out)
    return merged @ w_o

def _memory_cross_attention(h, mem_n, w_q, w_kv, w_o):
    b, s, _ = h.shape
    q = _split_heads(h @ w_q, N_MEM_HEADS)
    k, v = jnp.split(mem_n @ w_kv, 2, axis=-1)
    k = _split_heads(k, N_MEM_HEADS)
    v = _split_heads(v, N_MEM_HEADS)
    sc = jnp.einsum('bhqd,bhkd->bhqk', q, k).astype(jnp.float32) * (MEM_HEAD_DIM ** -0.5)
    p = jax.nn.softmax(sc, axis=-1).astype(v.dtype)
    o = jnp.einsum('bhqk,bhkd->bhqd', p, v).transpose(0, 2, 1, 3).reshape(b, s, D_MODEL)
    return o @ w_o

def _sq_relu_mlp(h, w1, w2):
    a = jax.nn.relu(h @ w1)
    return (a * a) @ w2

def first_inputs(seed: int = 0) -> dict:
    key = jax.random.key(seed)
    ks = jax.random.split(key, 24)
    n = lambda k, shape, s: jax.random.normal(k, shape, jnp.float32) * s
    gain = lambda k, shape: 1.0 + 0.02 * jax.random.normal(k, shape, jnp.float32)
    L = DEPTH
    return {
        "x": n(ks[0], (BATCH, SEQ, D_MODEL), 1.0),
        "mem": n(ks[1], (BATCH, MEM_LEN, D_MODEL), 1.0),
        "w_in": n(ks[2], (L, D_MODEL, IN_COLS), D_MODEL ** -0.5),
        "b_forget": 3.0 + n(ks[3], (L, N_FOX_HEADS), 1.0),
        "lambda_q1": n(ks[4], (L, HEAD_DIM), 0.1),
        "lambda_k1": n(ks[5], (L, HEAD_DIM), 0.1),
        "lambda_q2": n(ks[6], (L, HEAD_DIM), 0.1),
        "lambda_k2": n(ks[7], (L, HEAD_DIM), 0.1),
        "g_subln": gain(ks[8], (L, DIFF_V_DIM)),
        "rel_bias": n(ks[9], (N_BUCKETS, N_DIFF_HEADS), 0.5),
        "w_diff_out": n(ks[10], (L, DIFF_V_W, D_MODEL), DIFF_V_W ** -0.5),
        "w_fox_out": n(ks[11], (L, FOX_W, D_MODEL), FOX_W ** -0.5),
        "w_o": n(ks[12], (L, D_MODEL, D_MODEL), D_MODEL ** -0.5),
        "g_mix": gain(ks[13], (L, D_MODEL)),
        "g_mem_q": gain(ks[14], (L, D_MODEL)),
        "g_mem_kv": gain(ks[15], (L, D_MODEL)),
        "w_q_mem": n(ks[16], (L, D_MODEL, D_MODEL), D_MODEL ** -0.5),
        "w_kv_mem": n(ks[17], (L, D_MODEL, 2 * D_MODEL), D_MODEL ** -0.5),
        "w_o_mem": n(ks[18], (L, D_MODEL, D_MODEL), D_MODEL ** -0.5),
        "g_mlp": gain(ks[19], (L, D_MODEL)),
        "w1": n(ks[20], (L, D_MODEL, D_FF), D_MODEL ** -0.5),
        "w2": n(ks[21], (L, D_FF, D_MODEL), D_FF ** -0.5),
        "g_final": gain(ks[22], (D_MODEL,)),
    }

def first_block(x, mem, w_in, b_forget, lambda_q1, lambda_k1, lambda_q2, lambda_k2, g_subln,
              rel_bias, w_diff_out, w_fox_out, w_o, g_mix, g_mem_q, g_mem_kv, w_q_mem,
              w_kv_mem, w_o_mem, g_mlp, w1, w2, g_final):
    for l in range(DEPTH):
        lambda_init = 0.8 - 0.6 * math.exp(-0.3 * l)
        x = x + _hybrid_mixer(_rmsnorm(x, g_mix[l]), w_in[l], b_forget[l], lambda_q1[l],
                              lambda_k1[l], lambda_q2[l], lambda_k2[l], g_subln[l], rel_bias,
                              w_diff_out[l], w_fox_out[l], w_o[l], lambda_init)
        x = x + _memory_cross_attention(_rmsnorm(x, g_mem_q[l]), _rmsnorm(mem, g_mem_kv[l]),
                                        w_q_mem[l], w_kv_mem[l], w_o_mem[l])
        x = x + _sq_relu_mlp(_rmsnorm(x, g_mlp[l]), w1[l], w2[l])
    return _rmsnorm(x, g_final)


DEPTH_2 = 2

N_EVEN = (DEPTH_2 + 1) // 2
N_ODD = DEPTH_2 // 2

XA_HEADS = 4
XA_HEAD_DIM = D_MODEL // XA_HEADS

POOL_W = D_MODEL // 2
POOL_WINDOWS = (2, 4, 8, 16)
N_POOL_GROUPS = len(POOL_WINDOWS)
POOL_GROUP = POOL_W // N_POOL_GROUPS
CONV_W = D_MODEL // 2
CONV_K = 31

MLA_HEADS = 16
QK_NOPE = 64
QK_ROPE = 32
V_HEAD = 64
Q_LORA = 384
KV_LORA = 256
ROPE_THETA = 10000.0
MLA_SCALE = 1.0 / math.sqrt(QK_NOPE + QK_ROPE)

D_FF_2 = 2816
FFN_CONV_K = 3

NEG = -1e30


def rmsnorm(x, g):
    xf = x.astype(jnp.float32)
    y = xf * lax.rsqrt(jnp.mean(xf * xf, axis=-1, keepdims=True) + EPS)
    return (y * g.astype(jnp.float32)).astype(x.dtype)

def layernorm(x, g, b):
    xf = x.astype(jnp.float32)
    mu = jnp.mean(xf, axis=-1, keepdims=True)
    xc = xf - mu
    y = xc * lax.rsqrt(jnp.mean(xc * xc, axis=-1, keepdims=True) + EPS)
    return (y * g.astype(jnp.float32) + b.astype(jnp.float32)).astype(x.dtype)

def causal_dwconv(u, w):
    k = w.shape[0]
    return lax.conv_general_dilated(
        u, w[:, None, :], window_strides=(1,), padding=[(k - 1, 0)],
        dimension_numbers=("NWC", "WIO", "NWC"), feature_group_count=u.shape[-1])

def window_mean_minus_self(u, w):
    t = u.shape[1]
    uf = u.astype(jnp.float32)
    cs = jnp.cumsum(uf, axis=1)
    cs_lag = jnp.pad(cs, ((0, 0), (w, 0), (0, 0)))[:, :t]
    cnt = jnp.minimum(jnp.arange(t) + 1, w).astype(jnp.float32)
    return ((cs - cs_lag) / cnt[None, :, None] - uf).astype(u.dtype)

def rope_tables(positions):
    inv = 1.0 / (ROPE_THETA ** (jnp.arange(0, QK_ROPE, 2, dtype=jnp.float32) / QK_ROPE))
    ang = positions.astype(jnp.float32)[..., None] * inv
    return jnp.cos(ang), jnp.sin(ang)

def apply_rope(x, cos, sin):
    half = x.shape[-1] // 2
    c = cos.astype(x.dtype)
    s = sin.astype(x.dtype)
    x1, x2 = x[..., :half], x[..., half:]
    return jnp.concatenate([x1 * c - x2 * s, x1 * s + x2 * c], axis=-1)

def pool_conv_mixer(h, w_in, pool_w, pool_scale, dw_w, dw_b, ln_g, ln_b, w_out):
    b, t, _ = h.shape
    z = h @ w_in
    u, glu_a, glu_b = jnp.split(z, [POOL_W, POOL_W + CONV_W], axis=-1)
    ug = u.reshape(b, t, N_POOL_GROUPS, POOL_GROUP)
    pooled = jnp.stack([window_mean_minus_self(ug[:, :, i], w)
                        for i, w in enumerate(POOL_WINDOWS)], axis=2)
    ya = jnp.einsum("btgc,gcd->btgd", pooled, pool_w).reshape(b, t, POOL_W) * pool_scale
    gl = glu_a * jax.nn.sigmoid(glu_b)
    cv = causal_dwconv(gl, dw_w) + dw_b
    yb = jax.nn.silu(layernorm(cv, ln_g, ln_b))
    return jnp.concatenate([ya, yb], axis=-1) @ w_out

def mla_attention(h, cos, sin, w_dq_dkv, q_norm_g, w_uq, kv_norm_g, w_ukv, w_o):
    b, t, _ = h.shape
    c = h @ w_dq_dkv
    cq, ckv, k_pe = jnp.split(c, [Q_LORA, Q_LORA + KV_LORA], axis=-1)
    q = (rmsnorm(cq, q_norm_g) @ w_uq).reshape(b, t, MLA_HEADS, QK_NOPE + QK_ROPE)
    q_nope = q[..., :QK_NOPE]
    q_pe = apply_rope(q[..., QK_NOPE:], cos[:, :, None, :], sin[:, :, None, :])
    kv = (rmsnorm(ckv, kv_norm_g) @ w_ukv).reshape(b, t, MLA_HEADS, QK_NOPE + V_HEAD)
    k_nope, v = kv[..., :QK_NOPE], kv[..., QK_NOPE:]
    k_pe = apply_rope(k_pe, cos, sin)
    nb = t // Q_BLOCK
    kpos = jnp.arange(t)

    def block(args):
        qn, qp, i = args
        s = (jnp.einsum("bqhd,bkhd->bhqk", qn, k_nope)
             + jnp.einsum("bqhr,bkr->bhqk", qp, k_pe)).astype(jnp.float32) * MLA_SCALE
        qpos = i * Q_BLOCK + jnp.arange(Q_BLOCK)
        s = jnp.where(kpos[None, :] <= qpos[:, None], s, NEG)
        p = jax.nn.softmax(s, axis=-1).astype(v.dtype)
        return jnp.einsum("bhqk,bkhd->bqhd", p, v)

    qn_b = q_nope.reshape(b, nb, Q_BLOCK, MLA_HEADS, QK_NOPE).transpose(1, 0, 2, 3, 4)
    qp_b = q_pe.reshape(b, nb, Q_BLOCK, MLA_HEADS, QK_ROPE).transpose(1, 0, 2, 3, 4)
    o = lax.map(block, (qn_b, qp_b, jnp.arange(nb)))
    o = o.transpose(1, 0, 2, 3, 4).reshape(b, t, MLA_HEADS * V_HEAD)
    return o @ w_o

def memory_cross_attention(h, m, wq, wkv, wo):
    b, t, _ = h.shape
    q = (h @ wq).reshape(b, t, XA_HEADS, XA_HEAD_DIM)
    k, v = jnp.split(m @ wkv, 2, axis=-1)
    k = k.reshape(b, MEM_LEN, XA_HEADS, XA_HEAD_DIM)
    v = v.reshape(b, MEM_LEN, XA_HEADS, XA_HEAD_DIM)
    s = jnp.einsum("bthd,bmhd->bhtm", q, k).astype(jnp.float32) * (XA_HEAD_DIM ** -0.5)
    p = jax.nn.softmax(s, axis=-1).astype(v.dtype)
    o = jnp.einsum("bhtm,bmhd->bthd", p, v).reshape(b, t, D_MODEL)
    return o @ wo

def conv_ffn(h, w_up, conv_w, conv_b, w_down):
    a, g = jnp.split(h @ w_up, 2, axis=-1)
    g = causal_dwconv(g, conv_w) + conv_b
    return (jax.nn.silu(g) * a) @ w_down

def second_inputs(seed: int = 0) -> dict:
    key = jax.random.key(seed)
    ks = iter(jax.random.split(key, 40))
    f32 = jnp.float32

    def dense(shape, fan_in, scale=1.0):
        return jax.random.normal(next(ks), shape, f32) * (scale * fan_in ** -0.5)

    def gain(shape):
        return 1.0 + 0.02 * jax.random.normal(next(ks), shape, f32)

    def bias(shape):
        return 0.01 * jax.random.normal(next(ks), shape, f32)

    out_scale = 0.5
    x = jax.random.normal(next(ks), (BATCH, SEQ, D_MODEL), f32)
    mem = jax.random.normal(next(ks), (BATCH, MEM_LEN, D_MODEL), f32)
    offsets = jax.random.randint(next(ks), (BATCH, 1), 0, 4096, dtype=jnp.int32)
    positions = offsets + jnp.arange(SEQ, dtype=jnp.int32)[None, :]
    return {
        "x": x,
        "mem": mem,
        "positions": positions,
        "norm_mix_g": gain((DEPTH_2, D_MODEL)),
        "norm_xa_g": gain((DEPTH_2, D_MODEL)),
        "norm_mem_g": gain((DEPTH_2, D_MODEL)),
        "xa_wq": dense((DEPTH_2, D_MODEL, D_MODEL), D_MODEL),
        "xa_wkv": dense((DEPTH_2, D_MODEL, 2 * D_MODEL), D_MODEL),
        "xa_wo": dense((DEPTH_2, D_MODEL, D_MODEL), D_MODEL, out_scale),
        "norm_ffn_g": gain((DEPTH_2, D_MODEL)),
        "ffn_w_up": dense((DEPTH_2, D_MODEL, 2 * D_FF_2), D_MODEL),
        "ffn_conv_w": dense((DEPTH_2, FFN_CONV_K, D_FF_2), FFN_CONV_K),
        "ffn_conv_b": bias((DEPTH_2, D_FF_2)),
        "ffn_w_down": dense((DEPTH_2, D_FF_2, D_MODEL), D_FF_2, out_scale),
        "pc_w_in": dense((N_EVEN, D_MODEL, POOL_W + 2 * CONV_W), D_MODEL),
        "pool_w": dense((N_EVEN, N_POOL_GROUPS, POOL_GROUP, POOL_GROUP), POOL_GROUP),
        "pool_scale": gain((N_EVEN, POOL_W)),
        "conv_dw_w": dense((N_EVEN, CONV_K, CONV_W), CONV_K),
        "conv_dw_b": bias((N_EVEN, CONV_W)),
        "conv_ln_g": gain((N_EVEN, CONV_W)),
        "conv_ln_b": bias((N_EVEN, CONV_W)),
        "pc_w_out": dense((N_EVEN, POOL_W + CONV_W, D_MODEL), POOL_W + CONV_W, out_scale),
        "mla_w_dq_dkv": dense((N_ODD, D_MODEL, Q_LORA + KV_LORA + QK_ROPE), D_MODEL),
        "mla_q_norm_g": gain((N_ODD, Q_LORA)),
        "mla_w_uq": dense((N_ODD, Q_LORA, MLA_HEADS * (QK_NOPE + QK_ROPE)), Q_LORA),
        "mla_kv_norm_g": gain((N_ODD, KV_LORA)),
        "mla_w_ukv": dense((N_ODD, KV_LORA, MLA_HEADS * (QK_NOPE + V_HEAD)), KV_LORA),
        "mla_w_o": dense((N_ODD, MLA_HEADS * V_HEAD, D_MODEL), MLA_HEADS * V_HEAD, out_scale),
        "final_norm_g": gain((D_MODEL,)),
    }

def second_block(x, mem, positions, norm_mix_g, norm_xa_g, norm_mem_g, xa_wq, xa_wkv, xa_wo,
              norm_ffn_g, ffn_w_up, ffn_conv_w, ffn_conv_b, ffn_w_down,
              pc_w_in, pool_w, pool_scale, conv_dw_w, conv_dw_b, conv_ln_g, conv_ln_b, pc_w_out,
              mla_w_dq_dkv, mla_q_norm_g, mla_w_uq, mla_kv_norm_g, mla_w_ukv, mla_w_o,
              final_norm_g):
    cos, sin = rope_tables(positions)
    for l in range(DEPTH_2):
        h = rmsnorm(x, norm_mix_g[l])
        if l % 2 == 0:
            e = l // 2
            x = x + pool_conv_mixer(h, pc_w_in[e], pool_w[e], pool_scale[e], conv_dw_w[e],
                                    conv_dw_b[e], conv_ln_g[e], conv_ln_b[e], pc_w_out[e])
        else:
            o = l // 2
            x = x + mla_attention(h, cos, sin, mla_w_dq_dkv[o], mla_q_norm_g[o], mla_w_uq[o],
                                  mla_kv_norm_g[o], mla_w_ukv[o], mla_w_o[o])
        x = x + memory_cross_attention(rmsnorm(x, norm_xa_g[l]), rmsnorm(mem, norm_mem_g[l]),
                                       xa_wq[l], xa_wkv[l], xa_wo[l])
        x = x + conv_ffn(rmsnorm(x, norm_ffn_g[l]), ffn_w_up[l], ffn_conv_w[l], ffn_conv_b[l],
                         ffn_w_down[l])
    return rmsnorm(x, final_norm_g)


def setup_inputs(seed=0):
    out = dict(first_inputs(seed))
    for name, value in second_inputs(seed + 1).items():
        if name != "x":
            out[name + "_2"] = value
    return out


def reference(
    x, mem, w_in, b_forget, lambda_q1, lambda_k1, lambda_q2, lambda_k2, g_subln, rel_bias,
    w_diff_out, w_fox_out, w_o, g_mix, g_mem_q, g_mem_kv, w_q_mem, w_kv_mem, w_o_mem, g_mlp, w1,
    w2, g_final, mem_2, positions_2, norm_mix_g_2, norm_xa_g_2, norm_mem_g_2, xa_wq_2, xa_wkv_2,
    xa_wo_2, norm_ffn_g_2, ffn_w_up_2, ffn_conv_w_2, ffn_conv_b_2, ffn_w_down_2, pc_w_in_2,
    pool_w_2, pool_scale_2, conv_dw_w_2, conv_dw_b_2, conv_ln_g_2, conv_ln_b_2, pc_w_out_2,
    mla_w_dq_dkv_2, mla_q_norm_g_2, mla_w_uq_2, mla_kv_norm_g_2, mla_w_ukv_2, mla_w_o_2,
    final_norm_g_2,
):
    x = first_block(
        x, mem, w_in, b_forget, lambda_q1, lambda_k1, lambda_q2, lambda_k2, g_subln, rel_bias,
        w_diff_out, w_fox_out, w_o, g_mix, g_mem_q, g_mem_kv, w_q_mem, w_kv_mem, w_o_mem, g_mlp,
        w1, w2, g_final,
    )
    return second_block(
        x, mem_2, positions_2, norm_mix_g_2, norm_xa_g_2, norm_mem_g_2, xa_wq_2, xa_wkv_2,
        xa_wo_2, norm_ffn_g_2, ffn_w_up_2, ffn_conv_w_2, ffn_conv_b_2, ffn_w_down_2, pc_w_in_2,
        pool_w_2, pool_scale_2, conv_dw_w_2, conv_dw_b_2, conv_ln_g_2, conv_ln_b_2, pc_w_out_2,
        mla_w_dq_dkv_2, mla_q_norm_g_2, mla_w_uq_2, mla_kv_norm_g_2, mla_w_ukv_2, mla_w_o_2,
        final_norm_g_2,
    )


_drawn_inputs = setup_inputs


def setup_inputs(seed=0):
    import zlib

    import numpy as np

    out = dict(_drawn_inputs(seed))
    spreads = {}
    factors = {'lambda_k1': 3.832,
     'lambda_q2': 4.063,
     'g_subln': 5.878,
     'g_mix': 3.012,
     'g_mem_q': 8.0,
     'g_mem_kv': 8.0,
     'g_mlp': 3.087,
     'norm_mix_g_2': 6.795,
     'norm_xa_g_2': 8.0,
     'norm_mem_g_2': 8.0,
     'norm_ffn_g_2': 5.169,
     'ffn_conv_b_2': 8.0,
     'pool_scale_2': 8.0,
     'conv_dw_b_2': 8.0,
     'conv_ln_g_2': 8.0,
     'conv_ln_b_2': 34.835,
     'mla_q_norm_g_2': 8.0,
     'mla_kv_norm_g_2': 8.0,
     'final_norm_g_2': 8.422}
    for name, (base, spread) in spreads.items():
        noise = np.random.default_rng([zlib.crc32(name.encode()), seed]).standard_normal(out[name].shape)
        drawn = base * np.exp(spread * noise) if base else spread * noise
        out[name] = __import__('jax').numpy.asarray(drawn.astype(out[name].dtype))
    for name, factor in factors.items():
        out[name] = (out[name] * factor).astype(out[name].dtype)
    return out
```

```python
from contextlib import ExitStack

import numpy as np

import concourse.bass as bass
from concourse import mybir

ALU = mybir.AluOpType
ACT = mybir.ActivationFunctionType
F32 = mybir.dt.float32
FR = mybir.dt.float32r
BF16 = mybir.dt.bfloat16
I32 = mybir.dt.int32
AX_X = mybir.AxisListType.X

P = 128
T = 512
TT = T // P
D = 1024
KD = D // P
MEM = 256
MT = MEM // P
EPS = 1e-6
NEG = -1e30
BLK = 2048

DIFF_HEADS = 4
FOX_HEADS = 8
XA_HEADS = 4
MLA_HEADS = 16
FF1, FF2 = 4096, 2816
CONV_K = 31
WINDOWS = (2, 4, 8, 16)


def t5_bucket(d):
    if d < 16:
        return d
    return min(31, 16 + int(np.log(d / 16.0) / np.log(8.0) * 16 + 1e-9))


def constants():
    keep = np.zeros((P, P + 66), np.float32)
    keep[:, :P] = np.eye(P)
    for g, w in enumerate(WINDOWS):
        keep[:, P + 16 * g:P + 16 * g + 16] = 1.0 / np.minimum(np.arange(16) + 1, w)
    inv = 1.0 / (10000.0 ** (np.arange(0, 32, 2, dtype=np.float32) / 32))
    keep[64:80, P + 64] = inv
    keep[80:96, P + 64] = inv
    keep[64:80, P + 65] = -1.0
    keep[80:96, P + 65] = 1.0
    once = np.zeros((P, 2 * P + 512), np.float32)
    once[:, :P] = np.eye(P)[::-1]
    once[:, P:2 * P] = np.where(np.arange(P)[None, :] > np.arange(P)[:, None], NEG, 0.0)
    for m in range(512):
        once[t5_bucket(511 - m), 2 * P + m] = 1.0
    return keep, once


class Ring:

    def __init__(self):
        self.who = []
        self.base = {}

    def add(self, name, who):
        self.base[name] = len(self.who)
        self.who += list(who)

    def done(self, g):
        return self.who[g], self.who[:g + 1].count(self.who[g])


def lin(f, i):
    if i is None:
        return f(0)
    if isinstance(i, int):
        return f(i)
    by = f(2) - f(1)
    assert f(3) - f(2) == by
    return i * by + (f(1) - by)


def attention_events(name, heads, lag, extra):
    ev = []
    n = heads * TT
    pending = []
    for step in range(n + lag):
        if step < n:
            h, i = divmod(step, TT)
            if i == 0 and "K" in extra:
                ev.append(("K", h, 0))
            ev.append(("S", h, i))
        if pending and pending[0][0] <= step:
            h = pending.pop(0)[1]
            ev.append(("V", h, 0))
            if "M" in extra:
                ev.append(("M", h, 0))
        if step >= lag:
            h, i = divmod(step - lag, TT)
            ev.append(("T", h, i))
            if i == TT - 1:
                pending.append((step + 1, h))
    for _, h in pending:
        ev.append(("V", h, 0))
        if "M" in extra:
            ev.append(("M", h, 0))
    return ev


class Plan:

    def __init__(self):
        self.L = Ring()
        self.S = Ring()
        self.blocks = []
        self.block_end = []
        self.block_base = {}
        self.events = {}

    def weights(self, name, src, nk, cols, places, groups_each):
        self.block_base[name] = len(self.blocks)
        for n, (r, c) in enumerate(places):
            self.blocks.append((src, nk, cols, r, c))
            self.block_end.append(self.L.base[name] + (n + 1) * groups_each)


def make_plan():
    p = Plan()
    L, S = p.L, p.S
    S.add("vecs", "vvvv")
    S.add("table", "v")
    L.add("x_in", "v" * KD)
    norm = [0]

    def feat(name, src, who, cols, row=0, nk=8, width=256, chunk=P):
        per = width // chunk
        L.add(name, who * (per * len(cols)))
        p.weights(name, src, nk, width, [(row, c) for c in cols], per)

    def a_norm():
        S.add(f"norm{norm[0]}", "a")
        norm[0] += 1

    a_norm()
    feat("qk_a", "w_in", "a", [0, 256, 512, 768])
    S.add("flip", "vvvv")
    feat("qk_b", "w_in", "a", [1536, 1792, 2048, 2304])
    L.add("v_ab", "a" * 16)
    p.weights("v_ab", "w_in", 8, 256, [(0, c) for c in (1024, 1280, 2560, 2816)], 4)
    S.add("forget", "v")
    S.add("cum", "v")

    def attention(name, heads, lag, score_who, per_score, t_who="a", v_who="v", v_groups=1, extra=""):
        ev = attention_events(name, heads, lag, extra)
        at = {}
        for kind, h, i in ev:
            if kind == "S":
                at[kind, h, i] = len(S.who)
                S.who += [score_who] * per_score
            elif kind == "K":
                at[kind, h, i] = len(S.who)
                S.who += ["v"]
            elif kind == "M":
                at[kind, h, i] = len(S.who)
                S.who += ["a"]
            elif kind == "T":
                at[kind, h, i] = len(L.who)
                L.who += [t_who]
            elif kind == "V":
                at[kind, h, i] = len(L.who)
                L.who += [v_who] * v_groups
        p.events[name] = (ev, at)

    attention("diff", DIFF_HEADS, 3, "v", 2, extra="M")

    def gates(tag, col, out):
        for half in (0, 1):
            feat(f"gate_{tag}{half}", "w_in", "a", [col + 512 * half, col + 512 * half + 256])
            feat(f"proj_{tag}{half}", out, "v", [512 * half], nk=4, width=512)

    gates("a", 3080, "w_diff_out")
    attention("fox", FOX_HEADS, 3, "v", 1, extra="K")
    gates("b", 4104, "w_fox_out")
    feat("w_o", "w_o", "v", [0, 256, 512, 768])

    def keys(c, wkv):
        L.add(f"memT{c}", "vvvv")
        feat(f"xk{c}", wkv, "a", [0, 256, 512, 768])

    def values(c, wkv, j):
        L.add(f"xv{c}{j}", "aa")
        p.weights(f"xv{c}{j}", wkv, 8, 256, [(0, D + 256 * j)], 2)

    def cross(c, wq, wkv, wo):
        if c != 1:
            keys(c, wkv)
        a_norm()
        for j in range(2 if c == 1 else 0, 4):
            values(c, wkv, j)
        feat(f"xq{c}", wq, "a", [0, 256, 512, 768])
        attention(f"xa{c}", XA_HEADS, 3, "a", 1, v_groups=2)
        feat(f"xo{c}", wo, "v", [0, 256, 512, 768])

    cross(0, "w_q_mem", "w_kv_mem", "w_o_mem")

    a_norm()

    def mlp(name, nf, up, up_who, down, second=None):
        L.base[name] = len(L.who)
        p.block_base[name] = len(p.blocks)

        def put(src, nk, cols, r, c, who):
            L.who.extend(who)
            p.blocks.append((src, nk, cols, r, c))
            p.block_end.append(len(L.who))

        def ups(f):
            for s, c0, who in up:
                put(s, 8, 256, 0, c0 + 256 * f, who * 2)

        ups(0)
        for f in range(nf):
            if f + 1 < nf:
                ups(f + 1)
            put(down, 2, 1024, 256 * f, 0, "v" * 8)
        L.base[name + "_last"] = len(L.who) - 8

    mlp("mlp", FF1 // 256, [("w1", 0, "a")], "a", "w2")
    a_norm()
    a_norm()
    feat("pool_u", "pc_w_in_2", "a", [0, 256])
    feat("glu", "pc_w_in_2", "a", [512, 1024, 768, 1280])
    L.add("pool_w", "vvvv")
    feat("pc_out_a", "pc_w_out_2", "v", [0, 512], nk=4, width=512)
    keys(1, "xa_wkv_2:0")
    S.add("ln_mean", "v")
    S.add("ln_var", "a")
    values(1, "xa_wkv_2:0", 0)
    values(1, "xa_wkv_2:0", 1)
    feat("pc_out_b", "pc_w_out_2", "v", [0, 512], row=512, nk=4, width=512)
    cross(1, "xa_wq_2:0", "xa_wkv_2:0", "xa_wo_2:0")
    a_norm()
    mlp("ffn0", FF2 // 256, [("ffn_w_up_2:0", FF2, "a"), ("ffn_w_up_2:0", 0, "v")], None, "ffn_w_down_2:0")
    a_norm()
    feat("dq", "mla_w_dq_dkv_2", "v", [0, 256])
    L.add("dq2", "vv")
    p.weights("dq2", "mla_w_dq_dkv_2", 8, 160, [(0, 512)], 2)
    S.add("c_norm", "aa")
    for half in (0, 1):
        for j in (0, 1):
            L.add(f"uq{half}{j}", "v" * 4)
            p.weights(f"uq{half}{j}", "mla_w_uq_2", 3, 384, [(0, 768 * half + 384 * j)], 4)
        L.add(f"uk{half}", "a" * 12)
        p.weights(f"uk{half}", "mla_w_ukv_2", 2, 1024, [(0, 1024 * half)], 12)
        attention(f"mla{half}", 8, 3, "a", 1)
    feat("mla_o", "mla_w_o_2", "v", [0, 256, 512, 768])
    cross(2, "xa_wq_2:1", "xa_wkv_2:1", "xa_wo_2:1")
    a_norm()
    mlp("ffn1", FF2 // 256, [("ffn_w_up_2:1", FF2, "a"), ("ffn_w_up_2:1", 0, "v")], None, "ffn_w_down_2:1")
    a_norm()
    L.add("out", "a" * 8)
    p.norms = norm[0]
    return p


LAMBDA_INIT = 0.8 - 0.6 * 1.0
ROUND = 12582912.0
TWO_PI = (6.28125, 2029 * 2.0 ** -20, 2 * np.pi - 6.28125 - 2029 * 2.0 ** -20)
PI32 = 3.1415925
TAPS = 4 * CONV_K
U = {"diff": 0, "fox": 16, "xa0": 48, "xa1": 64, "mla0": 80, "mla1": 112, "xa2": 144}
NM = {"diff": 0, "fox": 32, "xa0": 64, "xa1": 80, "mla0": 96, "mla1": 128, "xa2": 160}
OH = {"diff": 0, "fox": 4, "xa0": 12, "xa1": 20, "mla0": 28, "mla1": 36, "xa2": 44}
UPB = {"mlp": 0, "ffn0": 32, "ffn1": 54}
CB = {"ffn0": 0, "ffn1": 22}


def n_base(k):
    return 8 * k - (8 if k > 3 else 0)


VECTORS = [
    ("g_mix", D), ("g_mem_q", D), ("g_mem_kv", D), ("g_mlp", D), ("norm_mix_g_2", 2 * D),
    ("norm_xa_g_2", 2 * D), ("norm_mem_g_2", 2 * D), ("norm_ffn_g_2", 2 * D), ("g_final", D),
    ("final_norm_g_2", D), ("ffn_conv_b_2", 2 * FF2), ("ffn_conv_w_2", 6 * FF2),
    ("conv_dw_w_2", CONV_K * 512), ("conv_dw_b_2", 512), ("conv_ln_g_2", 512), ("conv_ln_b_2", 512),
    ("pool_scale_2", 512), ("mla_q_norm_g_2", 384), ("mla_kv_norm_g_2", 256), ("g_subln", 128),
]


def vector_columns():
    at, n = {}, 0
    for name, size in VECTORS:
        at[name] = n
        n += size // P
    return at, n


def build(nc, A, out):
    plan = make_plan()
    L, S = plan.L, plan.S
    COL, NCOL = vector_columns()
    VT = -(-NCOL // P)
    keep_np, once_np = constants()
    keep_d = nc.inline_tensor(keep_np, "keep_constants").ap()
    once_d = nc.inline_tensor(once_np, "start_constants").ap()
    scratch = nc.dram_tensor("bias_rows", (DIFF_HEADS, 640), F32, kind="Internal").ap()

    def flat(name):
        a = A[name]
        n = len(a.shape)
        if n == 1:
            return a
        if n == 2:
            return a.rearrange("a b -> (a b)")
        return a.rearrange("a b c -> (a b c)")

    def weight(name):
        name, _, layer = name.partition(":")
        a = A[name]
        return a[int(layer or 0)] if len(a.shape) == 3 else a

    with ExitStack() as ctx:
        def sb(name, shape, dt=F32):
            return ctx.enter_context(nc.sbuf_tensor(name, shape, dt))

        def sem(name):
            return ctx.enter_context(nc.semaphore(name))

        x = sb("x_T", [P, KD, T])
        A_hi, A_lo = sb("a_hi", [P, KD, T], FR), sb("a_lo", [P, KD, T], FR)
        B_hi, B_lo = sb("b_hi", [P, 4, T], FR), sb("b_lo", [P, 4, T], FR)
        w_raw = sb("w_raw", [P, 2, BLK])
        w_hi, w_lo = sb("w_hi", [P, 2, BLK], FR), sb("w_lo", [P, 2, BLK], FR)
        keep = sb("keep", [P, P + 66])
        ident = keep[:, 0:P]
        cols = sb("cols", [P, VT * P])
        ident_bf, mask_bf = sb("ident_bf", [P, P], BF16), sb("mask_bf", [P, P], BF16)
        avg = {n: sb(f"avg{n}", [P, P]) for n in (1024, 512, 384, 256, 128)}
        small = sb("small", [P, 64])
        eps_col, lam_neg, lam_t = small[:, 0:1], small[:, 1:2], small[:, 2:8]
        bf_col, g08 = sb("forget_bias", [8, 1])[:, :], small[:, 9:10]
        mem_s = small[:, 10:16]
        mx, nm, ls, rl = small[:, 16:24], small[:, 24:32], small[:, 32:40], small[:, 40:48]
        warm = small[:, 48:64]
        ck8 = sb("ck8", [P, TT * 8])[:, :]
        GKV = (COL["g_mem_kv"], COL["norm_mem_g_2"], COL["norm_mem_g_2"] + 8)
        GAIN = [COL["g_mix"], COL["g_mem_q"], COL["g_mlp"], COL["g_final"], COL["norm_mix_g_2"],
                COL["norm_xa_g_2"], COL["norm_ffn_g_2"], COL["norm_mix_g_2"] + 8, COL["norm_xa_g_2"] + 8,
                COL["norm_ffn_g_2"] + 8, COL["final_norm_g_2"]]
        wf_raw = sb("wf_raw", [P, KD, 8])
        wf_hi, wf_lo = sb("wf_hi", [P, KD, 8], FR), sb("wf_lo", [P, KD, 8], FR)
        arena = sb("arena", [P, 22016])

        def ar(off, *shape):
            n = int(np.prod(shape))
            assert off + n <= 22016
            v = arena[:, off:off + n]
            if len(shape) == 2:
                v = v.rearrange("p (a b) -> p a b", a=shape[0])
            return v

        sq, acc, rst, h32 = ar(0, 2, T), ar(1024, T), ar(1536, T), ar(2048, 2, T)
        s_buf = ar(0, 8, T)
        PT_OFF = [0, 512, 896, 1152]

        def pt(h, k, q0, n):
            o = 4096 + 1280 * (h % 2) + PT_OFF[k] + q0 - P * k
            return arena[:, o:o + n]

        R0 = 6656
        qa, ka, va = ar(R0, 4, T), ar(R0 + 2048, 4, T), ar(R0 + 4096, 4, T)
        qb, kb, vb = ar(R0 + 6144, 4, T), ar(R0 + 8192, 4, T), ar(R0 + 10240, 4, T)
        bias8, nck = ar(R0 + 12288, 4, T), ar(R0 + 14336, 2, T)
        merged, sg = ar(R0, 8, T), ar(R0 + 4096, 4, T)
        x_st = ar(R0, TT, D)
        once = ar(R0 + 4096, 768)
        v_st = ar(R0 + 4864, 4, P)
        rel = arena[0:32, R0 + 5376:R0 + 5380]
        lams = ar(R0 + 5400, 4, 64)
        rrow = arena[0:4, R0 + 5700:R0 + 6340]
        bias_up = ar(4096, 4, T)
        fz, fm, fe, flg, fone, fmin = (arena[0:8, o:o + T] for o in (0, 512, 1024, 1536, 2048, 2560))
        cum = sb("cum", [8, T])[:, :]
        kT, qT, vM = ar(R0 + 2168, 8, MEM), ar(R0 + 4280, 8, T), ar(R0 + 8952, 2, D)
        mem_st, mem_junk = ar(R0 + 6328, 2, D), ar(R0 + 11512, D)
        p_x = ar(0, 4, MEM)

        def ptx(h, m, q0, n):
            o = 4096 + 1024 * (h % 2) + 512 * m + q0
            return arena[:, o:o + n]

        r32, f32 = ar(R0, 2, T), ar(R0 + 1024, 2, T)
        gp = ar(R0 + 2048, 2, T + 2)
        cv, sl = ar(R0 + 3200, 2, T), ar(R0 + 4224, 2, T)
        GW, UW = T + CONV_K - 1, T + 16
        gl, up_ = ar(R0, 4, GW), ar(R0 + 2168, 4, UW)
        cvt, sgb = ar(R0 + 4280, 4, T), ar(R0 + 6328, 2, T)
        pw_a, pw_b = ar(R0 + 7352, UW), ar(R0 + 7880, UW)
        pooled = ar(R0 + 8408, 4, T)
        pool_wt = ar(R0 + 10456, 4, P)
        ptmp = ar(R0 + 10968, 16)
        lmu, lrs, ly = ar(R0 + 11000, T), ar(R0 + 12536, T), ar(R0 + 13048, 4, T)
        qh, kh, vh = ar(R0, 8, T), ar(R0 + 4096, 8, T), ar(R0 + 8192, 4, T)
        cosT, sinT = ar(R0 + 10240, T), ar(R0 + 10752, T)
        kpe, rop, rsh = ar(R0 + 11264, T), ar(R0 + 11776, 2, T), ar(R0 + 12800, 2, T)
        cc = ar(R0, 5, T)
        posi = arena[:, R0 + 4096:R0 + 4608].bitcast(I32)
        ang, nrn = ar(R0 + 4608, T), ar(R0 + 5120, T)
        cacc = ar(R0 + 5632, 2, T)
        crst = ar(R0 + 6656, 2, T)
        o_st = ar(R0, TT, D)

        ps_l = [ctx.enter_context(nc.psum_tensor(f"ps_l{i}", [P, T], F32)) for i in range(4)]
        ps_s = [ctx.enter_context(nc.psum_tensor(f"ps_s{i}", [P, T], F32)) for i in range(4)]

        ld_keep, ld_once, ld_vec, ld_x, ld_small = (sem(s) for s in ("ld_keep", "ld_once", "ld_vec", "ld_x", "ld_small"))
        ld_bias, ld_mem, ld_pw, ld_pos, st_out = (sem(s) for s in ("ld_bias", "ld_mem", "ld_pw", "ld_pos", "st_out"))
        w_loaded = [sem("w_loaded0"), sem("w_loaded1")]
        w_hi_made, w_lo_made = sem("w_hi_made"), sem("w_lo_made")
        l_full, s_full = sem("l_full"), sem("s_full")
        l_free = {"v": sem("l_free_v"), "a": sem("l_free_a")}
        s_free = {"v": sem("s_free_v"), "a": sem("s_free_a")}
        n_sq, n_acc, n_rstd, n_h, n_hi, n_lo = (sem(s) for s in ("n_sq", "n_acc", "n_rstd", "n_h", "n_hi", "n_lo"))
        setup_v, setup_a, v_step, a_step = sem("setup_v"), sem("setup_a"), sem("v_step"), sem("a_step")
        u_nm, u_exp, u_p = sem("neg_max_ready"), sem("exp_done"), sem("probs_ready")
        o_hi = sem("o_hi")
        sub_sq, sub_rs, sub_lo = sem("sub_sq"), sem("sub_rs"), sem("sub_lo")
        forget_m, forget_l, cum_ready = sem("forget_m"), sem("forget_l"), sem("cum_ready")
        sg_ready, m_ready, m_hi, m_lo = sem("sg_ready"), sem("merged_ready"), sem("m_hi"), sem("m_lo")
        mem_ss, mem_rs, mem_sc, mem_hi, mem_lo = (sem(s) for s in ("mem_ss", "mem_rs", "mem_sc", "mem_hi", "mem_lo"))
        up_act, up_f, up_hi, up_lo = (sem(s) for s in ("up_act", "up_f", "up_hi", "up_lo"))
        g_conv = sem("g_conv")
        glu_sg, glu_r, tap, pool_r, ya_hi, ya_lo = (sem(s) for s in ("glu_sg", "glu_r", "tap", "pool_r", "ya_hi", "ya_lo"))
        ln_v, ln_sq, ln_rs, ln_y, ln_s, yb_hi, yb_lo = (sem(s) for s in ("ln_v", "ln_sq", "ln_rs", "ln_y", "ln_s", "yb_hi", "yb_lo"))
        ang_r, sincos, c_sq, c_acc, c_rs, c_h, c_hi, c_lo = (
            sem(s) for s in ("ang_r", "sincos", "c_sq", "c_acc", "c_rs", "c_h", "c_hi", "c_lo"))
        rope_k, rope_q, kpe_put = sem("rope_k"), sem("rope_q"), sem("kpe_put")

        n_vec_dmas = sum((COL[v] + n // P - 1) // P - COL[v] // P + 1 for v, n in VECTORS)

        def wait_group(e, ring, g, i=None, dg=0):
            e.wait_ge(l_full if ring is L else s_full, lin(lambda r: g + 1 + r * dg, i))

        def wait_read(e, ring, g, i=None, dg=0):
            free = l_free if ring is L else s_free
            who = ring.who[g if i is None else g + dg * (i if isinstance(i, int) else 1)]
            e.wait_ge(free[who], lin(lambda r: ring.done(g + r * dg)[1], i))

        def claim(e, ring, g, i=None, dg=0):
            if g >= 4:
                wait_read(e, ring, g - 4, i, dg)

        def bank(ring, g):
            return (ps_l if ring is L else ps_s)[g % 4]

        def freed(ring, who):
            return (l_free if ring is L else s_free)[who]

        def wview(t, slot, nk, c):
            return t[:, slot, 0:nk * c].rearrange("p (k c) -> p k c", k=nk)

        NB = len(plan.blocks)

        def rep(e, n, body):
            body(0)
            with e.Fori(1, n - 1) as i:
                body(i)
            body(n - 1)

        block = ctx.enter_context(nc.Block())

        @block.sync
        def _(sp):
            sp.dma_start(keep[:, :], keep_d).then_inc(ld_keep, 16)
            sp.dma_start(once, once_d).then_inc(ld_once, 16)
            sp.dma_start(x_st, A["x"][0].rearrange("(t p) d -> p t d", p=P)).then_inc(ld_x, 16)
            n_small = 0
            with nc.allow_non_contiguous_dma(reason="a few bytes of each"):
                sp.dma_start(rel, A["rel_bias"]).then_inc(ld_small, 16)
                for j, nme in enumerate(("lambda_q1", "lambda_k1", "lambda_q2", "lambda_k2")):
                    sp.dma_start(lams[:, j, :], A[nme].to_broadcast([P, 64])).then_inc(ld_small, 16)
                sp.dma_start(bf_col, A["b_forget"].rearrange("a h -> h a")).then_inc(ld_small, 16)
                sp.dma_start(wf_raw[:, :, :], weight("w_in")[:, 3072:3080].rearrange("(k p) n -> p k n", p=P))\
                    .then_inc(ld_small, 16)
            n_vec = 0
            for name, size in VECTORS:
                v = flat(name).rearrange("(r p) -> r p", p=P)
                r, n = COL[name], size // P
                done = 0
                while done < n:
                    m = min(n - done, P - (r + done) % P)
                    q = (r + done) % P
                    sp.dma_start(v_st[q:q + m, (r + done) // P, :], v[done:done + m, :]).then_inc(ld_vec, 16)
                    done += m

            def load_block(b):
                src, nk, c, r0, c0 = plan.blocks[b]
                if b >= 2:
                    sp.wait_ge(w_hi_made, b - 1)
                    sp.wait_ge(w_lo_made, b - 1)
                w = weight(src)[r0:r0 + nk * P, c0:c0 + c].rearrange("(k p) c -> p k c", p=P)
                sp.dma_start(wview(w_raw, b % 2, nk, c), w).then_inc(w_loaded[b % 2], 16)

            def load_mem(c):
                m = A["mem"] if c == 0 else A["mem_2"]
                sp.dma_start(mem_st, m[0].rearrange("(t p) d -> p t d", p=P)).then_inc(ld_mem, 16)

            load_block(0)
            load_block(1)
            sp.wait_ge(setup_v, 3)
            wait_read(sp, S, S.base["table"])
            sp.dma_start(scratch, rrow).then_inc(ld_bias, 16)
            sp.wait_ge(ld_bias, 16)
            for h in range(DIFF_HEADS):
                sp.dma_start(bias_up[:, h, :], bass.AP(scratch.tensor, h * 640, [[1, P], [1, T]]))\
                    .then_inc(ld_bias, 16)
            BB = plan.block_base

            def load_range(b0, b1):
                for b in range(max(2, b0), b1):
                    load_block(b)

            load_range(0, BB["proj_b0"])
            wait_group(sp, L, plan.events["fox"][1]["V", FOX_HEADS - 1, 0])
            load_mem(0)
            load_range(BB["proj_b0"], BB["mlp"] + 3)
            wait_group(sp, L, L.base["mlp"])
            sp.dma_start(pool_wt, A["pool_w_2"][0].rearrange("g p d -> p g d")).then_inc(ld_pw, 16)
            load_range(BB["mlp"] + 3, BB["pc_out_a"] + 1)
            wait_group(sp, L, L.base["pool_w"] + 3)
            sp.wait_ge(glu_r, 4)
            load_mem(1)
            load_range(BB["pc_out_a"] + 1, BB["dq"] + 2)
            wait_read(sp, L, L.base["dq"] - 1)
            sp.dma_start(posi[64:96, :], A["positions_2"].to_broadcast([32, T])).then_inc(ld_pos, 16)
            load_range(BB["dq"] + 2, BB["mla_o"] + 2)
            wait_group(sp, L, plan.events["mla1"][1]["V", 7, 0])
            load_mem(2)
            load_range(BB["mla_o"] + 2, NB)
            for j in range(8):
                wait_read(sp, L, L.base["out"] + j)
                sp.dma_start(out[0].rearrange("(t p) d -> p t d", p=P)[:, :, j * P:(j + 1) * P],
                             o_st[:, :, j * P:(j + 1) * P]).then_inc(st_out, 16)
            sp.wait_ge(st_out, 16 * 8)

        @block.gpsimd
        def _(pool):
            def low(b):
                pool.wait_ge(w_hi_made, b + 1)
                if b >= 2:
                    pool.wait_ge(l_full, plan.block_end[b - 2])
                pool.tensor_tensor(w_lo[:, b % 2, :], w_raw[:, b % 2, :], w_hi[:, b % 2, :].bitcast(F32),
                                   ALU.subtract).then_inc(w_lo_made, 1)

            for b in range(NB):
                low(b)

        @block.tensor
        def _(pe):
            def mm3(o, wh, wl, xh, xl, first, last, swap=False):
                for n, (w, v) in enumerate(((wh, xh), (wh, xl), (wl, xh))):
                    ins = pe.matmul(o, *((v, w) if swap else (w, v)), start=first and n == 0,
                                    stop=last and n == 2)
                return ins

            def wait_block(b, i=None, db=0):
                pe.wait_ge(w_lo_made, lin(lambda r: b + 1 + r * db, i))

            def feat(b, g, nk, c, xs, ready=None, i=None, db=0, dg=0, n=T, chunks=None):
                wait_block(b, i, db)
                h, l = wview(w_hi, b % 2, nk, c), wview(w_lo, b % 2, nk, c)
                chunks = chunks or [(P * q, P) for q in range(c // P)]

                def product(j, k):
                    c0, m = chunks[j]
                    xh, xl = xs(k)
                    ins = mm3(bank(L, g + j)[0:m, 0:n], h[:, k, c0:c0 + m], l[:, k, c0:c0 + m], xh, xl,
                              k == 0, k == nk - 1)
                    if k == nk - 1:
                        ins.then_inc(l_full, 1)

                if ready:
                    for j in range(len(chunks)):
                        claim(pe, L, g + j, i, dg)
                    for k in range(nk):
                        ready(k)
                        for j in range(len(chunks)):
                            product(j, k)
                else:
                    for j in range(len(chunks)):
                        claim(pe, L, g + j, i, dg)
                        for k in range(nk):
                            product(j, k)

            def tok(b, g, nk, c, xs, tiles):
                wait_block(b)
                h, l = wview(w_hi, b % 2, nk, c), wview(w_lo, b % 2, nk, c)
                for t in range(tiles):
                    claim(pe, L, g + t)
                    for k in range(nk):
                        xh, xl = xs(k)
                        q = slice(t * P, (t + 1) * P)
                        ins = mm3(bank(L, g + t)[:, 0:c], h[:, k, :], l[:, k, :], xh[:, q], xl[:, q],
                                  k == 0, k == nk - 1, swap=True)
                    ins.then_inc(l_full, 1)

            def xa(k):
                return A_hi[:, k, :], A_lo[:, k, :]

            def xb(k):
                return B_hi[:, k, :], B_lo[:, k, :]

            def xm(k):
                o = slice(MEM * (k % 2), MEM * (k % 2) + MEM)
                return B_hi[:, k // 2, o], B_lo[:, k // 2, o]

            def norm(k):
                g = S.base[f"norm{k}"]
                claim(pe, S, g)
                pe.wait_ge(n_acc, 7 * (k + 1))
                pe.matmul(bank(S, g)[:, :], avg[1024][:, :], acc, start=True, stop=True).then_inc(s_full, 1)

            def h_ready(k):
                return lambda c: pe.wait_ge(n_lo, n_base(k) + c + 1)

            def stage(name, xs, nk=8, c=256, nb=4, ready=None, n=T):
                b, g = plan.block_base[name], L.base[name]
                per = c // P
                for j in range(nb):
                    feat(b + j, g + per * j, nk, c, xs, ready if j == 0 else None, n=n)

            def turn(o, v):
                return pe.transpose(o, v, ident)

            pe.wait_ge(ld_keep, 16)
            pe.wait_ge(ld_vec, 16 * n_vec_dmas)
            g = S.base["vecs"]
            for t in range(VT):
                m = min(P, NCOL - t * P)
                pe.transpose(bank(S, g + t)[:, 0:m], v_st[0:m, t, :], ident[0:m, 0:m]).then_inc(s_full, 1)
            g = S.base["table"]
            pe.wait_ge(ld_small, 16 * 7)
            pe.wait_ge(ld_once, 16)
            claim(pe, S, g)
            pe.matmul(bank(S, g)[0:4, :], rel, once[0:32, 256:768], start=True, stop=True).then_inc(s_full, 1)
            pe.wait_ge(ld_x, 16)
            g = L.base["x_in"]
            for c in range(KD):
                claim(pe, L, g + c)
                for t in range(TT):
                    ins = turn(bank(L, g + c)[:, t * P:(t + 1) * P], x_st[:, t, c * P:(c + 1) * P])
                ins.then_inc(l_full, 1)
            norm(0)
            stage("qk_a", xa, ready=h_ready(0))
            g = S.base["flip"]
            pe.wait_ge(ld_bias, 16 * 5)
            for h in range(DIFF_HEADS):
                claim(pe, S, g + h)
                pe.matmul(bank(S, g + h)[:, :], once[:, 0:P], bias_up[:, h, :], start=True, stop=True)\
                    .then_inc(s_full, 1)
            stage("qk_b", xa)
            b, g = plan.block_base["v_ab"], L.base["v_ab"]
            for j in range(4):
                tok(b + j, g + 4 * j, 8, 256, xa, TT)
            g = S.base["forget"]
            claim(pe, S, g)
            pe.wait_ge(setup_v, 5)
            for k in range(KD):
                ins = mm3(bank(S, g)[0:8, :], wf_hi[:, k, :], wf_lo[:, k, :], A_hi[:, k, :], A_lo[:, k, :],
                          k == 0, k == KD - 1)
            ins.then_inc(s_full, 1)
            g = S.base["cum"]
            claim(pe, S, g)
            pe.wait_ge(cum_ready, 1)
            for t in range(TT):
                ins = pe.transpose(bank(S, g)[:, 8 * t:8 * t + 8], cum[:, t * P:(t + 1) * P], ident[0:8, 0:8])
            ins.then_inc(s_full, 1)

            def attention(name, score, values, before=None, turned=None, subln=None, keys=None):
                ev, at = plan.events[name]
                for kind, h, i in ev:
                    g = at[kind, h, i]
                    if kind == "K":
                        keys(g, h)
                    if kind == "S":
                        score(g, h, i)
                    if kind == "T":
                        turned(g, h, i)
                    if kind == "V":
                        values(g, h)
                    if kind == "M":
                        subln(g, h)

            def causal_turn(ubase, buf):
                def turned(g, h, i):
                    claim(pe, L, g)
                    u = TT * h + i
                    pe.wait_ge(u_p, ubase + u + 1)
                    for k in range(i + 1):
                        ins = turn(bank(L, g)[:, k * P:(k + 1) * P], buf(h, i)[:, k * P:(k + 1) * P])
                    ins.then_inc(l_full, 1)
                return turned

            def causal_values(name, rows, vt):
                at = plan.events[name][1]

                def values(g, h):
                    claim(pe, L, g)
                    wait_read(pe, L, at["T", h, TT - 1])
                    for k in range(TT):
                        n = T - k * P
                        ins = pe.matmul(bank(L, g)[rows(h), k * P:T], vt(h, k), pt(h, k, k * P, n),
                                        start=k == 0, stop=k == TT - 1)
                    ins.then_inc(l_full, 1)
                return values

            def diff_score(g, h, i):
                if h == 0 and i == 0:
                    wait_read(pe, L, L.base["v_ab"] + 15)
                n = P * (i + 1)
                for s in (0, 1):
                    claim(pe, S, g + s)
                    r = slice(64 * s, 64 * s + 64)
                    pe.matmul(bank(S, g + s)[:, 0:n], qa[r, h, i * P:(i + 1) * P], ka[r, h, 0:n],
                              start=True, stop=True).then_inc(s_full, 1)

            def diff_subln(g, h):
                claim(pe, S, g)
                pe.wait_ge(sub_sq, h + 1)
                pe.matmul(bank(S, g)[:, :], avg[128][:, :], nck[:, h % 2, :], start=True, stop=True)\
                    .then_inc(s_full, 1)

            attention("diff", diff_score, causal_values("diff", lambda h: slice(0, P), lambda h, k: va[:, k, h * P:(h + 1) * P]),
                      turned=causal_turn(U["diff"], lambda h, i: s_buf[:, 2 * (i % 4), :]), subln=diff_subln)

            def gates(tag, wait_first):
                for half in (0, 1):
                    stage(f"gate_{tag}{half}", xa, nb=2)
                    if half == 0:
                        wait_first()
                    stage(f"proj_{tag}{half}", xb, nk=4, c=512, nb=1)

            gates("a", lambda: pe.wait_ge(sub_lo, DIFF_HEADS))

            def fox_keys(g, h):
                claim(pe, S, g)
                pe.wait_ge(cum_ready, 2)
                pe.matmul(bank(S, g)[:, :], ident[0:8, h:h + 1].to_broadcast([8, P]), cum, start=True, stop=True)\
                    .then_inc(s_full, 1)

            def masked_score(g, i, pairs):
                n = P * (i + 1)
                claim(pe, S, g)
                for j, (q, k) in enumerate(pairs):
                    pe.matmul(bank(S, g)[:, 0:n], q, k[:, 0:n] if n < T else k, start=j == 0, stop=False)
                pe.matmul(bank(S, g)[:, i * P:n], ident_bf[:, :], mask_bf[:, :], start=False, stop=True)\
                    .then_inc(s_full, 1)

            def fox_score(g, h, i):
                r = slice(64 * (h % 2), 64 * (h % 2) + 64)
                masked_score(g, i, [(qb[r, h // 2, i * P:(i + 1) * P], kb[r, h // 2, :])])

            attention("fox", fox_score,
                      causal_values("fox", lambda h: slice(64 * (h % 2), 64 * (h % 2) + 64),
                                    lambda h, k: vb[:, k, h * 64:(h + 1) * 64]),
                      turned=causal_turn(U["fox"], lambda h, i: s_buf[:, i, :]), keys=fox_keys)
            gates("b", lambda: wait_read(pe, L, plan.events["fox"][1]["V", FOX_HEADS - 1, 0]))
            stage("w_o", xa, ready=lambda k: pe.wait_ge(m_lo, k + 1))

            def mem_keys(c):
                g = L.base[f"memT{c}"]
                pe.wait_ge(mem_sc, 2 * (c + 1))
                for q in range(4):
                    claim(pe, L, g + q)
                    for j in (0, 1):
                        for t in range(MT):
                            ins = turn(bank(L, g + q)[:, MEM * j + P * t:MEM * j + P * (t + 1)],
                                       mem_st[:, t, (2 * q + j) * P:(2 * q + j + 1) * P])
                    ins.then_inc(l_full, 1)
                stage(f"xk{c}", xm, n=MEM, ready=lambda k: wait_read(pe, L, L.base[f"memT{c}"] + k // 2))

            def mem_values(c, j):
                tok(plan.block_base[f"xv{c}{j}"], L.base[f"xv{c}{j}"], 8, 256, xm, MT)

            def cross(c, k_norm):
                if c != 1:
                    mem_keys(c)
                norm(k_norm)
                for j in range(2 if c == 1 else 0, 4):
                    mem_values(c, j)
                stage(f"xq{c}", xa, ready=h_ready(k_norm))
                at = plan.events[f"xa{c}"][1]

                def score(g, h, i):
                    claim(pe, S, g)
                    if i == 0:
                        wait_read(pe, L, L.base[f"xq{c}"] + 2 * h + 1)
                    for d in (0, 1):
                        ins = pe.matmul(bank(S, g)[:, 0:MEM], qT[:, 2 * h + d, i * P:(i + 1) * P],
                                        kT[:, 2 * h + d, :], start=d == 0, stop=d == 1)
                    ins.then_inc(s_full, 1)

                def turned(g, h, i):
                    claim(pe, L, g)
                    u = TT * h + i
                    pe.wait_ge(u_p, U[f"xa{c}"] + u + 1)
                    for m in range(MT):
                        ins = turn(bank(L, g)[:, m * P:(m + 1) * P], p_x[:, i, m * P:(m + 1) * P])
                    ins.then_inc(l_full, 1)

                def values(g, h):
                    wait_read(pe, L, at["T", h, TT - 1])
                    for d in (0, 1):
                        claim(pe, L, g + d)
                        for m in range(MT):
                            ins = pe.matmul(bank(L, g + d)[:, :], vM[:, m, h * 256 + d * P:h * 256 + (d + 1) * P],
                                            ptx(h, m, 0, T), start=m == 0, stop=m == MT - 1)
                        ins.then_inc(l_full, 1)

                attention(f"xa{c}", score, values, turned=turned)

                def o_ready(k):
                    wait_read(pe, L, at["V", k // 2, 0] + k % 2)
                stage(f"xo{c}", xa, ready=o_ready)

            def mlp(name, nf, n_up, k_norm, lo_base):
                b0, g0 = plan.block_base[name], L.base[name]
                nb, ng = n_up + 1, 2 * n_up + 8

                def ups(b, g, ready=None, i=None):
                    for j in range(n_up):
                        feat(b + j, g + 2 * j, 8, 256, xa, ready if j == 0 else None, i, 2 * nb, 2 * ng)

                def down(f, b, g, i=None):
                    pe.wait_ge(up_lo, lin(lambda r: lo_base + 2 * (f + 1) + 4 * r, i))
                    feat(b, g, 2, 1024, lambda k: xb(2 * (f % 2) + k), None, i, 2 * nb, 2 * ng)

                norm(k_norm)
                ups(b0, g0, h_ready(k_norm))
                pairs = (nf - 1) // 2

                def body(i):
                    for f in (0, 1):
                        b, g = b0 + n_up + nb * f, g0 + 2 * n_up + ng * f
                        ups(b, g, None, i)
                        down(f, b + n_up, g + 2 * n_up, i)
                rep(pe, pairs, body)
                for f in range(2 * pairs, nf):
                    b, g = b0 + n_up + nb * f, g0 + 2 * n_up + ng * f
                    if f + 1 < nf:
                        ups(b, g)
                        down(f, b + n_up, g + 2 * n_up)
                    else:
                        down(f, b, g)

            cross(0, 1)
            mlp("mlp", FF1 // 256, 1, 2, UPB["mlp"])
            norm(3)
            norm(4)
            stage("pool_u", xa, nb=2, ready=h_ready(4))
            stage("glu", xa)
            g = L.base["pool_w"]
            pe.wait_ge(ld_pw, 16)
            for q in range(4):
                claim(pe, L, g + q)
                pe.wait_ge(pool_r, q + 1)
                pe.matmul(bank(L, g + q)[:, :], pool_wt[:, q, :], pooled[:, q, :], start=True, stop=True)\
                    .then_inc(l_full, 1)
            stage("pc_out_a", lambda k: xa(4 + k), nk=4, c=512, nb=2,
                  ready=lambda k: wait_read(pe, L, L.base["pool_w"] + k))
            mem_keys(1)
            g = S.base["ln_mean"]
            claim(pe, S, g)
            pe.wait_ge(tap, TAPS)
            for q in range(4):
                ins = pe.matmul(bank(S, g)[:, :], avg[512][:, :], cvt[:, q, :], start=q == 0, stop=q == 3)
            ins.then_inc(s_full, 1)
            mem_values(1, 0)
            g = S.base["ln_var"]
            claim(pe, S, g)
            for q in range(4):
                pe.wait_ge(ln_sq, q + 1)
                ins = pe.matmul(bank(S, g)[:, :], avg[512][:, :], ly[:, q, :], start=q == 0, stop=q == 3)
            ins.then_inc(s_full, 1)
            mem_values(1, 1)
            stage("pc_out_b", xa, nk=4, c=512, nb=2, ready=lambda k: pe.wait_ge(yb_lo, k + 1))
            cross(1, 5)
            mlp("ffn0", FF2 // 256, 2, 6, UPB["ffn0"])
            norm(7)
            stage("dq", xa, nb=2, ready=h_ready(7))
            feat(plan.block_base["dq2"], L.base["dq2"], 8, 160, xa, chunks=[(0, P), (P, 32)])
            g = S.base["c_norm"]
            for j, (n, cnt) in enumerate(((384, 2), (256, 1))):
                claim(pe, S, g + j)
                pe.wait_ge(c_acc, (2, 3)[j])
                pe.matmul(bank(S, g + j)[:, :], avg[n][:, :], cacc[:, j, :], start=True, stop=True)\
                    .then_inc(s_full, 1)
            for half in (0, 1):
                for j in (0, 1):
                    feat(plan.block_base[f"uq{half}{j}"], L.base[f"uq{half}{j}"], 3, 384, xa,
                         (lambda k: pe.wait_ge(c_lo, k + 1)), chunks=[(96 * q, 96) for q in range(4)])
                b, g = plan.block_base[f"uk{half}"], L.base[f"uk{half}"]
                wait_block(b)
                pe.wait_ge(c_lo, 5)
                h, l = wview(w_hi, b % 2, 2, 1024), wview(w_lo, b % 2, 2, 1024)
                for q in range(8):
                    claim(pe, L, g + q)
                    for k in (0, 1):
                        xh, xl = xa(3 + k)
                        ins = mm3(bank(L, g + q)[0:64, :], h[:, k, P * q:P * q + 64], l[:, k, P * q:P * q + 64],
                                  xh, xl, k == 0, k == 1)
                    ins.then_inc(l_full, 1)
                for t in range(TT):
                    claim(pe, L, g + 8 + t)
                    for k in (0, 1):
                        xh, xl = xa(3 + k)
                        q = slice(t * P, (t + 1) * P)
                        vh_ = h[:, k, :].rearrange("p (h c) -> p h c", c=P)[:, :, 64:P]
                        vl_ = l[:, k, :].rearrange("p (h c) -> p h c", c=P)[:, :, 64:P]
                        o = bank(L, g + 8 + t)[:, :].rearrange("p (h c) -> p h c", c=64)
                        ins = mm3(o, vh_, vl_, xh[:, q], xl[:, q], k == 0, k == 1, swap=True)
                    ins.then_inc(l_full, 1)
                at = plan.events[f"mla{half}"][1]

                def score(g, h, i, half=half):
                    if i == 0:
                        pe.wait_ge(rope_q, 8 * half + h + 1)
                        pe.wait_ge(kpe_put, 8 * half + h + 1)
                    if h == 0 and i == 0:
                        wait_read(pe, L, L.base[f"uk{half}"] + 11)
                    masked_score(g, i, [(qh[0:96, h, i * P:(i + 1) * P], kh[0:96, h, :])])

                attention(f"mla{half}", score,
                          causal_values(f"mla{half}", lambda h: slice(64 * (h % 2), 64 * (h % 2) + 64),
                                        lambda h, k: vh[:, k, h * 64:(h + 1) * 64]),
                          turned=causal_turn(U[f"mla{half}"], lambda h, i: s_buf[:, i, :]))

            def mo_ready(k):
                half, h = (0, 2 * k + 1) if k < 4 else (1, 2 * (k - 4) + 1)
                wait_read(pe, L, plan.events[f"mla{half}"][1]["V", h, 0])
            stage("mla_o", lambda k: xb(k) if k < 4 else xa(k - 4), ready=mo_ready)
            cross(2, 8)
            mlp("ffn1", FF2 // 256, 2, 9, UPB["ffn1"])
            norm(10)
            g = L.base["out"]
            for c in range(KD):
                claim(pe, L, g + c)
                pe.wait_ge(n_h, 8 * 10 + c + 1)
                for t in range(TT):
                    ins = turn(bank(L, g + c)[:, t * P:(t + 1) * P], h32[:, c % 2, t * P:(t + 1) * P])
                ins.then_inc(l_full, 1)

        @block.scalar
        def _(act):
            def hi(b, i=None, db=0):
                if b + (db * i if isinstance(i, int) else 0) >= NB:
                    return
                act.wait_ge(w_loaded[b % 2], lin(lambda r: 16 * ((b + r * db) // 2 + 1), i))
                if b >= 2:
                    act.wait_ge(l_full, lin(lambda r: plan.block_end[b - 2 + r * db], i))
                act.activation(w_hi[:, b % 2, :], w_raw[:, b % 2, :], ACT.Copy).then_inc(w_hi_made, 1)

            steps = [0]

            def step(ins):
                steps[0] += 1
                ins.then_inc(a_step, 1)

            def sync():
                act.wait_ge(a_step, steps[0])

            act.wait_ge(ld_keep, 16)
            act.wait_ge(ld_once, 16)
            act.activation(ident_bf[:, :], ident, ACT.Copy).then_inc(setup_a, 1)
            act.activation(mask_bf[:, :], once[:, P:2 * P], ACT.Copy).then_inc(setup_a, 1)
            hi(0)
            hi(1)

            def copy_groups(name, dst, n, last_col=None):
                g = L.base[name]
                for j in range(n):
                    wait_group(act, L, g + j)
                    act.activation(dst(j), bank(L, g + j)[:, 0:last_col or T], ACT.Copy).then_inc(l_free["a"], 1)

            def block_copies(name, nb, per, dst, cols=T):
                g, b = L.base[name], plan.block_base[name]
                for j in range(nb):
                    for q in range(per):
                        wait_group(act, L, g + per * j + q)
                        act.activation(dst(per * j + q), bank(L, g + per * j + q)[:, 0:cols], ACT.Copy)\
                            .then_inc(l_free["a"], 1)
                    hi(b + j + 2)

            def just_hi(name, nb):
                for j in range(nb):
                    hi(plan.block_base[name] + j + 2)

            def square(k, n, g_x):
                wait_read(act, L, g_x + n)
                if n >= 2:
                    act.wait_ge(n_acc, 7 * k + max(1, n - 2))
                elif k:
                    act.wait_ge(n_acc, 7 * k)
                act.activation(sq[:, n % 2, :], x[:, n, :], ACT.Square).then_inc(n_sq, 1)

            def norm_squares(k, g_x):
                for n in range(KD):
                    square(k, n, g_x)

            def hi_and_squares(name, nb, k):
                g, b, per = L.base[name], plan.block_base[name], KD // nb
                for j in range(nb):
                    last = j == nb - 1
                    for q in range(per if last else per - 1):
                        square(k, per * j + q, g)
                    hi(b + j + 2)
                    if not last:
                        square(k, per * j + per - 1, g)

            def norm_rstd(k):
                g = S.base[f"norm{k}"]
                act.activation(warm[:, k:k + 1], eps_col, ACT.Ln)
                wait_group(act, S, g)
                act.activation(rst, bank(S, g)[:, :], ACT.Ln, bias=eps_col).then_inc(s_free["a"], 1)
                wait_read(act, S, g)
                act.activation(rst, rst, ACT.Exp, scale=-0.5).then_inc(n_rstd, 1)

            def norm_hi(k, between=()):
                for n in range(KD):
                    act.wait_ge(n_h, 8 * k + n + 1)
                    act.activation(A_hi[:, n, :], h32[:, n % 2, :], ACT.Copy).then_inc(n_hi, 1)
                    if between and (n + 1) % (KD // len(between)) == 0:
                        between[n // (KD // len(between))]()

            act.wait_ge(setup_v, 2)
            norm_squares(0, L.base["x_in"])
            norm_rstd(0)
            norm_hi(0)
            act.wait_ge(setup_v, 9)
            act.activation(lam_t[:, 2:4], lam_t[:, 0:2], ACT.Exp).then_inc(setup_a, 1)
            block_copies("qk_a", 4, 2, lambda j: qa[:, j, :] if j < 4 else ka[:, j - 4, :])
            block_copies("qk_b", 4, 2, lambda j: qb[:, j, :] if j < 4 else kb[:, j - 4, :])

            def v_dst(j):
                blk, t = divmod(j, 4)
                v = va if blk < 2 else vb
                return v[:, t, 256 * (blk % 2):256 * (blk % 2) + 256]
            block_copies("v_ab", 4, 4, v_dst, cols=256)
            act.wait_ge(forget_m, 3)
            act.activation(fe, fm, ACT.Exp).then_inc(forget_l, 1)
            act.wait_ge(forget_l, 1)
            act.activation(flg, fe, ACT.Ln, bias=1.0).then_inc(forget_l, 1)

            def turned_copy(name, pt_):
                def t(g, h, i):
                    wait_group(act, L, g)
                    u = plan.events[name][1]
                    if h >= 2:
                        act.wait_ge(l_full, u["V", h - 2, 0] + (2 if name[0] == "x" else 1))
                    pt_(g, h, i)
                return t

            def causal_copy(g, h, i):
                for k in range(i + 1):
                    ins = act.activation(pt(h, k, i * P, P), bank(L, g)[:, k * P:(k + 1) * P], ACT.Copy)
                ins.then_inc(l_free["a"], 1)

            ev, at = plan.events["diff"]
            tc = turned_copy("diff", causal_copy)
            for kind, h, i in ev:
                g = at[kind, h, i]
                if kind == "S":
                    n = P * (i + 1)
                    for s in (0, 1):
                        u = 2 * (TT * h + i) + s
                        act.wait_ge(u_nm, NM["diff"] + u + 1)
                        b_ = s_buf[:, 2 * (i % 4) + s, 0:n]
                        act.activation(b_, b_, ACT.Exp, bias=nm[:, u % 8:u % 8 + 1], scale=0.125,
                                       accum_out=ls[:, u % 8:u % 8 + 1]).then_inc(u_exp, 1)
                if kind == "T":
                    tc(g, h, i)
                if kind == "V":
                    wait_group(act, L, g)
                    if h >= 2:
                        wait_group(act, S, at["M", h - 2, 0])
                    act.activation(nck[:, h % 2, :], bank(L, g)[:, :], ACT.Square).then_inc(sub_sq, 1)
                if kind == "M":
                    wait_group(act, S, g)
                    act.activation(nck[:, h % 2, :], bank(S, g)[:, :], ACT.Ln, bias=eps_col).then_inc(s_free["a"], 1)
                    wait_read(act, S, g)
                    act.activation(nck[:, h % 2, :], nck[:, h % 2, :], ACT.Exp, scale=-0.5).then_inc(sub_rs, 1)
                    wait_read(act, L, at["V", h, 0])
                    act.activation(B_hi[:, h, :], bias8[:, h, :], ACT.Copy).then_inc(o_hi, 1)

            def mem_rstd(c):
                act.wait_ge(ld_mem, 16 * (c + 1))
                for t in range(MT):
                    act.activation(mem_junk, mem_st[:, t, :], ACT.Square, accum_out=mem_s[:, t:t + 1])\
                        .then_inc(mem_ss, 1)
                    act.wait_ge(mem_ss, (MT + 1) * c + t + 1)
                act.activation(mem_s[:, 2:4], mem_s[:, 0:2], ACT.Ln, bias=eps_col, scale=1.0 / D).then_inc(mem_ss, 1)
                act.wait_ge(mem_ss, (MT + 1) * (c + 1))
                act.activation(mem_s[:, 4:6], mem_s[:, 2:4], ACT.Exp, scale=-0.5).then_inc(mem_rs, 1)

            def gate_sigmoids(tag, half, ns):
                g, b = L.base[f"gate_{tag}{half}"], plan.block_base[f"gate_{tag}{half}"]
                if ns:
                    wait_read(act, L, L.base[ns] + 3)
                for j in range(4):
                    wait_group(act, L, g + j)
                    act.activation(sg[:, j, :], bank(L, g + j)[:, :], ACT.Sigmoid).then_inc(l_free["a"], 1)
                    if j % 2:
                        hi(b + j // 2 + 2)
                hi(plan.block_base[f"proj_{tag}{half}"] + 2)

            gate_sigmoids("a", 0, None)
            gate_sigmoids("a", 1, "proj_a0")

            ev, at = plan.events["fox"]
            tc = turned_copy("fox", causal_copy)
            for kind, h, i in ev:
                g = at[kind, h, i]
                n = P * (i + 1)
                if kind == "S":
                    u = TT * h + i
                    act.wait_ge(u_nm, NM["fox"] + u + 1)
                    act.activation(s_buf[:, i, 0:n], s_buf[:, i, 0:n], ACT.Exp, bias=nm[:, u % 8:u % 8 + 1],
                                   scale=0.125, accum_out=ls[:, u % 8:u % 8 + 1]).then_inc(u_exp, 1)
                if kind == "T":
                    tc(g, h, i)
                if kind == "V":
                    r = slice(64 * (h % 2), 64 * (h % 2) + 64)
                    wait_group(act, L, g)
                    if h == 0:
                        act.wait_ge(l_full, L.base["proj_a1"] + 4)
                    act.activation(B_hi[r, h // 2, :], bank(L, g)[r, :], ACT.Copy).then_inc(o_hi, 1)
            gate_sigmoids("b", 0, "proj_a1")
            mem_rstd(0)
            gate_sigmoids("b", 1, "proj_b0")
            act.wait_ge(l_full, L.base["gate_b1"] + 4)
            for n in range(KD):
                act.wait_ge(m_ready, n + 1)
                act.activation(A_hi[:, n, :], merged[:, n, :], ACT.Copy).then_inc(m_hi, 1)
            hi_and_squares("w_o", 4, 1)

            def mem_keys(c):
                g = L.base[f"memT{c}"]
                for n in range(KD):
                    wait_group(act, L, g + n // 2)
                    o = slice(MEM * (n % 2), MEM * (n % 2) + MEM)
                    act.activation(B_hi[:, n // 2, o], bank(L, g + n // 2)[:, o], ACT.Copy,
                                   scale=cols[:, GKV[c] + n:GKV[c] + n + 1]).then_inc(mem_hi, 1)
                block_copies(f"xk{c}", 4, 2, lambda j: kT[:, j, :], cols=MEM)

            def mem_values(c, v):
                return lambda: block_copies(f"xv{c}{v}", 1, 2, lambda j: vM[:, j, 256 * v:256 * v + 256], cols=256)

            def cross(c, k_norm, after):
                if c != 1:
                    mem_keys(c)
                norm_rstd(k_norm)
                norm_hi(k_norm, [mem_values(c, v) for v in range(2 if c == 1 else 0, 4)])
                block_copies(f"xq{c}", 4, 2, lambda j: qT[:, j, :])
                ev, at = plan.events[f"xa{c}"]

                def copy(g, h, i):
                    for m in range(MT):
                        ins = act.activation(ptx(h, m, i * P, P), bank(L, g)[:, m * P:(m + 1) * P], ACT.Copy)
                    ins.then_inc(l_free["a"], 1)
                tc = turned_copy(f"xa{c}", copy)
                for kind, h, i in ev:
                    g = at[kind, h, i]
                    if kind == "S":
                        u = TT * h + i
                        act.wait_ge(u_nm, NM[f"xa{c}"] + u + 1)
                        if u >= 4:
                            wait_group(act, L, at["T", (u - 4) // 4, i])
                        act.activation(p_x[:, i, :], bank(S, g)[:, 0:MEM], ACT.Exp, bias=nm[:, u % 8:u % 8 + 1],
                                       scale=1 / 16, accum_out=ls[:, u % 8:u % 8 + 1]).then_inc(s_free["a"], 1)
                    if kind == "T":
                        tc(g, h, i)
                    if kind == "V":
                        for d in (0, 1):
                            wait_group(act, L, g + d)
                            act.activation(A_hi[:, 2 * h + d, :], bank(L, g + d)[:, :], ACT.Copy).then_inc(o_hi, 1)
                hi_and_squares(f"xo{c}", 4, after)

            def mlp_up(f, b, g, ub, hb, i=None):
                for c in (0, 1):
                    wait_group(act, L, g + c, i, 20)
                    act.activation(r32[:, c, :], bank(L, g + c)[:, :], ACT.Relu).then_inc(l_free["a"], 1)
                hi(b + 2, i, 4)
                for c in (0, 1):
                    act.wait_ge(up_f, lin(lambda r: ub + 2 * f + c + 1 + 4 * r, i))
                    act.activation(B_hi[:, 2 * (f % 2) + c, :], f32[:, c, :], ACT.Copy).then_inc(up_hi, 1)

            def last_squares(name, k):
                for n in range(KD):
                    square(k, n, L.base[name + "_last"])

            def mlp(k_norm, after):
                b0, g0 = plan.block_base["mlp"], L.base["mlp"]
                norm_rstd(k_norm)
                norm_hi(k_norm)
                u = UPB["mlp"]
                mlp_up(0, b0, g0, u, u)
                nf = FF1 // 256
                pairs = (nf - 1) // 2

                def body(i):
                    for f in (0, 1):
                        b, g = b0 + 1 + 2 * f, g0 + 2 + 10 * f
                        mlp_up(f + 1, b, g, u, u, i)
                        hi(b + 3, i, 4)
                rep(act, pairs, body)
                for f in range(2 * pairs, nf):
                    b, g = b0 + 1 + 2 * f, g0 + 2 + 10 * f
                    if f + 1 < nf:
                        mlp_up(f + 1, b, g, u, u)
                        hi(b + 3)
                    else:
                        last_squares("mlp", after)
                        hi(b + 2)

            def ffn_up(f, b, g, cb, i=None):
                for c in (0, 1):
                    wait_group(act, L, g + c, i, 24)
                    if cb + 2 * f + c > 1:
                        act.wait_ge(g_conv, lin(lambda r: 3 * (cb + 2 * f + c - 1 + 4 * r), i))
                    act.activation(gp[:, c, 2:T + 2], bank(L, g + c)[:, :], ACT.Copy).then_inc(l_free["a"], 1)
                hi(b + 2, i, 6)
                for c in (0, 1):
                    act.wait_ge(g_conv, lin(lambda r: 3 * (cb + 2 * f + c + 1 + 4 * r), i))
                    act.activation(sl[:, c, :], cv[:, c, :], ACT.Silu).then_inc(up_act, 1)
                for c in (0, 1):
                    wait_read(act, L, g + 2 + c, i, 24)
                    act.activation(B_hi[:, 2 * (f % 2) + c, :], f32[:, c, :], ACT.Copy).then_inc(up_hi, 1)
                hi(b + 3, i, 6)

            def ffn(name, k_norm, after):
                b0, g0, cb = plan.block_base[name], L.base[name], CB[name]
                norm_rstd(k_norm)
                norm_hi(k_norm)
                ffn_up(0, b0, g0, cb)
                nf = FF2 // 256

                def body(i):
                    for f in (0, 1):
                        b, g = b0 + 2 + 3 * f, g0 + 4 + 12 * f
                        ffn_up(f + 1, b, g, cb, i)
                        hi(b + 4, i, 6)
                rep(act, (nf - 1) // 2, body)
                last_squares(name, after)
                hi(b0 + 3 * nf - 1 + 2)

            cross(0, 1, 2)
            mlp(2, 3)
            norm_rstd(3)
            for n in range(KD):
                act.wait_ge(n_h, 8 * 3 + n + 1)
                if n >= 2:
                    act.wait_ge(n_acc, 7 * 4 + max(1, n - 2))
                act.activation(sq[:, n % 2, :], x[:, n, :], ACT.Square).then_inc(n_sq, 1)
            norm_rstd(4)
            norm_hi(4)
            block_copies("pool_u", 2, 2, lambda j: up_[:, j, 16:UW])
            g, b = L.base["glu"], plan.block_base["glu"]
            for pair in (0, 1):
                for c in (0, 1):
                    wait_group(act, L, g + 4 * pair + c)
                    act.activation(gl[:, 2 * pair + c, CONV_K - 1:GW], bank(L, g + 4 * pair + c)[:, :], ACT.Copy)\
                        .then_inc(l_free["a"], 1)
                hi(b + 2 * pair + 2)
                if pair:
                    act.wait_ge(glu_r, 2)
                for c in (0, 1):
                    wait_group(act, L, g + 4 * pair + 2 + c)
                    act.activation(sgb[:, c, :], bank(L, g + 4 * pair + 2 + c)[:, :], ACT.Sigmoid)\
                        .then_inc(l_free["a"], 1)
                hi(b + 2 * pair + 3)
            for q in range(4):
                wait_group(act, L, L.base["pool_w"] + q)
                act.activation(A_hi[:, 4 + q, :], bank(L, L.base["pool_w"] + q)[:, :], ACT.Copy,
                               scale=cols[:, COL["pool_scale_2"] + q:COL["pool_scale_2"] + q + 1]).then_inc(ya_hi, 1)
            hi(plan.block_base["pc_out_a"] + 2)
            mem_rstd(1)
            hi(plan.block_base["pc_out_a"] + 3)
            mem_keys(1)
            for q in range(4):
                act.wait_ge(ln_v, q + 1)
                act.activation(ly[:, q, :], cvt[:, q, :], ACT.Square).then_inc(ln_sq, 1)
            mem_values(1, 0)()
            g = S.base["ln_var"]
            wait_group(act, S, g)
            act.activation(lrs, bank(S, g)[:, :], ACT.Ln, bias=eps_col).then_inc(s_free["a"], 1)
            wait_read(act, S, g)
            act.activation(lrs, lrs, ACT.Exp, scale=-0.5).then_inc(ln_rs, 1)
            for q in range(4):
                act.wait_ge(ln_y, q + 1)
                act.activation(ly[:, q, :], cvt[:, q, :], ACT.Silu,
                               bias=cols[:, COL["conv_ln_b_2"] + q:COL["conv_ln_b_2"] + q + 1]).then_inc(ln_s, 1)
            for q in range(4):
                act.wait_ge(ln_s, q + 1)
                act.activation(A_hi[:, q, :], ly[:, q, :], ACT.Copy).then_inc(yb_hi, 1)
            mem_values(1, 1)()
            hi_and_squares("pc_out_b", 2, 5)
            cross(1, 5, 6)
            ffn("ffn0", 6, 7)
            norm_rstd(7)
            norm_hi(7)
            act.wait_ge(ang_r, 1)
            act.activation(sinT[64:96, :], sinT[64:96, :], ACT.Sin).then_inc(sincos, 1)
            act.wait_ge(ang_r, 2)
            act.activation(cosT[64:96, :], cosT[64:96, :], ACT.Sin).then_inc(sincos, 1)
            just_hi("dq", 2)
            hi(plan.block_base["dq2"] + 2)
            for n in range(5):
                wait_read(act, L, L.base["dq"] + n)
                if n in (2, 3, 4):
                    act.wait_ge(c_acc, (1, 1, 2)[n - 2])
                act.activation(h32[:, n % 2, :], cc[:, n, :], ACT.Square).then_inc(c_sq, 1)
            g = S.base["c_norm"]
            for j in (0, 1):
                wait_group(act, S, g + j)
                act.activation(crst[:, j, :], bank(S, g + j)[:, :], ACT.Ln, bias=eps_col).then_inc(s_free["a"], 1)
                wait_read(act, S, g + j)
                act.activation(crst[:, j, :], crst[:, j, :], ACT.Exp, scale=-0.5).then_inc(c_rs, 1)
            for n in range(5):
                act.wait_ge(c_h, n + 1)
                act.activation(A_hi[:, n, :], cc[:, n, :], ACT.Copy).then_inc(c_hi, 1)
            act.wait_ge(rope_k, 1)
            for half in (0, 1):
                if half:
                    wait_group(act, L, plan.events["mla0"][1]["V", 7, 0])
                for h in range(8):
                    if half == 0 and h == 0:
                        act.wait_ge(c_lo, 5)
                    act.activation(kh[64:96, h, :], kpe[64:96, :], ACT.Copy).then_inc(kpe_put, 1)
                for j in (0, 1):
                    hi(plan.block_base[f"uq{half}{j}"] + 2)
                g = L.base[f"uk{half}"]
                for q in range(8):
                    wait_group(act, L, g + q)
                    act.activation(kh[0:64, q, :], bank(L, g + q)[0:64, :], ACT.Copy).then_inc(l_free["a"], 1)
                for t in range(TT):
                    wait_group(act, L, g + 8 + t)
                    act.activation(vh[:, t, :], bank(L, g + 8 + t)[:, :], ACT.Copy).then_inc(l_free["a"], 1)
                hi(plan.block_base[f"uk{half}"] + 2)
                name = f"mla{half}"
                ev, at = plan.events[name]
                tc = turned_copy(name, causal_copy)
                for kind, h, i in ev:
                    g = at[kind, h, i]
                    n = P * (i + 1)
                    if kind == "S":
                        u = TT * h + i
                        act.wait_ge(u_nm, NM[name] + u + 1)
                        if u >= 4:
                            wait_group(act, L, at["T", h - 1, i])
                        act.activation(s_buf[:, i, 0:n], bank(S, g)[:, 0:n], ACT.Exp, bias=nm[:, u % 8:u % 8 + 1],
                                       scale=96.0 ** -0.5, accum_out=ls[:, u % 8:u % 8 + 1]).then_inc(s_free["a"], 1)
                    if kind == "T":
                        tc(g, h, i)
                    if kind == "V":
                        r = slice(64 * (h % 2), 64 * (h % 2) + 64)
                        wait_group(act, L, g)
                        dst = A_hi if half else B_hi
                        act.activation(dst[r, h // 2, :], bank(L, g)[r, :], ACT.Copy).then_inc(o_hi, 1)
            mem_rstd(2)
            hi_and_squares("mla_o", 4, 8)
            cross(2, 8, 9)
            ffn("ffn1", 9, 10)
            norm_rstd(10)
            g = L.base["out"]
            for c in range(KD):
                wait_group(act, L, g + c)
                act.activation(o_st[:, :, c * P:(c + 1) * P],
                               bank(L, g + c)[:, :].rearrange("p (t d) -> p t d", t=TT), ACT.Copy)\
                    .then_inc(l_free["a"], 1)

        @block.vector
        def _(dve):
            steps = [0]

            def step(ins):
                steps[0] += 1
                ins.then_inc(v_step, 1)
                return steps[0]

            def sync():
                dve.wait_ge(v_step, steps[0])

            def col(name, n=0):
                return cols[:, COL[name] + n:COL[name] + n + 1]

            for n, a in avg.items():
                dve.memset(a[:, :], 1.0 / n)
            dve.memset(small[:, 48:64], 0.0).then_inc(setup_v, 1)
            dve.memset(eps_col, EPS).then_inc(setup_v, 1)
            dve.memset(rrow[:, 512:640], NEG).then_inc(setup_v, 1)
            g = S.base["vecs"]
            for t in range(VT):
                m = min(P, NCOL - t * P)
                wait_group(dve, S, g + t)
                dve.tensor_copy(cols[:, t * P:t * P + m], bank(S, g + t)[:, 0:m]).then_inc(s_free["v"], 1)
            g = S.base["table"]
            wait_group(dve, S, g)
            dve.tensor_scalar(rrow[:, 0:512], bank(S, g)[0:4, :], 8.0, None, ALU.mult).then_inc(s_free["v"], 1)
            dve.wait_ge(ld_small, 16 * 7)
            dve.tensor_copy(wf_hi[:, :, :], wf_raw[:, :, :]).then_inc(setup_v, 1)
            dve.wait_ge(setup_v, 4)
            dve.tensor_tensor(wf_lo[:, :, :], wf_raw[:, :, :], wf_hi[:, :, :].bitcast(F32), ALU.subtract)\
                .then_inc(setup_v, 1)
            for j in (0, 1):
                dve.tensor_tensor(lams[:, 2 * j, :], lams[:, 2 * j, :], lams[:, 2 * j + 1, :], ALU.mult)\
                    .then_inc(setup_v, 1)
            dve.wait_ge(setup_v, 7)
            for j in (0, 1):
                dve.reduce_sum(lam_t[:, j:j + 1], lams[:, 2 * j, :], AX_X).then_inc(setup_v, 1)

            def norm_acc(k, n):
                dve.wait_ge(n_sq, 8 * k + n + 1)
                if n > 1:
                    dve.wait_ge(n_acc, 7 * k + n - 1)
                elif k:
                    wait_group(dve, S, S.base[f"norm{k - 1}"])
                dve.tensor_tensor(acc, sq[:, 0, :] if n == 1 else acc, sq[:, n % 2, :], ALU.add).then_inc(n_acc, 1)

            def with_acc(k, part):
                for n in range(KD):
                    part(n)
                    if n >= 2:
                        norm_acc(k, n - 1)
                norm_acc(k, KD - 1)

            def norm_h(k, split=True, into_x=False):
                gain = GAIN[k]
                dve.wait_ge(n_rstd, k + 1)

                def low(n):
                    dve.wait_ge(n_hi, n_base(k) + n + 1)
                    dve.tensor_tensor(A_lo[:, n, :], h32[:, n % 2, :], A_hi[:, n, :].bitcast(F32), ALU.subtract)\
                        .then_inc(n_lo, 1)
                for n in range(KD):
                    if not into_x and n >= 2:
                        if split:
                            dve.wait_ge(n_hi, n_base(k) + n - 1)
                            dve.wait_ge(n_lo, n_base(k) + n - 1)
                        else:
                            wait_group(dve, L, L.base["out"] + n - 2)
                    elif not into_x and n_base(k) and split:
                        dve.wait_ge(n_lo, n_base(k))
                    dve.scalar_tensor_tensor(out=x[:, n, :] if into_x else h32[:, n % 2, :], in0=x[:, n, :],
                                             scalar=cols[:, gain + n:gain + n + 1],
                                             in1=rst, op0=ALU.mult, op1=ALU.mult).then_inc(n_h, 1)
                    if into_x and n >= 2:
                        norm_acc(k + 1, n - 1)
                    if split and n >= 1:
                        low(n - 1)
                if split:
                    low(KD - 1)
                if into_x:
                    norm_acc(k + 1, KD - 1)

            def x_in(c):
                g = L.base["x_in"] + c
                wait_group(dve, L, g)
                dve.tensor_copy(x[:, c, :], bank(L, g)[:, :]).then_inc(l_free["v"], 1)

            with_acc(0, x_in)
            norm_h(0)
            g = S.base["flip"]
            for h in range(DIFF_HEADS):
                wait_group(dve, S, g + h)
                dve.tensor_copy(bias8[:, h, :], bank(S, g + h)[:, :]).then_inc(s_free["v"], 1)
            dve.wait_ge(setup_a, 3)
            step(dve.tensor_tensor(lam_t[:, 4:5], lam_t[:, 3:4], lam_t[:, 2:3], ALU.subtract))
            sync()
            step(dve.tensor_scalar(lam_neg, lam_t[:, 4:5], -LAMBDA_INIT, None, ALU.add))
            step(dve.tensor_scalar(g08, col("g_subln"), 1.0 - LAMBDA_INIT, None, ALU.mult))
            sync()
            g = S.base["forget"]
            wait_group(dve, S, g)
            dve.tensor_scalar(fz, bank(S, g)[0:8, :], bf_col, None, ALU.add).then_inc(s_free["v"], 1)
            wait_read(dve, S, g)
            dve.tensor_scalar(fmin, fz, 0.0, None, ALU.min).then_inc(forget_m, 1)
            dve.tensor_scalar(fone, fz, -1.0, None, ALU.mult).then_inc(forget_m, 1)
            dve.wait_ge(forget_m, 2)
            dve.tensor_tensor(fm, fz, fone, ALU.min).then_inc(forget_m, 1)
            dve.wait_ge(forget_m, 3)
            step(dve.memset(fone, 1.0))
            dve.wait_ge(forget_l, 2)
            step(dve.tensor_tensor(fmin, fmin, flg, ALU.subtract))
            sync()
            dve.tensor_tensor_scan(cum, fone, fmin, 0.0, ALU.mult, ALU.add).then_inc(cum_ready, 1)
            g = S.base["cum"]
            wait_group(dve, S, g)
            dve.tensor_scalar(ck8, bank(S, g)[:, 0:TT * 8], 8.0, None, ALU.mult).then_inc(s_free["v"], 1)
            dve.tensor_scalar(cum, cum, -8.0, None, ALU.mult).then_inc(cum_ready, 1)

            ev, at = plan.events["diff"]

            def combine(h, i):
                n = P * (i + 1)
                u = 2 * (TT * h + i)
                dve.wait_ge(u_exp, u + 2)
                a, b = u % 8, u % 8 + 1
                step(dve.reciprocal(rl[:, a:a + 2], ls[:, a:a + 2]))
                sync()
                step(dve.tensor_tensor(rl[:, b:b + 1], rl[:, b:b + 1], lam_neg, ALU.mult))
                p1, p2 = s_buf[:, 2 * i, 0:n], s_buf[:, 2 * i + 1, 0:n]
                step(dve.tensor_scalar(p1, p1, rl[:, a:a + 1], None, ALU.mult))
                sync()
                dve.scalar_tensor_tensor(out=p1, in0=p2, scalar=rl[:, b:b + 1], in1=p1, op0=ALU.mult,
                                         op1=ALU.add).then_inc(u_p, 1)

            for kind, h, i in ev:
                g = at[kind, h, i]
                n = P * (i + 1)
                if kind == "S":
                    for s in (0, 1):
                        u = 2 * (TT * h + i) + s
                        wait_group(dve, S, g + s)
                        if h:
                            wait_group(dve, L, at["T", h - 1, i])
                        dve.tensor_tensor_reduce(s_buf[:, 2 * i + s, 0:n], bank(S, g + s)[:, 0:n],
                                                 bias8[:, h, T - n:T], 1.0, -3e38, ALU.add, ALU.max,
                                                 mx[:, u % 8:u % 8 + 1]).then_inc(s_free["v"], 1)
                    for s in (0, 1):
                        u = 2 * (TT * h + i) + s
                        wait_read(dve, S, g + s)
                        dve.tensor_scalar(nm[:, u % 8:u % 8 + 1], mx[:, u % 8:u % 8 + 1], -0.125, None, ALU.mult)\
                            .then_inc(u_nm, 1)
                    if i or h:
                        combine(*divmod(TT * h + i - 1, TT))
                    if (h, i) == (DIFF_HEADS - 1, TT - 1):
                        combine(h, i)
                if kind == "M":
                    dve.wait_ge(sub_rs, h + 1)
                    gv = at["V", h, 0]
                    wait_group(dve, L, gv)
                    dve.scalar_tensor_tensor(out=bias8[:, h, :], in0=bank(L, gv)[:, :], scalar=g08,
                                             in1=nck[:, h % 2, :], op0=ALU.mult, op1=ALU.mult)\
                        .then_inc(l_free["v"], 1)
                    wait_read(dve, L, gv)
                    dve.wait_ge(o_hi, h + 1)
                    dve.tensor_tensor(B_lo[:, h, :], bias8[:, h, :], B_hi[:, h, :].bitcast(F32), ALU.subtract)\
                        .then_inc(sub_lo, 1)

            def gates(tag, half):
                g = L.base[f"proj_{tag}{half}"]
                for j in range(4):
                    n = 4 * half + j
                    wait_read(dve, L, L.base[f"gate_{tag}{half}"] + j)
                    wait_group(dve, L, g + j)
                    dst = merged[:, n, :] if tag == "a" else s_buf[:, j, :]
                    dve.tensor_tensor(dst, bank(L, g + j)[:, :], sg[:, j, :], ALU.mult).then_inc(l_free["v"], 1)
                    if tag == "b":
                        wait_read(dve, L, g + j)
                        dve.tensor_tensor(merged[:, n, :], merged[:, n, :], s_buf[:, j, :], ALU.add)\
                            .then_inc(m_ready, 1)

            gates("a", 0)
            gates("a", 1)

            def plain_norm(name, exp_done, buf, width, h, i):
                u = TT * h + i
                exp_done(h, i)
                a = u % 8
                step(dve.reciprocal(rl[:, a:a + 1], ls[:, a:a + 1]))
                sync()
                dve.tensor_scalar(buf[:, i, 0:width(i)], buf[:, i, 0:width(i)], rl[:, a:a + 1], None, ALU.mult)\
                    .then_inc(u_p, 1)

            def walk(name, heads, scores, exp_done, buf, width, values, keys=None):
                ev, at = plan.events[name]
                for kind, h, i in ev:
                    g = at[kind, h, i]
                    if kind == "K":
                        keys(g, h)
                    if kind == "S":
                        scores(g, h, i)
                        if h or i:
                            plain_norm(name, exp_done, buf, width, *divmod(TT * h + i - 1, TT))
                        if (h, i) == (heads - 1, TT - 1):
                            plain_norm(name, exp_done, buf, width, h, i)
                    if kind == "V":
                        values(g, h)

            at_fox = plan.events["fox"][1]

            def fox_keys(g, h):
                wait_group(dve, S, g)
                dve.tensor_copy(nck[:, h % 2, :], bank(S, g)[:, :]).then_inc(s_free["v"], 1)
                wait_read(dve, S, g)

            def fox_scores(g, h, i):
                n, u = P * (i + 1), TT * h + i
                wait_group(dve, S, g)
                if h:
                    wait_group(dve, L, at_fox["T", h - 1, i])
                dve.scalar_tensor_tensor(out=s_buf[:, i, 0:n], in0=bank(S, g)[:, 0:n],
                                         scalar=ck8[:, 8 * i + h:8 * i + h + 1], in1=nck[:, h % 2, 0:n],
                                         op0=ALU.add, op1=ALU.add).then_inc(s_free["v"], 1)
                wait_read(dve, S, g)
                step(dve.reduce_max(mx[:, u % 8:u % 8 + 1], s_buf[:, i, 0:n], AX_X))
                sync()
                dve.tensor_scalar(nm[:, u % 8:u % 8 + 1], mx[:, u % 8:u % 8 + 1], -0.125, None, ALU.mult)\
                    .then_inc(u_nm, 1)

            def half_values(name, hi_t, lo_t):
                def values(g, h):
                    r = slice(64 * (h % 2), 64 * (h % 2) + 64)
                    wait_group(dve, L, g)
                    dve.wait_ge(o_hi, OH[name] + h + 1)
                    dve.tensor_tensor(lo_t[r, h // 2, :], bank(L, g)[r, :], hi_t[r, h // 2, :].bitcast(F32),
                                      ALU.subtract).then_inc(l_free["v"], 1)
                return values

            walk("fox", FOX_HEADS, fox_scores, lambda h, i: dve.wait_ge(u_exp, 32 + TT * h + i + 1),
                 s_buf, lambda i: P * (i + 1), half_values("fox", B_hi, B_lo), keys=fox_keys)

            def mem_scale(c):
                dve.wait_ge(mem_rs, c + 1)
                for t in range(MT):
                    dve.tensor_scalar(mem_st[:, t, :], mem_st[:, t, :], mem_s[:, 4 + t:5 + t], None, ALU.mult)\
                        .then_inc(mem_sc, 1)

            gates("b", 0)
            mem_scale(0)
            gates("b", 1)
            for n in range(KD):
                dve.wait_ge(m_hi, n + 1)
                dve.tensor_tensor(A_lo[:, n, :], merged[:, n, :], A_hi[:, n, :].bitcast(F32), ALU.subtract)\
                    .then_inc(m_lo, 1)

            def residual(g, k):
                def add(n):
                    wait_group(dve, L, g + n)
                    dve.tensor_tensor(x[:, n, :], bank(L, g + n)[:, :], x[:, n, :], ALU.add).then_inc(l_free["v"], 1)
                wait_read(dve, L, g - 1)
                with_acc(k, add)

            def mem_keys(c):
                g = L.base[f"memT{c}"]
                for n in range(KD):
                    wait_group(dve, L, g + n // 2)
                    dve.wait_ge(mem_hi, 8 * c + 2 * (n // 2) + 2)
                    o = slice(MEM * (n % 2), MEM * (n % 2) + MEM)
                    ins = dve.scalar_tensor_tensor(
                        out=B_lo[:, n // 2, o], in0=bank(L, g + n // 2)[:, o],
                        scalar=cols[:, GKV[c] + n:GKV[c] + n + 1], in1=B_hi[:, n // 2, o].bitcast(F32),
                        op0=ALU.mult, op1=ALU.subtract)
                    if n % 2:
                        ins.then_inc(l_free["v"], 1)
                        if c == 1:
                            taps(4)

            def cross(c, k_norm, after):
                if c != 1:
                    mem_keys(c)
                norm_h(k_norm)
                name = f"xa{c}"
                at = plan.events[name][1]

                def scores(g, h, i):
                    u = TT * h + i
                    wait_group(dve, S, g)
                    step(dve.reduce_max(mx[:, u % 8:u % 8 + 1], bank(S, g)[:, 0:MEM], AX_X))
                    sync()
                    dve.tensor_scalar(nm[:, u % 8:u % 8 + 1], mx[:, u % 8:u % 8 + 1], -1 / 16, None, ALU.mult)\
                        .then_inc(u_nm, 1)

                def values(g, h):
                    for d in (0, 1):
                        wait_group(dve, L, g + d)
                        dve.wait_ge(o_hi, OH[name] + 2 * h + d + 1)
                        dve.tensor_tensor(A_lo[:, 2 * h + d, :], bank(L, g + d)[:, :],
                                          A_hi[:, 2 * h + d, :].bitcast(F32), ALU.subtract).then_inc(l_free["v"], 1)

                walk(name, XA_HEADS, scores, lambda h, i: wait_read(dve, S, at["S", h, i]), p_x, lambda i: MEM, values)
                residual(L.base[f"xo{c}"], after)

            residual(L.base["w_o"], 1)
            cross(0, 1, 2)

            def mlp():
                b = L.base["mlp"]
                nf, ub = FF1 // 256, UPB["mlp"]

                def up(f, g, i=None):
                    for c in (0, 1):
                        wait_read(dve, L, g + c, i, 20)
                        if f or i is not None:
                            dve.wait_ge(up_lo, lin(lambda r: ub + 2 * f + c - 1 + 4 * r, i))
                        dve.tensor_tensor(f32[:, c, :], r32[:, c, :], r32[:, c, :], ALU.mult).then_inc(up_f, 1)
                    for c in (0, 1):
                        dve.wait_ge(up_f, lin(lambda r: ub + 2 * f + c + 1 + 4 * r, i))
                        dve.wait_ge(up_hi, lin(lambda r: ub + 2 * f + c + 1 + 4 * r, i))
                        dve.tensor_tensor(B_lo[:, 2 * (f % 2) + c, :], f32[:, c, :],
                                          B_hi[:, 2 * (f % 2) + c, :].bitcast(F32), ALU.subtract).then_inc(up_lo, 1)

                norm_h(2)
                up(0, b)
                pairs = (nf - 1) // 2

                def body(i):
                    for f in (0, 1):
                        g = b + 2 + 10 * f
                        up(f + 1, g, i)
                        residual_loop(g + 2, i, 20)

                def residual_loop(g, i, dg):
                    for n in range(KD):
                        wait_group(dve, L, g + n, i, dg)
                        dve.tensor_tensor(x[:, n, :], bank(L, g + n)[:, :], x[:, n, :], ALU.add)\
                            .then_inc(l_free["v"], 1)
                    wait_read(dve, L, g + 7, i, dg)
                rep(dve, pairs, body)
                for f in range(2 * pairs, nf):
                    g = b + 2 + 10 * f
                    if f + 1 < nf:
                        up(f + 1, g)
                        residual_loop(g + 2, None, 0)
                    else:
                        residual(g, 3)

            mlp()
            norm_h(3, split=False, into_x=True)
            dve.wait_ge(n_h, 8 * 4)
            norm_h(4)
            step(dve.memset(gl[:, :, 0:CONV_K - 1], 0.0))
            step(dve.memset(up_[:, :, 0:16], 0.0))
            sync()

            def glu(pair):
                for c in (0, 1):
                    q = 2 * pair + c
                    wait_read(dve, L, L.base["glu"] + 4 * pair + 2 + c)
                    dve.tensor_tensor(gl[:, q, CONV_K - 1:GW], gl[:, q, CONV_K - 1:GW], sgb[:, c, :], ALU.mult)\
                        .then_inc(glu_r, 1)
                dve.wait_ge(glu_r, 2 * pair + 2)

            tap_n = [0]

            def taps(count):
                for k in range(tap_n[0], min(tap_n[0] + count, TAPS)):
                    j, c = divmod(k % (2 * CONV_K), 2)
                    q = 2 * (k // (2 * CONV_K)) + c
                    w = col("conv_dw_w_2", 4 * j + q)
                    if j == 0:
                        ins = dve.tensor_scalar(cvt[:, q, :], gl[:, q, 0:T], w, col("conv_dw_b_2", q), ALU.mult, ALU.add)
                    else:
                        dve.wait_ge(tap, k - 1)
                        ins = dve.scalar_tensor_tensor(out=cvt[:, q, :], in0=gl[:, q, j:j + T], scalar=w,
                                                       in1=cvt[:, q, :], op0=ALU.mult, op1=ALU.add)
                    ins.then_inc(tap, 1)
                tap_n[0] = min(tap_n[0] + count, TAPS)

            for q, w in enumerate(WINDOWS):
                wait_read(dve, L, L.base["pool_u"] + q)
                src, st, d = up_[:, q, :], 0, 1
                for n in range(q + 1):
                    st += d
                    dst = (pw_a, pw_b)[n % 2]
                    step(dve.tensor_tensor(dst[:, st:UW], src[:, st:UW], src[:, st - d:UW - d], ALU.add))
                    sync()
                    src, d = dst, 2 * d
                step(dve.scalar_tensor_tensor(out=pooled[:, q, :], in0=src[:, 16:UW], scalar=1.0 / w,
                                              in1=up_[:, q, 16:UW], op0=ALU.mult, op1=ALU.subtract))
                step(dve.tensor_tensor(ptmp, src[:, 16:32], keep[:, P + 16 * q:P + 16 * q + 16], ALU.mult))
                sync()
                dve.tensor_tensor(pooled[:, q, 0:16], ptmp, up_[:, q, 16:32], ALU.subtract).then_inc(pool_r, 1)
                dve.wait_ge(pool_r, q + 1)
            glu(0)
            taps(CONV_K)
            glu(1)
            for q in range(4):
                g = L.base["pool_w"] + q
                wait_group(dve, L, g)
                dve.wait_ge(ya_hi, q + 1)
                dve.scalar_tensor_tensor(out=A_lo[:, 4 + q, :], in0=bank(L, g)[:, :], scalar=col("pool_scale_2", q),
                                         in1=A_hi[:, 4 + q, :].bitcast(F32), op0=ALU.mult, op1=ALU.subtract)\
                    .then_inc(l_free["v"], 1)
            for n in range(KD):
                taps(4)
                g = L.base["pc_out_a"] + n
                wait_group(dve, L, g)
                dve.tensor_tensor(x[:, n, :], bank(L, g)[:, :], x[:, n, :], ALU.add).then_inc(l_free["v"], 1)
                if n == 5:
                    mem_scale(1)
            mem_keys(1)
            taps(TAPS)
            g = S.base["ln_mean"]
            wait_group(dve, S, g)
            dve.tensor_copy(lmu, bank(S, g)[:, :]).then_inc(s_free["v"], 1)
            wait_read(dve, S, g)
            for q in range(4):
                dve.tensor_tensor(cvt[:, q, :], cvt[:, q, :], lmu, ALU.subtract).then_inc(ln_v, 1)
            dve.wait_ge(ln_v, 4)
            dve.wait_ge(ln_rs, 1)
            for q in range(4):
                dve.scalar_tensor_tensor(out=cvt[:, q, :], in0=cvt[:, q, :], scalar=col("conv_ln_g_2", q), in1=lrs,
                                         op0=ALU.mult, op1=ALU.mult).then_inc(ln_y, 1)
            for q in range(4):
                dve.wait_ge(yb_hi, q + 1)
                dve.tensor_tensor(A_lo[:, q, :], ly[:, q, :], A_hi[:, q, :].bitcast(F32), ALU.subtract)\
                    .then_inc(yb_lo, 1)
            wait_read(dve, L, L.base["pc_out_a"] + 7)
            residual(L.base["pc_out_b"], 5)
            cross(1, 5, 6)

            def ffn(name, layer, k_norm, after):
                b, cb, ub = L.base[name], CB[name], UPB[name]
                cw, cbias = COL["ffn_conv_w_2"] + 66 * layer, COL["ffn_conv_b_2"] + 22 * layer

                def wcol(base, n, i):
                    if i is None or isinstance(i, int):
                        n += 4 * (i or 0)
                        return cols[:, base + n:base + n + 1]
                    return cols[:, bass.ds(base + n + 4 * i, 1)]

                def up(f, g, i=None):
                    for c in (0, 1):
                        k = 2 * f + c
                        wait_read(dve, L, g + c, i, 24)
                        if cb + k > 1:
                            dve.wait_ge(up_act, lin(lambda r: cb + k - 1 + 4 * r, i))
                        dve.tensor_scalar(cv[:, c, :], gp[:, c, 2:T + 2], wcol(cw + 44, k, i), wcol(cbias, k, i),
                                          ALU.mult, ALU.add).then_inc(g_conv, 1)
                        for j in (1, 0):
                            dve.wait_ge(g_conv, lin(lambda r: 3 * (cb + k + 4 * r) + 2 - j, i))
                            dve.scalar_tensor_tensor(out=cv[:, c, :], in0=gp[:, c, j:T + j],
                                                     scalar=wcol(cw + 22 * j, k, i), in1=cv[:, c, :],
                                                     op0=ALU.mult, op1=ALU.add).then_inc(g_conv, 1)
                    for c in (0, 1):
                        k = 2 * f + c
                        wait_group(dve, L, g + 2 + c, i, 24)
                        dve.wait_ge(up_act, lin(lambda r: cb + k + 1 + 4 * r, i))
                        if k > 1:
                            dve.wait_ge(up_lo, lin(lambda r: ub + k - 1 + 4 * r, i))
                        dve.tensor_tensor(f32[:, c, :], bank(L, g + 2 + c)[:, :], sl[:, c, :], ALU.mult)\
                            .then_inc(l_free["v"], 1)
                    for c in (0, 1):
                        k = 2 * f + c
                        wait_read(dve, L, g + 2 + c, i, 24)
                        dve.wait_ge(up_hi, lin(lambda r: ub + k + 1 + 4 * r, i))
                        dve.tensor_tensor(B_lo[:, 2 * (f % 2) + c, :], f32[:, c, :],
                                          B_hi[:, 2 * (f % 2) + c, :].bitcast(F32), ALU.subtract).then_inc(up_lo, 1)

                def down(g, i=None):
                    for n in range(KD):
                        wait_group(dve, L, g + n, i, 24)
                        dve.tensor_tensor(x[:, n, :], bank(L, g + n)[:, :], x[:, n, :], ALU.add)\
                            .then_inc(l_free["v"], 1)
                    wait_read(dve, L, g + 7, i, 24)

                norm_h(k_norm)
                step(dve.memset(gp[:, :, 0:2], 0.0))
                sync()
                up(0, b)
                nf = FF2 // 256

                def body(i):
                    for f in (0, 1):
                        g = b + 4 + 12 * f
                        up(f + 1, g, i)
                        down(g + 4, i)
                rep(dve, (nf - 1) // 2, body)
                residual(b + 4 + 12 * (nf - 1), after)

            ffn("ffn0", 0, 6, 7)
            norm_h(7)
            r = slice(64, 96)
            dve.wait_ge(ld_pos, 16)
            step(dve.tensor_copy(ang[r, :], posi[r, :]))
            sync()
            step(dve.tensor_scalar(ang[r, :], ang[r, :], keep[r, P + 64:P + 65], None, ALU.mult))
            sync()

            def reduced(dst, quarter, shift):
                step(dve.tensor_scalar(nrn[r, :], ang[r, :], float(np.float32(1 / (2 * np.pi))), quarter,
                                       ALU.mult, ALU.add))
                sync()
                step(dve.tensor_scalar(nrn[r, :], nrn[r, :], ROUND, None, ALU.add))
                sync()
                step(dve.tensor_scalar(nrn[r, :], nrn[r, :], -ROUND, None, ALU.add))
                sync()
                src = ang
                for part in TWO_PI:
                    step(dve.scalar_tensor_tensor(out=dst[r, :], in0=nrn[r, :], scalar=-float(part), in1=src[r, :],
                                                  op0=ALU.mult, op1=ALU.add))
                    sync()
                    src = dst
                step(dve.tensor_scalar(dst[r, :], dst[r, :], shift, PI32, ALU.add, ALU.min))
                sync()
                dve.tensor_scalar(dst[r, :], dst[r, :], -PI32, None, ALU.max).then_inc(ang_r, 1)

            reduced(sinT, 0.0, 0.0)
            reduced(cosT, 0.25, float(np.pi / 2))
            for n in range(5):
                wait_group(dve, L, L.base["dq"] + n)
                dve.tensor_copy(cc[:, n, :], bank(L, L.base["dq"] + n)[:, :]).then_inc(l_free["v"], 1)
            g = L.base["dq2"] + 1
            wait_group(dve, L, g)
            dve.tensor_copy(kpe[r, :], bank(L, g)[0:32, :]).then_inc(l_free["v"], 1)
            for a, n, first in ((0, 1, True), (0, 2, False), (1, 4, True)):
                dve.wait_ge(c_sq, n + 1)
                if n == 2:
                    dve.wait_ge(c_acc, 1)
                other = h32[:, (n - 1) % 2, :] if first else cacc[:, a, :]
                dve.tensor_tensor(cacc[:, a, :], other, h32[:, n % 2, :], ALU.add).then_inc(c_acc, 1)
            dve.wait_ge(sincos, 2)
            step(dve.tensor_scalar(sinT[r, :], sinT[r, :], keep[r, P + 65:P + 66], None, ALU.mult))
            SWAP = [16 + q for q in range(16)] + list(range(16))

            def rope(v, j, done):
                step(dve.stream_shuffle(rsh[r, j, :], v, SWAP))
                step(dve.tensor_tensor(rop[r, j, :], v, cosT[r, :], ALU.mult))
                sync()
                step(dve.tensor_tensor(rsh[r, j, :], rsh[r, j, :], sinT[r, :], ALU.mult))
                sync()
                dve.tensor_tensor(v, rop[r, j, :], rsh[r, j, :], ALU.add).then_inc(done, 1)

            wait_read(dve, L, g)
            rope(kpe[r, :], 0, rope_k)
            for n in range(5):
                j = n // 3
                dve.wait_ge(c_rs, j + 1)
                gcol = col("mla_q_norm_g_2", n) if j == 0 else col("mla_kv_norm_g_2", n - 3)
                dve.scalar_tensor_tensor(out=cc[:, n, :], in0=cc[:, n, :], scalar=gcol, in1=crst[:, j, :],
                                         op0=ALU.mult, op1=ALU.mult).then_inc(c_h, 1)
            for n in range(5):
                dve.wait_ge(c_hi, n + 1)
                dve.tensor_tensor(A_lo[:, n, :], cc[:, n, :], A_hi[:, n, :].bitcast(F32), ALU.subtract)\
                    .then_inc(c_lo, 1)
            dve.wait_ge(c_lo, 5)
            for half in (0, 1):
                for q in range(8):
                    g = L.base[f"uq{half}0"] + q
                    wait_group(dve, L, g)
                    dve.tensor_copy(qh[0:96, q, :], bank(L, g)[0:96, :]).then_inc(l_free["v"], 1)
                    wait_read(dve, L, g)
                    rope(qh[r, q, :], q % 2, rope_q)
                name = f"mla{half}"
                at = plan.events[name][1]

                def scores(g, h, i):
                    u, n = TT * h + i, P * (i + 1)
                    wait_group(dve, S, g)
                    step(dve.reduce_max(mx[:, u % 8:u % 8 + 1], bank(S, g)[:, 0:n], AX_X))
                    sync()
                    dve.tensor_scalar(nm[:, u % 8:u % 8 + 1], mx[:, u % 8:u % 8 + 1], -96.0 ** -0.5, None, ALU.mult)\
                        .then_inc(u_nm, 1)

                walk(name, 8, scores, lambda h, i, at=at: wait_read(dve, S, at["S", h, i]), s_buf,
                     lambda i: P * (i + 1), half_values(name, *((A_hi, A_lo) if half else (B_hi, B_lo))))
            mem_scale(2)
            residual(L.base["mla_o"], 8)
            cross(2, 8, 9)
            ffn("ffn1", 1, 9, 10)
            norm_h(10, split=False)


_INS = [
    "x", "mem", "w_in", "b_forget", "lambda_q1", "lambda_k1", "lambda_q2", "lambda_k2", "g_subln", "rel_bias",
    "w_diff_out", "w_fox_out", "w_o", "g_mix", "g_mem_q", "g_mem_kv", "w_q_mem", "w_kv_mem", "w_o_mem", "g_mlp",
    "w1", "w2", "g_final", "mem_2", "positions_2", "norm_mix_g_2", "norm_xa_g_2", "norm_mem_g_2", "xa_wq_2",
    "xa_wkv_2", "xa_wo_2", "norm_ffn_g_2", "ffn_w_up_2", "ffn_conv_w_2", "ffn_conv_b_2", "ffn_w_down_2",
    "pc_w_in_2", "pool_w_2", "pool_scale_2", "conv_dw_w_2", "conv_dw_b_2", "conv_ln_g_2", "conv_ln_b_2",
    "pc_w_out_2", "mla_w_dq_dkv_2", "mla_q_norm_g_2", "mla_w_uq_2", "mla_kv_norm_g_2", "mla_w_ukv_2",
    "mla_w_o_2", "final_norm_g_2",
]


def kernel(**inputs):
    import numpy as _np
    import concourse.bacc as _bacc
    from concourse import mybir as _mybir
    from concourse.bass_utils import run_bass_kernel_spmd as _run

    nc = _bacc.Bacc("TRN2", target_bir_lowering=False, num_devices=1)
    arrays, aps = {}, {}
    for name in _INS:
        a = _np.ascontiguousarray(inputs[name])
        arrays[f"in_{name}_dram"] = a
        aps[name] = nc.dram_tensor(f"in_{name}_dram", a.shape, _mybir.dt.from_np(a.dtype), kind="ExternalInput").ap()
    out = nc.dram_tensor("out_0_dram", (1, T, D), _mybir.dt.float32, kind="ExternalOutput").ap()
    build(nc, aps, out)
    r = _run(nc, [arrays], core_ids=[0])
    return r.results[0]["out_0_dram"]
```

```python
from contextlib import ExitStack

import numpy as np

import concourse.bass as bass
from concourse import mybir

ALU = mybir.AluOpType
ACT = mybir.ActivationFunctionType
F32 = mybir.dt.float32
FR = mybir.dt.float32r
BF16 = mybir.dt.bfloat16
I32 = mybir.dt.int32
AX_X = mybir.AxisListType.X

P = 128
T = 512
TT = T // P
D = 1024
KD = D // P
MEM = 256
MT = MEM // P
EPS = 1e-6
NEG = -1e30
BLK = 2048

DIFF_HEADS = 4
FOX_HEADS = 8
XA_HEADS = 4
FF1, FF2 = 4096, 2816
CONV_K = 31
WINDOWS = (2, 4, 8, 16)


def t5_bucket(d):
    if d < 16:
        return d
    return min(31, 16 + int(np.log(d / 16.0) / np.log(8.0) * 16 + 1e-9))


def constants():
    keep = np.zeros((P, P + 66), np.float32)
    keep[:, :P] = np.eye(P)
    for g, w in enumerate(WINDOWS):
        keep[:, P + 16 * g:P + 16 * g + 16] = 1.0 / np.minimum(np.arange(16) + 1, w)
    inv = 1.0 / (10000.0 ** (np.arange(0, 32, 2, dtype=np.float32) / 32))
    keep[64:80, P + 64] = inv
    keep[80:96, P + 64] = inv
    keep[64:80, P + 65] = -1.0
    keep[80:96, P + 65] = 1.0
    once = np.zeros((P, 2 * P + 512), np.float32)
    once[:, :P] = np.eye(P)[::-1]
    once[:, P:2 * P] = np.where(np.arange(P)[None, :] > np.arange(P)[:, None], NEG, 0.0)
    for m in range(512):
        once[t5_bucket(511 - m), 2 * P + m] = 1.0
    return keep, once


class Ring:

    def __init__(self):
        self.who = []
        self.base = {}

    def add(self, name, who):
        self.base[name] = len(self.who)
        self.who += list(who)

    def done(self, g):
        return self.who[g], self.who[:g + 1].count(self.who[g])


def lin(f, i):
    if i is None:
        return f(0)
    if isinstance(i, int):
        return f(i)
    by = f(2) - f(1)
    assert f(3) - f(2) == by
    return i * by + (f(1) - by) if by else f(1)


def attention_events(heads, lag, extra):
    ev = []
    n = heads * TT
    due = {}
    for step in range(n + lag + 6):
        if step < n:
            h, i = divmod(step, TT)
            if "K" in extra:
                if step == 0:
                    ev.append(("K", 0, 0))
                if i == 2 and h + 1 < heads:
                    ev.append(("K", h + 1, 0))
            ev.append(("S", h, i))
        for kind in "PVOMN":
            if (step, kind) in due and (kind in "PVO" or "M" in extra):
                ev.append((kind, due[step, kind], 0))
        if lag <= step < n + lag:
            h, i = divmod(step - lag, TT)
            ev.append(("T", h, i))
            if i == TT - 1:
                for kind in "VOMN":
                    due[step + 3, kind] = h
                due[step + 4, "P"] = h
    return ev


class Plan:

    def __init__(self):
        self.L = Ring()
        self.S = Ring()
        self.low_by = []
        self.blocks = []
        self.block_end = []
        self.block_base = {}
        self.events = {}

    def low(self, b):
        return self.low_by[b], self.low_by[:b + 1].count(self.low_by[b])

    def weights(self, name, src, nk, cols, places, groups_each, low_by=None):
        self.block_base[name] = len(self.blocks)
        for n, (r, c) in enumerate(places):
            self.blocks.append((src, nk, cols, r, c))
            self.low_by.append(low_by[n] if low_by else "p")
            self.block_end.append(self.L.base[name] + (n + 1) * groups_each)


def make_plan():
    p = Plan()
    L, S = p.L, p.S
    L.add("x_in", "v" * KD)
    S.add("vecs", "vvvv")
    norm = [0]

    def feat(name, src, who, cols, row=0, nk=8, width=256, chunk=P, low_by=None):
        per = width // chunk
        L.add(name, who * (per * len(cols)))
        p.weights(name, src, nk, width, [(row, c) for c in cols], per, low_by)

    def a_norm():
        S.add(f"norm{norm[0]}", "a")
        norm[0] += 1

    a_norm()
    S.add("table", "v")
    feat("qk_a", "w_in", "a", [0, 256, 512, 768])
    S.add("flip", "vvvv")
    feat("qk_b", "w_in", "a", [1536, 1792, 2048, 2304])
    L.add("v_ab", "a" * 16)
    p.weights("v_ab", "w_in", 8, 256, [(0, c) for c in (1024, 1280, 2560, 2816)], 4)
    S.add("forget", "v")
    S.add("cum", "v")

    def attention(name, heads, lag, score_who, per_score, t_who="a", v_who="v", v_groups=1, extra=""):
        ev = attention_events(heads, lag, extra)
        at = {}
        for kind, h, i in ev:
            if kind == "S":
                at[kind, h, i] = len(S.who)
                S.who += [score_who] * per_score
            elif kind == "K":
                at[kind, h, i] = len(S.who)
                S.who += ["v"]
            elif kind == "M":
                at[kind, h, i] = len(S.who)
                S.who += ["a"]
            elif kind == "T":
                at[kind, h, i] = len(L.who)
                L.who += [t_who]
            elif kind == "V":
                at[kind, h, i] = len(L.who)
                L.who += [v_who] * v_groups
            elif kind in "OPN":
                at[kind, h, i] = at["V", h, 0]
        p.events[name] = (ev, at)

    attention("diff", DIFF_HEADS, 3, "v", 2, extra="M")

    def gates(tag, col, out):
        for half in (0, 1):
            feat(f"gate_{tag}{half}", "w_in", "a", [col + 512 * half, col + 512 * half + 256])
            feat(f"proj_{tag}{half}", out, "v", [512 * half], nk=4, width=512)

    gates("a", 3080, "w_diff_out")
    attention("fox", FOX_HEADS, 3, "v", 1, extra="K")
    gates("b", 4104, "w_fox_out")
    feat("w_o", "w_o", "v", [0, 256, 512, 768])

    def keys(c, wkv):
        feat(f"xk{c}", wkv, "a", [0, 256, 512, 768], low_by="pppp" if c == 1 else "ppvv")

    def values(c, wkv, j):
        L.add(f"xv{c}{j}", "aa")
        p.weights(f"xv{c}{j}", wkv, 8, 256, [(0, D + 256 * j)], 2, low_by="p" if c == 1 and j < 2 else "v")

    def cross(c, wq, wkv, wo):
        if c != 1:
            L.add(f"memT{c}", "vvvv")
            keys(c, wkv)
        a_norm()
        for j in range(2 if c == 1 else 0, 4):
            values(c, wkv, j)
        feat(f"xq{c}", wq, "a", [0, 256, 512, 768])
        attention(f"xa{c}", XA_HEADS, 3, "a", 1, v_groups=2)
        feat(f"xo{c}", wo, "v", [0, 256, 512, 768])

    cross(0, "w_q_mem", "w_kv_mem", "w_o_mem")

    a_norm()

    def mlp(name, nf, up, up_who, down, second=None):
        L.base[name] = len(L.who)
        p.block_base[name] = len(p.blocks)

        def put(src, nk, cols, r, c, who):
            L.who.extend(who)
            p.blocks.append((src, nk, cols, r, c))
            p.low_by.append("p")
            p.block_end.append(len(L.who))

        def ups(f):
            for s, c0, who in up:
                put(s, 8, 256, 0, c0 + 256 * f, who * 2)

        ups(0)
        for f in range(nf):
            if f + 1 < nf:
                ups(f + 1)
            put(down, 2, 1024, 256 * f, 0, "v" * 8)
        L.base[name + "_last"] = len(L.who) - 8

    mlp("mlp", FF1 // 256, [("w1", 0, "a")], "a", "w2")
    a_norm()
    a_norm()
    feat("glu", "pc_w_in_2", "a", [512, 1024, 768, 1280])
    L.add("memT1", "vvvv")
    feat("pool_u", "pc_w_in_2", "a", [0, 256])
    keys(1, "xa_wkv_2:0")
    L.add("pool_w", "vvvv")
    feat("pc_out_a", "pc_w_out_2", "v", [0, 512], nk=4, width=512)
    S.add("ln_mean", "v")
    S.add("ln_var", "a")
    values(1, "xa_wkv_2:0", 0)
    values(1, "xa_wkv_2:0", 1)
    feat("pc_out_b", "pc_w_out_2", "v", [0, 512], row=512, nk=4, width=512)
    cross(1, "xa_wq_2:0", "xa_wkv_2:0", "xa_wo_2:0")
    a_norm()
    mlp("ffn0", FF2 // 256, [("ffn_w_up_2:0", FF2, "a"), ("ffn_w_up_2:0", 0, "v")], None, "ffn_w_down_2:0")
    a_norm()
    feat("dq", "mla_w_dq_dkv_2", "v", [0, 256])
    L.add("dq2", "vv")
    p.weights("dq2", "mla_w_dq_dkv_2", 8, 160, [(0, 512)], 2)
    S.add("c_norm", "aa")
    for half in (0, 1):
        for j in (0, 1):
            L.add(f"uq{half}{j}", "a" * 4)
            p.weights(f"uq{half}{j}", "mla_w_uq_2", 3, 384, [(0, 768 * half + 384 * j)], 4)
        L.add(f"uk{half}", "a" * 12)
        p.weights(f"uk{half}", "mla_w_ukv_2", 2, 1024, [(0, 1024 * half)], 12)
        attention(f"mla{half}", 8, 3, "a", 1)
    feat("mla_o", "mla_w_o_2", "v", [0, 256, 512, 768])
    cross(2, "xa_wq_2:1", "xa_wkv_2:1", "xa_wo_2:1")
    a_norm()
    mlp("ffn1", FF2 // 256, [("ffn_w_up_2:1", FF2, "a"), ("ffn_w_up_2:1", 0, "v")], None, "ffn_w_down_2:1")
    a_norm()
    L.add("out", "a" * 8)
    p.norms = norm[0]
    return p


LAMBDA_INIT = 0.8 - 0.6 * 1.0
ROUND = 12582912.0
TWO_PI = (6.28125, 2029 * 2.0 ** -20, 2 * np.pi - 6.28125 - 2029 * 2.0 ** -20)
PI32 = 3.1415925
TAPS = 4 * CONV_K
U = {"diff": 0, "fox": 16, "xa0": 48, "xa1": 64, "mla0": 80, "mla1": 112, "xa2": 144}
NM = {"diff": 0, "fox": 32, "xa0": 64, "xa1": 80, "mla0": 96, "mla1": 128, "xa2": 160}
OH = {"diff": 0, "fox": 4, "xa0": 12, "xa1": 20, "mla0": 28, "mla1": 36, "xa2": 44}
UPB = {"mlp": 0, "ffn0": 32, "ffn1": 54}
CB = {"ffn0": 0, "ffn1": 22}


def n_base(k):
    return 8 * k - (8 if k > 3 else 0)


VECTORS = [
    ("g_mix", D), ("g_mem_q", D), ("g_mem_kv", D), ("g_mlp", D), ("norm_mix_g_2", 2 * D),
    ("norm_xa_g_2", 2 * D), ("norm_mem_g_2", 2 * D), ("norm_ffn_g_2", 2 * D), ("g_final", D),
    ("final_norm_g_2", D), ("ffn_conv_b_2", 2 * FF2), ("ffn_conv_w_2", 6 * FF2),
    ("conv_dw_w_2", CONV_K * 512), ("conv_dw_b_2", 512), ("conv_ln_g_2", 512), ("conv_ln_b_2", 512),
    ("pool_scale_2", 512), ("mla_q_norm_g_2", 384), ("mla_kv_norm_g_2", 256), ("g_subln", 128),
]


def vector_columns():
    at, n = {}, 0
    for name, size in VECTORS:
        at[name] = n
        n += size // P
    return at, n


def build(nc, A, out):
    plan = make_plan()
    L, S = plan.L, plan.S
    COL, NCOL = vector_columns()
    VT = -(-NCOL // P)
    keep_np, once_np = constants()
    keep_d = nc.inline_tensor(keep_np, "keep_constants").ap()
    once_d = nc.inline_tensor(once_np, "start_constants").ap()
    scratch = nc.dram_tensor("bias_rows", (DIFF_HEADS, 640), F32, kind="Internal").ap()

    def flat(name):
        a = A[name]
        n = len(a.shape)
        if n == 1:
            return a
        if n == 2:
            return a.rearrange("a b -> (a b)")
        return a.rearrange("a b c -> (a b c)")

    def weight(name):
        name, _, layer = name.partition(":")
        a = A[name]
        return a[int(layer or 0)] if len(a.shape) == 3 else a

    with ExitStack() as ctx:
        def sb(name, shape, dt=F32):
            return ctx.enter_context(nc.sbuf_tensor(name, shape, dt))

        def sem(name):
            return ctx.enter_context(nc.semaphore(name))

        x = sb("x_T", [P, KD, T])
        A_hi, A_lo = sb("a_hi", [P, KD, T], FR), sb("a_lo", [P, KD, T], FR)
        B_hi, B_lo = sb("b_hi", [P, 4, T], FR), sb("b_lo", [P, 4, T], FR)
        w_raw = sb("w_raw", [P, 2, BLK])
        w_hi, w_lo = sb("w_hi", [P, 2, BLK], FR), sb("w_lo", [P, 2, BLK], FR)
        keep = sb("keep", [P, P + 66])
        ident = keep[:, 0:P]
        cols = sb("cols", [P, VT * P])
        ident_bf, mask_bf = sb("ident_bf", [P, P], BF16), sb("mask_bf", [P, P], BF16)
        avg = {n: sb(f"avg{n}", [P, P]) for n in (1024, 512, 384, 256, 128)}
        small = sb("small", [P, 64])
        eps_col, lam_neg, lam_t = small[:, 0:1], small[:, 1:2], small[:, 2:8]
        bf_col, g08 = sb("forget_bias", [8, 1])[:, :], small[:, 9:10]
        mem_s = small[:, 10:16]
        mx, nm, ls, rl = small[:, 16:24], small[:, 24:32], small[:, 32:40], small[:, 40:48]
        warm = small[:, 48:64]
        ck8 = sb("ck8", [P, TT * 8])[:, :]
        GKV = (COL["g_mem_kv"], COL["norm_mem_g_2"], COL["norm_mem_g_2"] + 8)
        GAIN = [COL["g_mix"], COL["g_mem_q"], COL["g_mlp"], COL["g_final"], COL["norm_mix_g_2"],
                COL["norm_xa_g_2"], COL["norm_ffn_g_2"], COL["norm_mix_g_2"] + 8, COL["norm_xa_g_2"] + 8,
                COL["norm_ffn_g_2"] + 8, COL["final_norm_g_2"]]
        wf_raw = sb("wf_raw", [P, KD, 8])
        wf_hi, wf_lo = sb("wf_hi", [P, KD, 8], FR), sb("wf_lo", [P, KD, 8], FR)
        arena = sb("arena", [P, 22016])

        def ar(off, *shape):
            n = int(np.prod(shape))
            assert off + n <= 22016
            v = arena[:, off:off + n]
            if len(shape) == 2:
                v = v.rearrange("p (a b) -> p a b", a=shape[0])
            return v

        sq, acc, rst, h32 = ar(0, 2, T), ar(1024, T), ar(1536, T), ar(2048, 2, T)
        s_buf = ar(0, 4, T)

        def s_diff(i, s):
            o = P * (i * (i + 1)) + s * P * (i + 1)
            return arena[:, o:o + P * (i + 1)]

        def pt(h):
            return ar(2560 + 2048 * (h % 2), TT, T)

        R0 = 6656
        qa, ka, va = ar(R0, 4, T), ar(R0 + 2048, 4, T), ar(R0 + 4096, 4, T)
        qb, kb, vb = ar(R0 + 6144, 4, T), ar(R0 + 8192, 4, T), ar(R0 + 10240, 4, T)
        bias8, nck = ar(R0 + 12288, 4, T), ar(R0 + 14336, 2, T)
        merged, sg = ar(R0, 8, T), ar(R0 + 4096, 4, T)
        x_st = ar(R0, TT, D)
        once = ar(R0 + 4096, 768)
        v_st = ar(R0 + 4864, 4, P)
        rel = arena[0:32, R0 + 5376:R0 + 5380]
        lams = ar(R0 + 5400, 4, 64)
        rrow = arena[0:4, R0 + 5700:R0 + 6340]
        bias_up = ar(4096, 4, T)
        fz, fm, fe, flg, fone, fmin = (arena[0:8, o:o + T] for o in (0, 512, 1024, 1536, 2048, 2560))
        cum = sb("cum", [8, T])[:, :]
        kT, qT, vM = ar(4096, 8, MEM), ar(R0 + 4280, 8, T), ar(R0 + 8952, 2, D)
        mem_st = [ar(o, 2, D) for o in (R0 + 6328, R0 + 13048, R0 + 6328)]
        mem_junk = ar(R0 + 11512, D)
        p_x = ar(0, 4, MEM)

        def ptx(h):
            return ar(1024 + 1024 * (h % 2), MT, T)

        r32, f32 = ar(R0, 2, T), ar(R0 + 1024, 2, T)
        gp = ar(R0 + 2048, 2, T + 2)
        cv, sl = ar(R0 + 3200, 2, T), ar(R0 + 4224, 2, T)
        GW, UW = T + CONV_K - 1, T + 16
        gl, up_ = ar(R0, 4, GW), ar(R0 + 2168, 4, UW)
        cvt, sgb = ar(R0 + 4280, 4, T), ar(R0 + 6328, 2, T)
        pw_a, pw_b = ar(R0 + 7352, UW), ar(R0 + 7880, UW)
        pooled = ar(R0 + 8408, 4, T)
        pool_wt = ar(R0 + 10456, 4, P)
        ptmp = ar(R0 + 10968, 16)
        lmu, lrs, ly = ar(R0 + 11000, T), ar(R0 + 12536, T), ar(R0 + 13048, 4, T)
        qh, kh, vh = ar(R0, 8, T), ar(R0 + 4096, 8, T), ar(R0 + 8192, 4, T)
        cosT, sinT = ar(R0 + 10240, T), ar(R0 + 10752, T)
        kpe, rsh = ar(R0 + 11264, T), ar(R0 + 11776, 4, T)
        cc = ar(R0, 5, T)
        posi = arena[:, R0 + 7680:R0 + 8192].bitcast(I32)
        ang, nrn = ar(R0 + 8192, T), ar(R0 + 8704, T)
        cacc = ar(R0 + 5632, 2, T)
        crst = ar(R0 + 6656, 2, T)
        o_st = ar(R0, TT, D)

        ps_l = [ctx.enter_context(nc.psum_tensor(f"ps_l{i}", [P, T], F32)) for i in range(4)]
        ps_s = [ctx.enter_context(nc.psum_tensor(f"ps_s{i}", [P, T], F32)) for i in range(4)]

        ld_keep, ld_once, ld_vec, ld_small = (sem(s) for s in ("ld_keep", "ld_once", "ld_vec", "ld_small"))
        ld_x = [sem("ld_x0"), sem("ld_x1")]
        ld_bias, ld_mem, ld_pw, ld_pos, st_out = (sem(s) for s in ("ld_bias", "ld_mem", "ld_pw", "ld_pos", "st_out"))
        w_loaded = [sem("w_loaded0"), sem("w_loaded1")]
        w_hi_made = sem("w_hi_made")
        w_lo_made = {"p": sem("w_lo_made_p"), "v": sem("w_lo_made_v")}
        l_full, s_full = sem("l_full"), sem("s_full")
        l_free = {"v": sem("l_free_v"), "a": sem("l_free_a")}
        s_free = {"v": sem("s_free_v"), "a": sem("s_free_a")}
        n_sq, n_acc, n_rstd, n_h, n_hi, n_lo = (sem(s) for s in ("n_sq", "n_acc", "n_rstd", "n_h", "n_hi", "n_lo"))
        setup_v, setup_a, v_step = sem("setup_v"), sem("setup_a"), sem("v_step")
        u_nm, u_exp, u_p = sem("neg_max_ready"), sem("exp_done"), sem("probs_ready")
        o_hi = sem("o_hi")
        sub_sq, sub_rs, sub_lo = sem("sub_sq"), sem("sub_rs"), sem("sub_lo")
        forget_m, forget_l, cum_ready = sem("forget_m"), sem("forget_l"), sem("cum_ready")
        m_ready, m_hi, m_lo = sem("merged_ready"), sem("m_hi"), sem("m_lo")
        mem_ss, mem_rs, mem_sc, mem_hi = (sem(s) for s in ("mem_ss", "mem_rs", "mem_sc", "mem_hi"))
        up_act, up_f, up_hi, up_lo = (sem(s) for s in ("up_act", "up_f", "up_hi", "up_lo"))
        g_conv = sem("g_conv")
        glu_r, tap, pool_r, ya_hi = (sem(s) for s in ("glu_r", "tap", "pool_r", "ya_hi"))
        ln_v, ln_sq, ln_rs, ln_y, ln_s, yb_hi, yb_lo = (sem(s) for s in ("ln_v", "ln_sq", "ln_rs", "ln_y", "ln_s", "yb_hi", "yb_lo"))
        ang_r, sincos, c_sq, c_acc, c_rs, c_h, c_hi, c_lo = (
            sem(s) for s in ("ang_r", "sincos", "c_sq", "c_acc", "c_rs", "c_h", "c_hi", "c_lo"))
        rope_k, rope_q, kpe_put = sem("rope_k"), sem("rope_q"), sem("kpe_put")

        n_vec_dmas = sum((COL[v] + n // P - 1) // P - COL[v] // P + 1 for v, n in VECTORS)

        def wait_group(e, ring, g, i=None, dg=0):
            e.wait_ge(l_full if ring is L else s_full, lin(lambda r: g + 1 + r * dg, i))

        def wait_read(e, ring, g, i=None, dg=0):
            free = l_free if ring is L else s_free
            who = ring.who[g if i is None else g + dg * (i if isinstance(i, int) else 1)]
            e.wait_ge(free[who], lin(lambda r: ring.done(g + r * dg)[1], i))

        def claim(e, ring, g, i=None, dg=0):
            if g >= 4:
                wait_read(e, ring, g - 4, i, dg)

        def bank(ring, g):
            return (ps_l if ring is L else ps_s)[g % 4]

        def freed(ring, who):
            return (l_free if ring is L else s_free)[who]

        def wait_low(e, b, i=None, db=0):
            e.wait_ge(w_lo_made[plan.low_by[b]], lin(lambda r: plan.low(b + r * db)[1], i))

        def low_part(e, b, i=None, db=0):
            e.wait_ge(w_hi_made, lin(lambda r: b + 1 + r * db, i))
            if b >= 2:
                e.wait_ge(l_full, lin(lambda r: plan.block_end[b - 2 + r * db], i))
            return e.tensor_tensor(w_lo[:, b % 2, :], w_raw[:, b % 2, :], w_hi[:, b % 2, :].bitcast(F32),
                                   ALU.subtract).then_inc(w_lo_made[plan.low_by[b]], 1)

        def wview(t, slot, nk, c):
            return t[:, slot, 0:nk * c].rearrange("p (k c) -> p k c", k=nk)

        NB = len(plan.blocks)

        def rep(e, n, body):
            body(0)
            with e.Fori(1, n - 1) as i:
                body(i)
            body(n - 1)

        block = ctx.enter_context(nc.Block())

        @block.sync
        def _(sp):
            sp.dma_start(keep[:, :], keep_d).then_inc(ld_keep, 16)
            x_in = A["x"][0].rearrange("(t p) d -> p t d", p=P)
            for half in (0, 1):
                o = slice(512 * half, 512 * half + 512)
                sp.dma_start(x_st[:, :, o], x_in[:, :, o]).then_inc(ld_x[half], 16)
            def load_block(b):
                src, nk, c, r0, c0 = plan.blocks[b]
                if b >= 2:
                    sp.wait_ge(w_hi_made, b - 1)
                    wait_low(sp, b - 2)
                w = weight(src)[r0:r0 + nk * P, c0:c0 + c].rearrange("(k p) c -> p k c", p=P)
                sp.dma_start(wview(w_raw, b % 2, nk, c), w).then_inc(w_loaded[b % 2], 16)

            def load_mem(c):
                m = A["mem"] if c == 0 else A["mem_2"]
                sp.dma_start(mem_st[c], m[0].rearrange("(t p) d -> p t d", p=P)).then_inc(ld_mem, 16)

            load_block(0)
            for name, size in VECTORS:
                v = flat(name).rearrange("(r p) -> r p", p=P)
                r, n = COL[name], size // P
                done = 0
                while done < n:
                    m = min(n - done, P - (r + done) % P)
                    q = (r + done) % P
                    sp.dma_start(v_st[q:q + m, (r + done) // P, :], v[done:done + m, :]).then_inc(ld_vec, 16)
                    done += m
            load_block(1)
            sp.dma_start(once, once_d).then_inc(ld_once, 16)
            with nc.allow_non_contiguous_dma(reason="a few bytes of each"):
                sp.dma_start(rel, A["rel_bias"]).then_inc(ld_small, 16)
                for j, nme in enumerate(("lambda_q1", "lambda_k1", "lambda_q2", "lambda_k2")):
                    sp.dma_start(lams[:, j, :], A[nme].to_broadcast([P, 64])).then_inc(ld_small, 16)
                sp.dma_start(bf_col, A["b_forget"].rearrange("a h -> h a")).then_inc(ld_small, 16)
                sp.dma_start(wf_raw[:, :, :], weight("w_in")[:, 3072:3080].rearrange("(k p) n -> p k n", p=P))\
                    .then_inc(ld_small, 16)
            sp.wait_ge(setup_v, 3)
            wait_read(sp, S, S.base["table"])
            sp.dma_start(scratch, rrow).then_inc(ld_bias, 16)
            sp.wait_ge(ld_bias, 16)
            for h in range(DIFF_HEADS):
                sp.dma_start(bias_up[:, h, :], bass.AP(scratch.tensor, h * 640, [[1, P], [1, T]]))\
                    .then_inc(ld_bias, 16)
            BB = plan.block_base

            def load_range(b0, b1):
                for b in range(b0, b1):
                    load_block(b)

            load_range(2, BB["proj_b0"])
            wait_group(sp, L, plan.events["fox"][1]["V", FOX_HEADS - 1, 0])
            load_mem(0)
            load_range(BB["proj_b0"], BB["mlp"] + 3)
            wait_group(sp, L, L.base["mlp"])
            sp.dma_start(pool_wt, A["pool_w_2"][0].rearrange("g p d -> p g d")).then_inc(ld_pw, 16)
            load_mem(1)
            load_range(BB["mlp"] + 3, BB["xo1"] + 2)
            wait_group(sp, L, plan.events["xa1"][1]["V", XA_HEADS - 1, 0] + 1)
            sp.dma_start(posi[64:96, :], A["positions_2"].to_broadcast([32, T])).then_inc(ld_pos, 16)
            load_range(BB["xo1"] + 2, BB["mla_o"] + 2)
            wait_group(sp, L, plan.events["mla1"][1]["V", 7, 0])
            load_mem(2)
            load_range(BB["mla_o"] + 2, NB)
            for j in range(8):
                wait_read(sp, L, L.base["out"] + j)
                sp.dma_start(out[0].rearrange("(t p) d -> p t d", p=P)[:, :, j * P:(j + 1) * P],
                             o_st[:, :, j * P:(j + 1) * P]).then_inc(st_out, 16)
            sp.wait_ge(st_out, 16 * 8)

        @block.gpsimd
        def _(pool):
            def low_range(b0, b1):
                for b in range(b0, b1):
                    if plan.low_by[b] == "p":
                        low_part(pool, b)

            def mlp_lows(name, n_up, nf):
                b, n, turns = plan.block_base[name] + n_up, 2 * (n_up + 1), (nf - 1) // 2
                low_range(b - n_up, b)

                def body(i):
                    for j in range(n):
                        low_part(pool, b + j, i, n)
                rep(pool, turns, body)
                low_range(b + turns * n, b - n_up + (n_up + 1) * nf)

            BB = plan.block_base
            low_range(0, BB["mlp"])
            mlp_lows("mlp", 1, FF1 // 256)
            low_range(BB["glu"], BB["ffn0"])
            mlp_lows("ffn0", 2, FF2 // 256)
            low_range(BB["dq"], BB["ffn1"])
            mlp_lows("ffn1", 2, FF2 // 256)

        @block.tensor
        def _(pe):
            def mm3(o, wh, wl, xh, xl, first, last, swap=False):
                for n, (w, v) in enumerate(((wh, xh), (wh, xl), (wl, xh))):
                    ins = pe.matmul(o, *((v, w) if swap else (w, v)), start=first and n == 0,
                                    stop=last and n == 2)
                return ins

            def wait_block(b, i=None, db=0):
                wait_low(pe, b, i, db)

            def feat(b, g, nk, c, xs, ready=None, i=None, db=0, dg=0, n=T, chunks=None):
                wait_block(b, i, db)
                h, l = wview(w_hi, b % 2, nk, c), wview(w_lo, b % 2, nk, c)
                chunks = chunks or [(P * q, P) for q in range(c // P)]

                def product(j, k):
                    c0, m = chunks[j]
                    xh, xl = xs(k)
                    ins = mm3(bank(L, g + j)[0:m, 0:n], h[:, k, c0:c0 + m], l[:, k, c0:c0 + m], xh, xl,
                              k == 0, k == nk - 1)
                    if k == nk - 1:
                        ins.then_inc(l_full, 1)

                if ready:
                    for j in range(len(chunks)):
                        claim(pe, L, g + j, i, dg)
                    for k in range(nk):
                        ready(k)
                        for j in range(len(chunks)):
                            product(j, k)
                else:
                    for j in range(len(chunks)):
                        claim(pe, L, g + j, i, dg)
                        for k in range(nk):
                            product(j, k)

            def tok(b, g, nk, c, xs, tiles):
                wait_block(b)
                h, l = wview(w_hi, b % 2, nk, c), wview(w_lo, b % 2, nk, c)
                for t in range(tiles):
                    claim(pe, L, g + t)
                    for k in range(nk):
                        xh, xl = xs(k)
                        q = slice(t * P, (t + 1) * P)
                        ins = mm3(bank(L, g + t)[:, 0:c], h[:, k, :], l[:, k, :], xh[:, q], xl[:, q],
                                  k == 0, k == nk - 1, swap=True)
                    ins.then_inc(l_full, 1)

            def xa(k):
                return A_hi[:, k, :], A_lo[:, k, :]

            def xb(k):
                return B_hi[:, k, :], B_lo[:, k, :]

            def xm(k):
                o = slice(MEM * (k % 2), MEM * (k % 2) + MEM)
                return B_hi[:, k // 2, o], B_lo[:, k // 2, o]

            def norm(k):
                g = S.base[f"norm{k}"]
                claim(pe, S, g)
                pe.wait_ge(n_acc, 6 * (k + 1))
                pe.matmul(bank(S, g)[:, :], avg[1024][:, :], acc, start=True, stop=False)
                pe.wait_ge(n_sq, 8 * (k + 1))
                pe.matmul(bank(S, g)[:, :], avg[1024][:, :], sq[:, 1, :], start=False, stop=True).then_inc(s_full, 1)

            def h_ready(k):
                return lambda c: pe.wait_ge(n_lo, n_base(k) + c + 1)

            def stage(name, xs, nk=8, c=256, nb=4, ready=None, n=T):
                b, g = plan.block_base[name], L.base[name]
                per = c // P
                for j in range(nb):
                    feat(b + j, g + per * j, nk, c, xs, ready if j == 0 else None, n=n)

            def turn(o, v):
                return pe.transpose(o, v, ident)

            pe.wait_ge(ld_keep, 16)
            g = L.base["x_in"]
            for c in range(KD):
                if c % 4 == 0:
                    pe.wait_ge(ld_x[c // 4], 16)
                claim(pe, L, g + c)
                for t in range(TT):
                    ins = turn(bank(L, g + c)[:, t * P:(t + 1) * P], x_st[:, t, c * P:(c + 1) * P])
                ins.then_inc(l_full, 1)
            pe.wait_ge(ld_vec, 16 * n_vec_dmas)
            g = S.base["vecs"]
            for t in range(VT):
                m = min(P, NCOL - t * P)
                pe.transpose(bank(S, g + t)[:, 0:m], v_st[0:m, t, :], ident[0:m, 0:m]).then_inc(s_full, 1)
            norm(0)
            g = S.base["table"]
            pe.wait_ge(ld_small, 16 * 7)
            pe.wait_ge(ld_once, 16)
            claim(pe, S, g)
            pe.matmul(bank(S, g)[0:4, :], rel, once[0:32, 256:768], start=True, stop=True).then_inc(s_full, 1)
            stage("qk_a", xa, ready=h_ready(0))
            g = S.base["flip"]
            pe.wait_ge(ld_bias, 16 * 5)
            for h in range(DIFF_HEADS):
                claim(pe, S, g + h)
                pe.matmul(bank(S, g + h)[:, :], once[:, 0:P], bias_up[:, h, :], start=True, stop=True)\
                    .then_inc(s_full, 1)
            stage("qk_b", xa)
            g = S.base["forget"]
            claim(pe, S, g)
            pe.wait_ge(setup_v, 5)
            for k in range(KD):
                ins = mm3(bank(S, g)[0:8, :], wf_hi[:, k, :], wf_lo[:, k, :], A_hi[:, k, :], A_lo[:, k, :],
                          k == 0, k == KD - 1)
            ins.then_inc(s_full, 1)
            b, g = plan.block_base["v_ab"], L.base["v_ab"]
            for j in range(4):
                tok(b + j, g + 4 * j, 8, 256, xa, TT)
            g = S.base["cum"]
            claim(pe, S, g)
            pe.wait_ge(cum_ready, 1)
            for t in range(TT):
                ins = pe.transpose(bank(S, g)[:, 8 * t:8 * t + 8], cum[:, t * P:(t + 1) * P], ident[0:8, 0:8])
            ins.then_inc(s_full, 1)

            def attention(name, score, values, before=None, turned=None, subln=None, keys=None):
                ev, at = plan.events[name]
                for kind, h, i in ev:
                    g = at[kind, h, i]
                    if kind == "K":
                        keys(g, h)
                    if kind == "S":
                        score(g, h, i)
                    if kind == "T":
                        turned(g, h, i)
                    if kind == "V":
                        values(g, h)
                    if kind == "M":
                        subln(g, h)

            def causal_turn(ubase, buf):
                def turned(g, h, i):
                    claim(pe, L, g)
                    u = TT * h + i
                    pe.wait_ge(u_p, ubase + u + 1)
                    for k in range(i + 1):
                        ins = turn(bank(L, g)[:, k * P:(k + 1) * P], buf(h, i)[:, k * P:(k + 1) * P])
                    ins.then_inc(l_full, 1)
                return turned

            def causal_values(name, rows, vt):
                at = plan.events[name][1]

                def values(g, h):
                    claim(pe, L, g)
                    wait_read(pe, L, at["T", h, TT - 1])
                    for k in range(TT):
                        ins = pe.matmul(bank(L, g)[rows(h), k * P:T], vt(h, k), pt(h)[:, k, k * P:T],
                                        start=k == 0, stop=k == TT - 1)
                    ins.then_inc(l_full, 1)
                return values

            def diff_score(g, h, i):
                if h == 0 and i == 0:
                    wait_read(pe, L, L.base["v_ab"] + 15)
                n = P * (i + 1)
                for s in (0, 1):
                    claim(pe, S, g + s)
                    r = slice(64 * s, 64 * s + 64)
                    pe.matmul(bank(S, g + s)[:, 0:n], qa[r, h, i * P:(i + 1) * P], ka[r, h, 0:n],
                              start=True, stop=True).then_inc(s_full, 1)

            def diff_subln(g, h):
                claim(pe, S, g)
                pe.wait_ge(sub_sq, h + 1)
                pe.matmul(bank(S, g)[:, :], avg[128][:, :], nck[:, h % 2, :], start=True, stop=True)\
                    .then_inc(s_full, 1)

            attention("diff", diff_score, causal_values("diff", lambda h: slice(0, P), lambda h, k: va[:, k, h * P:(h + 1) * P]),
                      turned=causal_turn(U["diff"], lambda h, i: s_diff(i, 0)), subln=diff_subln)

            def gates(tag, wait_first):
                for half in (0, 1):
                    stage(f"gate_{tag}{half}", xa, nb=2)
                    if half == 0:
                        wait_first()
                    stage(f"proj_{tag}{half}", xb, nk=4, c=512, nb=1)

            gates("a", lambda: pe.wait_ge(sub_lo, DIFF_HEADS))

            def fox_keys(g, h):
                claim(pe, S, g)
                pe.wait_ge(cum_ready, 2)
                pe.matmul(bank(S, g)[:, :], ident[0:8, h:h + 1].to_broadcast([8, P]), cum, start=True, stop=True)\
                    .then_inc(s_full, 1)

            def masked_score(g, i, pairs):
                n = P * (i + 1)
                claim(pe, S, g)
                for j, (q, k) in enumerate(pairs):
                    pe.matmul(bank(S, g)[:, 0:n], q, k[:, 0:n] if n < T else k, start=j == 0, stop=False)
                pe.matmul(bank(S, g)[:, i * P:n], ident_bf[:, :], mask_bf[:, :], start=False, stop=True)\
                    .then_inc(s_full, 1)

            def fox_score(g, h, i):
                r = slice(64 * (h % 2), 64 * (h % 2) + 64)
                masked_score(g, i, [(qb[r, h // 2, i * P:(i + 1) * P], kb[r, h // 2, :])])

            attention("fox", fox_score,
                      causal_values("fox", lambda h: slice(64 * (h % 2), 64 * (h % 2) + 64),
                                    lambda h, k: vb[:, k, h * 64:(h + 1) * 64]),
                      turned=causal_turn(U["fox"], lambda h, i: s_buf[:, i, :]), keys=fox_keys)
            gates("b", lambda: wait_read(pe, L, plan.events["fox"][1]["V", FOX_HEADS - 1, 0]))
            stage("w_o", xa, ready=lambda k: pe.wait_ge(m_lo, k + 1))

            def mem_turn(c):
                g = L.base[f"memT{c}"]
                pe.wait_ge(mem_sc, 2 * (c + 1))
                for q in range(4):
                    claim(pe, L, g + q)
                    for j in (0, 1):
                        for t in range(MT):
                            ins = turn(bank(L, g + q)[:, MEM * j + P * t:MEM * j + P * (t + 1)],
                                       mem_st[c][:, t, (2 * q + j) * P:(2 * q + j + 1) * P])
                    ins.then_inc(l_full, 1)

            def mem_keys(c):
                stage(f"xk{c}", xm, n=MEM, ready=lambda k: wait_read(pe, L, L.base[f"memT{c}"] + k // 2))

            def mem_values(c, j):
                tok(plan.block_base[f"xv{c}{j}"], L.base[f"xv{c}{j}"], 8, 256, xm, MT)

            def cross(c, k_norm):
                if c != 1:
                    mem_turn(c)
                    mem_keys(c)
                norm(k_norm)
                for j in range(2 if c == 1 else 0, 4):
                    mem_values(c, j)
                stage(f"xq{c}", xa, ready=h_ready(k_norm))
                at = plan.events[f"xa{c}"][1]

                def score(g, h, i):
                    claim(pe, S, g)
                    if i == 0:
                        wait_read(pe, L, L.base[f"xq{c}"] + 2 * h + 1)
                    for d in (0, 1):
                        ins = pe.matmul(bank(S, g)[:, 0:MEM], qT[:, 2 * h + d, i * P:(i + 1) * P],
                                        kT[:, 2 * h + d, :], start=d == 0, stop=d == 1)
                    ins.then_inc(s_full, 1)

                def turned(g, h, i):
                    claim(pe, L, g)
                    u = TT * h + i
                    pe.wait_ge(u_p, U[f"xa{c}"] + u + 1)
                    for m in range(MT):
                        ins = turn(bank(L, g)[:, m * P:(m + 1) * P], p_x[:, i, m * P:(m + 1) * P])
                    ins.then_inc(l_full, 1)

                def values(g, h):
                    wait_read(pe, L, at["T", h, TT - 1])
                    for d in (0, 1):
                        claim(pe, L, g + d)
                        for m in range(MT):
                            ins = pe.matmul(bank(L, g + d)[:, :], vM[:, m, h * 256 + d * P:h * 256 + (d + 1) * P],
                                            ptx(h)[:, m, :], start=m == 0, stop=m == MT - 1)
                        ins.then_inc(l_full, 1)

                attention(f"xa{c}", score, values, turned=turned)

                def o_ready(k):
                    wait_read(pe, L, at["V", k // 2, 0] + k % 2)
                stage(f"xo{c}", xa, ready=o_ready)

            def mlp(name, nf, n_up, k_norm, lo_base):
                b0, g0 = plan.block_base[name], L.base[name]
                nb, ng = n_up + 1, 2 * n_up + 8

                def ups(b, g, ready=None, i=None):
                    for j in range(n_up):
                        feat(b + j, g + 2 * j, 8, 256, xa, ready if j == 0 else None, i, 2 * nb, 2 * ng)

                def down(f, b, g, i=None):
                    pe.wait_ge(up_lo, lin(lambda r: lo_base + 2 * (f + 1) + 4 * r, i))
                    feat(b, g, 2, 1024, lambda k: xb(2 * (f % 2) + k), None, i, 2 * nb, 2 * ng)

                norm(k_norm)
                ups(b0, g0, h_ready(k_norm))
                pairs = (nf - 1) // 2

                def body(i):
                    for f in (0, 1):
                        b, g = b0 + n_up + nb * f, g0 + 2 * n_up + ng * f
                        ups(b, g, None, i)
                        down(f, b + n_up, g + 2 * n_up, i)
                rep(pe, pairs, body)
                for f in range(2 * pairs, nf):
                    b, g = b0 + n_up + nb * f, g0 + 2 * n_up + ng * f
                    if f + 1 < nf:
                        ups(b, g)
                        down(f, b + n_up, g + 2 * n_up)
                    else:
                        down(f, b, g)

            cross(0, 1)
            mlp("mlp", FF1 // 256, 1, 2, UPB["mlp"])
            norm(3)
            norm(4)
            stage("glu", xa, ready=h_ready(4))
            mem_turn(1)
            stage("pool_u", xa, nb=2)
            mem_keys(1)
            g = L.base["pool_w"]
            pe.wait_ge(ld_pw, 16)
            for q in range(4):
                claim(pe, L, g + q)
                pe.wait_ge(pool_r, q + 1)
                pe.matmul(bank(L, g + q)[:, :], pool_wt[:, q, :], pooled[:, q, :], start=True, stop=True)\
                    .then_inc(l_full, 1)
            stage("pc_out_a", lambda k: xa(4 + k), nk=4, c=512, nb=2,
                  ready=lambda k: wait_read(pe, L, L.base["pool_w"] + k))
            g = S.base["ln_mean"]
            claim(pe, S, g)
            pe.wait_ge(tap, TAPS)
            for q in range(4):
                ins = pe.matmul(bank(S, g)[:, :], avg[512][:, :], cvt[:, q, :], start=q == 0, stop=q == 3)
            ins.then_inc(s_full, 1)
            mem_values(1, 0)
            g = S.base["ln_var"]
            claim(pe, S, g)
            for q in range(4):
                pe.wait_ge(ln_sq, q + 1)
                ins = pe.matmul(bank(S, g)[:, :], avg[512][:, :], ly[:, q, :], start=q == 0, stop=q == 3)
            ins.then_inc(s_full, 1)
            mem_values(1, 1)
            stage("pc_out_b", xa, nk=4, c=512, nb=2, ready=lambda k: pe.wait_ge(yb_lo, k + 1))
            cross(1, 5)
            mlp("ffn0", FF2 // 256, 2, 6, UPB["ffn0"])
            norm(7)
            stage("dq", xa, nb=2, ready=h_ready(7))
            g = S.base["c_norm"]
            for j, n in enumerate((384, 256)):
                if j:
                    feat(plan.block_base["dq2"], L.base["dq2"], 8, 160, xa, chunks=[(0, P), (P, 32)])
                claim(pe, S, g + j)
                pe.wait_ge(c_acc, (2, 3)[j])
                pe.matmul(bank(S, g + j)[:, :], avg[n][:, :], cacc[:, j, :], start=True, stop=True)\
                    .then_inc(s_full, 1)
            for half in (0, 1):
                for j in (0, 1):
                    feat(plan.block_base[f"uq{half}{j}"], L.base[f"uq{half}{j}"], 3, 384, xa,
                         (lambda k: pe.wait_ge(c_lo, k + 1)), chunks=[(96 * q, 96) for q in range(4)])
                b, g = plan.block_base[f"uk{half}"], L.base[f"uk{half}"]
                wait_block(b)
                pe.wait_ge(c_lo, 5)
                h, l = wview(w_hi, b % 2, 2, 1024), wview(w_lo, b % 2, 2, 1024)
                for q in range(8):
                    claim(pe, L, g + q)
                    for k in (0, 1):
                        xh, xl = xa(3 + k)
                        ins = mm3(bank(L, g + q)[0:64, :], h[:, k, P * q:P * q + 64], l[:, k, P * q:P * q + 64],
                                  xh, xl, k == 0, k == 1)
                    ins.then_inc(l_full, 1)
                for t in range(TT):
                    claim(pe, L, g + 8 + t)
                    for k in (0, 1):
                        xh, xl = xa(3 + k)
                        q = slice(t * P, (t + 1) * P)
                        vh_ = h[:, k, :].rearrange("p (h c) -> p h c", c=P)[:, :, 64:P]
                        vl_ = l[:, k, :].rearrange("p (h c) -> p h c", c=P)[:, :, 64:P]
                        o = bank(L, g + 8 + t)[:, :].rearrange("p (h c) -> p h c", c=64)
                        ins = mm3(o, vh_, vl_, xh[:, q], xl[:, q], k == 0, k == 1, swap=True)
                    ins.then_inc(l_full, 1)
                at = plan.events[f"mla{half}"][1]

                def score(g, h, i, half=half):
                    if i == 0:
                        pe.wait_ge(rope_q, 2 * half + h // 4 + 1)
                        pe.wait_ge(kpe_put, half + 1)
                    if h == 0 and i == 0:
                        wait_read(pe, L, L.base[f"uk{half}"] + 11)
                    masked_score(g, i, [(qh[0:96, h, i * P:(i + 1) * P], kh[0:96, h, :])])

                attention(f"mla{half}", score,
                          causal_values(f"mla{half}", lambda h: slice(64 * (h % 2), 64 * (h % 2) + 64),
                                        lambda h, k: vh[:, k, h * 64:(h + 1) * 64]),
                          turned=causal_turn(U[f"mla{half}"], lambda h, i: s_buf[:, i, :]))

            def mo_ready(k):
                half, h = (0, 2 * k + 1) if k < 4 else (1, 2 * (k - 4) + 1)
                wait_read(pe, L, plan.events[f"mla{half}"][1]["V", h, 0])
            stage("mla_o", lambda k: xb(k) if k < 4 else xa(k - 4), ready=mo_ready)
            cross(2, 8)
            mlp("ffn1", FF2 // 256, 2, 9, UPB["ffn1"])
            norm(10)
            g = L.base["out"]
            for c in range(KD):
                claim(pe, L, g + c)
                pe.wait_ge(n_h, 8 * 10 + c + 1)
                for t in range(TT):
                    ins = turn(bank(L, g + c)[:, t * P:(t + 1) * P], h32[:, c % 2, t * P:(t + 1) * P])
                ins.then_inc(l_full, 1)

        @block.scalar
        def _(act):
            def hi(b, i=None, db=0):
                if b + (db * i if isinstance(i, int) else 0) >= NB:
                    return
                act.wait_ge(w_loaded[b % 2], lin(lambda r: 16 * ((b + r * db) // 2 + 1), i))
                if b >= 2:
                    act.wait_ge(l_full, lin(lambda r: plan.block_end[b - 2 + r * db], i))
                act.activation(w_hi[:, b % 2, :], w_raw[:, b % 2, :], ACT.Copy).then_inc(w_hi_made, 1)


            def block_copies(name, nb, per, dst, cols=T):
                g, b = L.base[name], plan.block_base[name]
                for j in range(nb):
                    for q in range(per):
                        wait_group(act, L, g + per * j + q)
                        act.activation(dst(per * j + q), bank(L, g + per * j + q)[:, 0:cols], ACT.Copy)\
                            .then_inc(l_free["a"], 1)
                    hi(b + j + 2)

            def just_hi(name, nb):
                for j in range(nb):
                    hi(plan.block_base[name] + j + 2)

            def square(k, n, g_x):
                wait_read(act, L, g_x + n)
                if n >= 2:
                    act.wait_ge(n_acc, 6 * k + max(1, n - 2))
                elif k:
                    wait_group(act, S, S.base[f"norm{k - 1}"])
                act.activation(sq[:, n % 2, :], x[:, n, :], ACT.Square).then_inc(n_sq, 1)

            def hi_and_squares(name, nb, k, last_hi=True):
                g, b, per = L.base[name], plan.block_base[name], KD // nb
                for j in range(nb):
                    last = j == nb - 1
                    for q in range(per if last else per - 1):
                        square(k, per * j + q, g)
                    if not last or last_hi:
                        hi(b + j + 2)
                    if not last:
                        square(k, per * j + per - 1, g)

            def norm_rstd(k, block=None):
                g = S.base[f"norm{k}"]
                act.activation(warm[:, k:k + 1], eps_col, ACT.Ln)
                wait_group(act, S, g)
                act.activation(rst, bank(S, g)[:, :], ACT.Ln, bias=eps_col).then_inc(s_free["a"], 1)
                wait_read(act, S, g)
                act.activation(rst, rst, ACT.Exp, scale=-0.5).then_inc(n_rstd, 1)
                if block is not None:
                    hi(block)

            def norm_hi(k, between=()):
                for n in range(KD):
                    act.wait_ge(n_h, 8 * k + n + 1)
                    act.activation(A_hi[:, n, :], h32[:, n % 2, :], ACT.Copy).then_inc(n_hi, 1)
                    if between and (n + 1) % (KD // len(between)) == 0:
                        between[n // (KD // len(between))]()

            act.wait_ge(setup_v, 2)
            for n in range(KD):
                if n in (3, 6):
                    hi(n // 3 - 1)
                square(0, n, L.base["x_in"])
            norm_rstd(0)
            norm_hi(0)
            act.wait_ge(ld_once, 16)
            act.activation(ident_bf[:, :], ident, ACT.Copy).then_inc(setup_a, 1)
            act.activation(mask_bf[:, :], once[:, P:2 * P], ACT.Copy).then_inc(setup_a, 1)
            act.wait_ge(setup_v, 9)
            act.activation(lam_t[:, 2:4], lam_t[:, 0:2], ACT.Exp).then_inc(setup_a, 1)
            block_copies("qk_a", 4, 2, lambda j: qa[:, j, :] if j < 4 else ka[:, j - 4, :])
            block_copies("qk_b", 4, 2, lambda j: qb[:, j, :] if j < 4 else kb[:, j - 4, :])

            act.wait_ge(forget_m, 3)
            act.activation(fe, fm, ACT.Exp).then_inc(forget_l, 1)
            act.wait_ge(forget_l, 1)
            act.activation(flg, fe, ACT.Ln, bias=1.0).then_inc(forget_l, 1)

            def v_dst(j):
                blk, t = divmod(j, 4)
                v = va if blk < 2 else vb
                return v[:, t, 256 * (blk % 2):256 * (blk % 2) + 256]
            block_copies("v_ab", 4, 4, v_dst, cols=256)
            def copies_of_turned(name, copy_tiles):
                def t(g, h, i):
                    wait_group(act, L, g)
                    u = plan.events[name][1]
                    if h >= 2:
                        act.wait_ge(l_full, u["V", h - 2, 0] + (2 if name[0] == "x" else 1))
                    copy_tiles(g, h, i)
                return t

            def causal_copy(g, h, i):
                tiles = bank(L, g)[:, 0:(i + 1) * P].rearrange("p (k q) -> p k q", q=P)
                act.activation(pt(h)[:, 0:i + 1, i * P:(i + 1) * P], tiles, ACT.Copy).then_inc(l_free["a"], 1)

            ev, at = plan.events["diff"]
            copy_turned = copies_of_turned("diff", causal_copy)
            for kind, h, i in ev:
                g = at[kind, h, i]
                if kind == "S":
                    n = P * (i + 1)
                    for s in (0, 1):
                        u = 2 * (TT * h + i) + s
                        act.wait_ge(u_nm, NM["diff"] + u + 1)
                        b_ = s_diff(i, s)
                        act.activation(b_, b_, ACT.Exp, bias=nm[:, u % 8:u % 8 + 1], scale=0.125,
                                       accum_out=ls[:, u % 8:u % 8 + 1]).then_inc(u_exp, 1)
                if kind == "T":
                    copy_turned(g, h, i)
                if kind == "O":
                    wait_group(act, L, g)
                    if h >= 2:
                        wait_group(act, S, at["M", h - 2, 0])
                    act.activation(nck[:, h % 2, :], bank(L, g)[:, :], ACT.Square).then_inc(sub_sq, 1)
                if kind == "N":
                    g = at["M", h, 0]
                    wait_group(act, S, g)
                    act.activation(nck[:, h % 2, :], bank(S, g)[:, :], ACT.Ln, bias=eps_col).then_inc(s_free["a"], 1)
                    wait_read(act, S, g)
                    act.activation(nck[:, h % 2, :], nck[:, h % 2, :], ACT.Exp, scale=-0.5).then_inc(sub_rs, 1)
                    wait_read(act, L, at["V", h, 0])
                    act.activation(B_hi[:, h, :], bias8[:, h, :], ACT.Copy).then_inc(o_hi, 1)

            def mem_rstd(c):
                act.wait_ge(ld_mem, 16 * (c + 1))
                for t in range(MT):
                    act.activation(mem_junk, mem_st[c][:, t, :], ACT.Square, accum_out=mem_s[:, t:t + 1])\
                        .then_inc(mem_ss, 1)
                    act.wait_ge(mem_ss, (MT + 1) * c + t + 1)
                act.activation(mem_s[:, 2:4], mem_s[:, 0:2], ACT.Ln, bias=eps_col, scale=1.0 / D).then_inc(mem_ss, 1)
                act.wait_ge(mem_ss, (MT + 1) * (c + 1))
                act.activation(mem_s[:, 4:6], mem_s[:, 2:4], ACT.Exp, scale=-0.5).then_inc(mem_rs, 1)
                act.wait_ge(mem_rs, c + 1)
                for t in range(MT):
                    act.activation(mem_st[c][:, t, :], mem_st[c][:, t, :], ACT.Copy, scale=mem_s[:, 4 + t:5 + t])\
                        .then_inc(mem_sc, 1)

            def gate_sigmoids(tag, half, ns):
                g, b = L.base[f"gate_{tag}{half}"], plan.block_base[f"gate_{tag}{half}"]
                if ns:
                    wait_read(act, L, L.base[ns] + 3)
                for j in range(4):
                    wait_group(act, L, g + j)
                    act.activation(sg[:, j, :], bank(L, g + j)[:, :], ACT.Sigmoid).then_inc(l_free["a"], 1)
                    if j % 2:
                        hi(b + j // 2 + 2)
                hi(plan.block_base[f"proj_{tag}{half}"] + 2)

            gate_sigmoids("a", 0, None)
            gate_sigmoids("a", 1, "proj_a0")

            ev, at = plan.events["fox"]
            copy_turned = copies_of_turned("fox", causal_copy)
            for kind, h, i in ev:
                g = at[kind, h, i]
                n = P * (i + 1)
                if kind == "S":
                    u = TT * h + i
                    act.wait_ge(u_nm, NM["fox"] + u + 1)
                    act.activation(s_buf[:, i, 0:n], s_buf[:, i, 0:n], ACT.Exp, bias=nm[:, u % 8:u % 8 + 1],
                                   scale=0.125, accum_out=ls[:, u % 8:u % 8 + 1]).then_inc(u_exp, 1)
                if kind == "T":
                    copy_turned(g, h, i)
                if kind == "O":
                    r = slice(64 * (h % 2), 64 * (h % 2) + 64)
                    wait_group(act, L, g)
                    if h == 0:
                        act.wait_ge(l_full, L.base["proj_a1"] + 4)
                    act.activation(B_hi[r, h // 2, :], bank(L, g)[r, :], ACT.Copy).then_inc(o_hi, 1)
            gate_sigmoids("b", 0, "proj_a1")
            mem_rstd(0)
            gate_sigmoids("b", 1, "proj_b0")
            act.wait_ge(l_full, L.base["gate_b1"] + 4)
            for n in range(KD):
                act.wait_ge(m_ready, n + 1)
                act.activation(A_hi[:, n, :], merged[:, n, :], ACT.Copy).then_inc(m_hi, 1)
            hi_and_squares("w_o", 4, 1)

            def mem_parts(c):
                g = L.base[f"memT{c}"]
                for n in range(KD):
                    wait_group(act, L, g + n // 2)
                    o = slice(MEM * (n % 2), MEM * (n % 2) + MEM)
                    act.activation(B_hi[:, n // 2, o], bank(L, g + n // 2)[:, o], ACT.Copy,
                                   scale=cols[:, GKV[c] + n:GKV[c] + n + 1]).then_inc(mem_hi, 1)

            def mem_keys(c):
                block_copies(f"xk{c}", 4, 2, lambda j: kT[:, j, :], cols=MEM)

            def mem_values(c, v):
                return lambda: block_copies(f"xv{c}{v}", 1, 2, lambda j: vM[:, j, 256 * v:256 * v + 256], cols=256)

            def cross(c, k_norm, after):
                if c != 1:
                    mem_parts(c)
                    mem_keys(c)
                norm_rstd(k_norm)
                norm_hi(k_norm, [mem_values(c, v) for v in range(2 if c == 1 else 0, 4)])
                block_copies(f"xq{c}", 4, 2, lambda j: qT[:, j, :])
                ev, at = plan.events[f"xa{c}"]

                def copy(g, h, i):
                    tiles = bank(L, g)[:, 0:MEM].rearrange("p (m q) -> p m q", q=P)
                    act.activation(ptx(h)[:, :, i * P:(i + 1) * P], tiles, ACT.Copy).then_inc(l_free["a"], 1)
                copy_turned = copies_of_turned(f"xa{c}", copy)
                for kind, h, i in ev:
                    g = at[kind, h, i]
                    if kind == "S":
                        u = TT * h + i
                        act.wait_ge(u_nm, NM[f"xa{c}"] + u + 1)
                        if u >= 4:
                            wait_group(act, L, at["T", (u - 4) // 4, i])
                        act.activation(p_x[:, i, :], bank(S, g)[:, 0:MEM], ACT.Exp, bias=nm[:, u % 8:u % 8 + 1],
                                       scale=1 / 16, accum_out=ls[:, u % 8:u % 8 + 1]).then_inc(s_free["a"], 1)
                    if kind == "T":
                        copy_turned(g, h, i)
                    if kind == "O":
                        for d in (0, 1):
                            wait_group(act, L, g + d)
                            act.activation(A_hi[:, 2 * h + d, :], bank(L, g + d)[:, :], ACT.Copy).then_inc(o_hi, 1)
                hi_and_squares(f"xo{c}", 4, after, last_hi=False)

            def mlp_up(f, b, g, ub, hb, i=None):
                for c in (0, 1):
                    wait_group(act, L, g + c, i, 20)
                    act.activation(r32[:, c, :], bank(L, g + c)[:, :], ACT.Relu).then_inc(l_free["a"], 1)
                hi(b + 2, i, 4)
                for c in (0, 1):
                    act.wait_ge(up_f, lin(lambda r: ub + 2 * f + c + 1 + 4 * r, i))
                    act.activation(B_hi[:, 2 * (f % 2) + c, :], f32[:, c, :], ACT.Copy).then_inc(up_hi, 1)

            def last_squares(name, k):
                for n in range(KD):
                    square(k, n, L.base[name + "_last"])

            def mlp(k_norm, after):
                b0, g0 = plan.block_base["mlp"], L.base["mlp"]
                norm_rstd(k_norm, b0 + 1)
                norm_hi(k_norm)
                u = UPB["mlp"]
                mlp_up(0, b0, g0, u, u)
                nf = FF1 // 256
                pairs = (nf - 1) // 2

                def body(i):
                    for f in (0, 1):
                        b, g = b0 + 1 + 2 * f, g0 + 2 + 10 * f
                        mlp_up(f + 1, b, g, u, u, i)
                        hi(b + 3, i, 4)
                rep(act, pairs, body)
                for f in range(2 * pairs, nf):
                    b, g = b0 + 1 + 2 * f, g0 + 2 + 10 * f
                    if f + 1 < nf:
                        mlp_up(f + 1, b, g, u, u)
                        hi(b + 3)
                    else:
                        last_squares("mlp", after)

            def ffn_up(f, b, g, cb, i=None):
                for c in (0, 1):
                    wait_group(act, L, g + c, i, 24)
                    if cb + 2 * f + c > 1:
                        act.wait_ge(g_conv, lin(lambda r: 3 * (cb + 2 * f + c - 1 + 4 * r), i))
                    act.activation(gp[:, c, 2:T + 2], bank(L, g + c)[:, :], ACT.Copy).then_inc(l_free["a"], 1)
                hi(b + 2, i, 6)
                for c in (0, 1):
                    act.wait_ge(g_conv, lin(lambda r: 3 * (cb + 2 * f + c + 1 + 4 * r), i))
                    act.activation(sl[:, c, :], cv[:, c, :], ACT.Silu).then_inc(up_act, 1)
                for c in (0, 1):
                    wait_read(act, L, g + 2 + c, i, 24)
                    act.activation(B_hi[:, 2 * (f % 2) + c, :], f32[:, c, :], ACT.Copy).then_inc(up_hi, 1)
                hi(b + 3, i, 6)

            def ffn(name, k_norm, after):
                b0, g0, cb = plan.block_base[name], L.base[name], CB[name]
                norm_rstd(k_norm, b0 + 1)
                norm_hi(k_norm)
                if name == "ffn0":
                    for n, t in enumerate((sinT, cosT)):
                        act.wait_ge(ang_r, n + 1)
                        act.activation(t[64:96, :], t[64:96, :], ACT.Sin).then_inc(sincos, 1)
                ffn_up(0, b0, g0, cb)
                nf = FF2 // 256

                def body(i):
                    for f in (0, 1):
                        b, g = b0 + 2 + 3 * f, g0 + 4 + 12 * f
                        ffn_up(f + 1, b, g, cb, i)
                        hi(b + 4, i, 6)
                rep(act, (nf - 1) // 2, body)
                last_squares(name, after)

            cross(0, 1, 2)
            mlp(2, 3)
            norm_rstd(3, plan.block_base["glu"] + 1)
            for n in range(KD):
                act.wait_ge(n_h, 8 * 3 + n + 1)
                if n >= 2:
                    act.wait_ge(n_acc, 6 * 4 + max(1, n - 2))
                act.activation(sq[:, n % 2, :], x[:, n, :], ACT.Square).then_inc(n_sq, 1)
            norm_rstd(4)
            norm_hi(4)
            mem_rstd(1)
            g, b = L.base["glu"], plan.block_base["glu"]
            for pair in (0, 1):
                for c in (0, 1):
                    wait_group(act, L, g + 4 * pair + c)
                    act.activation(gl[:, 2 * pair + c, CONV_K - 1:GW], bank(L, g + 4 * pair + c)[:, :], ACT.Copy)\
                        .then_inc(l_free["a"], 1)
                hi(b + 2 * pair + 2)
                if pair:
                    act.wait_ge(glu_r, 2)
                for c in (0, 1):
                    wait_group(act, L, g + 4 * pair + 2 + c)
                    act.activation(sgb[:, c, :], bank(L, g + 4 * pair + 2 + c)[:, :], ACT.Sigmoid)\
                        .then_inc(l_free["a"], 1)
                hi(b + 2 * pair + 3)
            mem_parts(1)
            block_copies("pool_u", 2, 2, lambda j: up_[:, j, 16:UW])
            mem_keys(1)
            for q in range(4):
                wait_group(act, L, L.base["pool_w"] + q)
                act.activation(A_hi[:, 4 + q, :], bank(L, L.base["pool_w"] + q)[:, :], ACT.Copy,
                               scale=cols[:, COL["pool_scale_2"] + q:COL["pool_scale_2"] + q + 1]).then_inc(ya_hi, 1)
            just_hi("pc_out_a", 2)
            for q in range(4):
                act.wait_ge(ln_v, q + 1)
                act.activation(ly[:, q, :], cvt[:, q, :], ACT.Square).then_inc(ln_sq, 1)
            mem_values(1, 0)()
            g = S.base["ln_var"]
            wait_group(act, S, g)
            act.activation(lrs, bank(S, g)[:, :], ACT.Ln, bias=eps_col).then_inc(s_free["a"], 1)
            wait_read(act, S, g)
            act.activation(lrs, lrs, ACT.Exp, scale=-0.5).then_inc(ln_rs, 1)
            for q in range(4):
                act.wait_ge(ln_y, q + 1)
                act.activation(ly[:, q, :], cvt[:, q, :], ACT.Silu,
                               bias=cols[:, COL["conv_ln_b_2"] + q:COL["conv_ln_b_2"] + q + 1]).then_inc(ln_s, 1)
            for q in range(4):
                act.wait_ge(ln_s, q + 1)
                act.activation(A_hi[:, q, :], ly[:, q, :], ACT.Copy).then_inc(yb_hi, 1)
            mem_values(1, 1)()
            hi_and_squares("pc_out_b", 2, 5)
            cross(1, 5, 6)
            ffn("ffn0", 6, 7)
            dq = plan.block_base["dq"]
            norm_rstd(7, dq + 1)
            norm_hi(7)

            def latent_squares(ns):
                for n in ns:
                    wait_read(act, L, L.base["dq"] + n)
                    if n >= 2:
                        act.wait_ge(c_acc, (1, 1, 2)[n - 2])
                    act.activation(h32[:, n % 2, :], cc[:, n, :], ACT.Square).then_inc(c_sq, 1)

            def latent_rstd(j):
                g = S.base["c_norm"] + j
                wait_group(act, S, g)
                act.activation(crst[:, j, :], bank(S, g)[:, :], ACT.Ln, bias=eps_col).then_inc(s_free["a"], 1)
                wait_read(act, S, g)
                act.activation(crst[:, j, :], crst[:, j, :], ACT.Exp, scale=-0.5).then_inc(c_rs, 1)

            hi(dq + 2)
            latent_squares((0, 1))
            hi(dq + 3)
            latent_squares((2, 3))
            latent_rstd(0)
            latent_squares((4,))
            hi(dq + 4)
            latent_rstd(1)
            for n in range(5):
                act.wait_ge(c_h, n + 1)
                act.activation(A_hi[:, n, :], cc[:, n, :], ACT.Copy).then_inc(c_hi, 1)
            for half in (0, 1):
                for j in (0, 1):
                    g = L.base[f"uq{half}{j}"]
                    if not half and not j:
                        act.wait_ge(c_lo, 5)
                    for q in range(4):
                        wait_group(act, L, g + q)
                        act.activation(qh[0:96, 4 * j + q, :], bank(L, g + q)[0:96, :], ACT.Copy)\
                            .then_inc(l_free["a"], 1)
                    hi(plan.block_base[f"uq{half}{j}"] + 2)
                act.wait_ge(rope_k, 1)
                act.activation(kh[64:96, :, :], kpe[64:96, :].unsqueeze(1).broadcast_to((32, 8, T)), ACT.Copy)\
                    .then_inc(kpe_put, 1)
                g = L.base[f"uk{half}"]
                for q in range(8):
                    wait_group(act, L, g + q)
                    act.activation(kh[0:64, q, :], bank(L, g + q)[0:64, :], ACT.Copy).then_inc(l_free["a"], 1)
                for t in range(TT):
                    wait_group(act, L, g + 8 + t)
                    act.activation(vh[:, t, :], bank(L, g + 8 + t)[:, :], ACT.Copy).then_inc(l_free["a"], 1)
                hi(plan.block_base[f"uk{half}"] + 2)
                name = f"mla{half}"
                ev, at = plan.events[name]
                copy_turned = copies_of_turned(name, causal_copy)
                for kind, h, i in ev:
                    g = at[kind, h, i]
                    n = P * (i + 1)
                    if kind == "S":
                        u = TT * h + i
                        act.wait_ge(u_nm, NM[name] + u + 1)
                        if u >= 4:
                            wait_group(act, L, at["T", h - 1, i])
                        act.activation(s_buf[:, i, 0:n], bank(S, g)[:, 0:n], ACT.Exp, bias=nm[:, u % 8:u % 8 + 1],
                                       scale=96.0 ** -0.5, accum_out=ls[:, u % 8:u % 8 + 1]).then_inc(s_free["a"], 1)
                    if kind == "T":
                        copy_turned(g, h, i)
                    if kind == "O":
                        r = slice(64 * (h % 2), 64 * (h % 2) + 64)
                        wait_group(act, L, g)
                        dst = A_hi if half else B_hi
                        act.activation(dst[r, h // 2, :], bank(L, g)[r, :], ACT.Copy).then_inc(o_hi, 1)
            mem_rstd(2)
            hi_and_squares("mla_o", 4, 8)
            cross(2, 8, 9)
            ffn("ffn1", 9, 10)
            norm_rstd(10)
            g = L.base["out"]
            for c in range(KD):
                wait_group(act, L, g + c)
                act.activation(o_st[:, :, c * P:(c + 1) * P],
                               bank(L, g + c)[:, :].rearrange("p (t d) -> p t d", t=TT), ACT.Copy)\
                    .then_inc(l_free["a"], 1)

        @block.vector
        def _(dve):
            steps = [0]

            def step(ins):
                steps[0] += 1
                ins.then_inc(v_step, 1)
                return steps[0]

            def sync():
                dve.wait_ge(v_step, steps[0])

            def col(name, n=0):
                return cols[:, COL[name] + n:COL[name] + n + 1]

            for n, a in avg.items():
                dve.memset(a[:, :], 1.0 / n)
            dve.memset(small[:, 48:64], 0.0).then_inc(setup_v, 1)
            dve.memset(eps_col, EPS).then_inc(setup_v, 1)
            dve.memset(rrow[:, 512:640], NEG).then_inc(setup_v, 1)
            def norm_acc(k, n):
                dve.wait_ge(n_sq, 8 * k + n + 1)
                if n > 1:
                    dve.wait_ge(n_acc, 6 * k + n - 1)
                elif k:
                    wait_group(dve, S, S.base[f"norm{k - 1}"])
                dve.tensor_tensor(acc, sq[:, 0, :] if n == 1 else acc, sq[:, n % 2, :], ALU.add).then_inc(n_acc, 1)

            def with_acc(k, part):
                for n in range(KD):
                    part(n)
                    if n >= 2:
                        norm_acc(k, n - 1)

            def norm_h(k, split=True, into_x=False, lows=()):
                gain = GAIN[k]
                dve.wait_ge(n_rstd, k + 1)

                def low(n):
                    dve.wait_ge(n_hi, n_base(k) + n + 1)
                    dve.tensor_tensor(A_lo[:, n, :], h32[:, n % 2, :], A_hi[:, n, :].bitcast(F32), ALU.subtract)\
                        .then_inc(n_lo, 1)
                for n in range(KD):
                    if not into_x and n >= 2:
                        if split:
                            dve.wait_ge(n_hi, n_base(k) + n - 1)
                            dve.wait_ge(n_lo, n_base(k) + n - 1)
                        else:
                            wait_group(dve, L, L.base["out"] + n - 2)
                    elif not into_x and n_base(k) and split:
                        dve.wait_ge(n_lo, n_base(k))
                    dve.scalar_tensor_tensor(out=x[:, n, :] if into_x else h32[:, n % 2, :], in0=x[:, n, :],
                                             scalar=cols[:, gain + n:gain + n + 1],
                                             in1=rst, op0=ALU.mult, op1=ALU.mult).then_inc(n_h, 1)
                    if into_x and n >= 2:
                        norm_acc(k + 1, n - 1)
                    for after, b in lows:
                        if after == n:
                            low_part(dve, b)
                    if split and n >= 1:
                        low(n - 1)
                if split:
                    low(KD - 1)

            def x_in(c):
                g = L.base["x_in"] + c
                wait_group(dve, L, g)
                dve.tensor_copy(x[:, c, :], bank(L, g)[:, :]).then_inc(l_free["v"], 1)

            with_acc(0, x_in)
            g = S.base["vecs"]
            for t in range(VT):
                m = min(P, NCOL - t * P)
                wait_group(dve, S, g + t)
                dve.tensor_copy(cols[:, t * P:t * P + m], bank(S, g + t)[:, 0:m]).then_inc(s_free["v"], 1)
            norm_h(0)
            g = S.base["table"]
            wait_group(dve, S, g)
            dve.tensor_scalar(rrow[:, 0:512], bank(S, g)[0:4, :], 8.0, None, ALU.mult).then_inc(s_free["v"], 1)
            dve.wait_ge(ld_small, 16 * 7)
            dve.tensor_copy(wf_hi[:, :, :], wf_raw[:, :, :]).then_inc(setup_v, 1)
            dve.wait_ge(setup_v, 4)
            dve.tensor_tensor(wf_lo[:, :, :], wf_raw[:, :, :], wf_hi[:, :, :].bitcast(F32), ALU.subtract)\
                .then_inc(setup_v, 1)
            for j in (0, 1):
                dve.tensor_tensor(lams[:, 2 * j, :], lams[:, 2 * j, :], lams[:, 2 * j + 1, :], ALU.mult)\
                    .then_inc(setup_v, 1)
            dve.wait_ge(setup_v, 7)
            for j in (0, 1):
                dve.reduce_sum(lam_t[:, j:j + 1], lams[:, 2 * j, :], AX_X).then_inc(setup_v, 1)
            g = S.base["flip"]
            for h in range(DIFF_HEADS):
                wait_group(dve, S, g + h)
                dve.tensor_copy(bias8[:, h, :], bank(S, g + h)[:, :]).then_inc(s_free["v"], 1)
            dve.wait_ge(setup_a, 3)
            step(dve.tensor_tensor(lam_t[:, 4:5], lam_t[:, 3:4], lam_t[:, 2:3], ALU.subtract))
            sync()
            step(dve.tensor_scalar(lam_neg, lam_t[:, 4:5], -LAMBDA_INIT, None, ALU.add))
            step(dve.tensor_scalar(g08, col("g_subln"), 1.0 - LAMBDA_INIT, None, ALU.mult))
            sync()
            g = S.base["forget"]
            wait_group(dve, S, g)
            dve.tensor_scalar(fz, bank(S, g)[0:8, :], bf_col, None, ALU.add).then_inc(s_free["v"], 1)
            wait_read(dve, S, g)
            dve.tensor_scalar(fmin, fz, 0.0, None, ALU.min).then_inc(forget_m, 1)
            dve.tensor_scalar(fone, fz, -1.0, None, ALU.mult).then_inc(forget_m, 1)
            dve.wait_ge(forget_m, 2)
            dve.tensor_tensor(fm, fz, fone, ALU.min).then_inc(forget_m, 1)
            dve.wait_ge(forget_m, 3)
            step(dve.memset(fone, 1.0))
            dve.wait_ge(forget_l, 2)
            step(dve.tensor_tensor(fmin, fmin, flg, ALU.subtract))
            sync()
            dve.tensor_tensor_scan(cum, fone, fmin, 0.0, ALU.mult, ALU.add).then_inc(cum_ready, 1)
            g = S.base["cum"]
            wait_group(dve, S, g)
            dve.tensor_scalar(ck8, bank(S, g)[:, 0:TT * 8], 8.0, None, ALU.mult).then_inc(s_free["v"], 1)
            dve.tensor_scalar(cum, cum, -8.0, None, ALU.mult).then_inc(cum_ready, 1)

            ev, at = plan.events["diff"]

            def combine(h, i):
                n = P * (i + 1)
                u = 2 * (TT * h + i)
                dve.wait_ge(u_exp, u + 2)
                a, b = u % 8, u % 8 + 1
                step(dve.reciprocal(rl[:, a:a + 2], ls[:, a:a + 2]))
                sync()
                step(dve.tensor_tensor(rl[:, b:b + 1], rl[:, b:b + 1], lam_neg, ALU.mult))
                p1, p2 = s_diff(i, 0), s_diff(i, 1)
                step(dve.tensor_scalar(p1, p1, rl[:, a:a + 1], None, ALU.mult))
                sync()
                dve.scalar_tensor_tensor(out=p1, in0=p2, scalar=rl[:, b:b + 1], in1=p1, op0=ALU.mult,
                                         op1=ALU.add).then_inc(u_p, 1)

            for kind, h, i in ev:
                g = at[kind, h, i]
                n = P * (i + 1)
                if kind == "S":
                    for s in (0, 1):
                        u = 2 * (TT * h + i) + s
                        wait_group(dve, S, g + s)
                        if h:
                            wait_group(dve, L, at["T", h - 1, i])
                        dve.tensor_tensor_reduce(s_diff(i, s), bank(S, g + s)[:, 0:n],
                                                 bias8[:, h, T - n:T], 1.0, -3e38, ALU.add, ALU.max,
                                                 mx[:, u % 8:u % 8 + 1]).then_inc(s_free["v"], 1)
                    for s in (0, 1):
                        u = 2 * (TT * h + i) + s
                        wait_read(dve, S, g + s)
                        dve.tensor_scalar(nm[:, u % 8:u % 8 + 1], mx[:, u % 8:u % 8 + 1], -0.125, None, ALU.mult)\
                            .then_inc(u_nm, 1)
                    if i or h:
                        combine(*divmod(TT * h + i - 1, TT))
                    if (h, i) == (DIFF_HEADS - 1, TT - 1):
                        combine(h, i)
                if kind == "N":
                    dve.wait_ge(sub_rs, h + 1)
                    gv = at["V", h, 0]
                    wait_group(dve, L, gv)
                    dve.scalar_tensor_tensor(out=bias8[:, h, :], in0=bank(L, gv)[:, :], scalar=g08,
                                             in1=nck[:, h % 2, :], op0=ALU.mult, op1=ALU.mult)\
                        .then_inc(l_free["v"], 1)
                    wait_read(dve, L, gv)
                    dve.wait_ge(o_hi, h + 1)
                    dve.tensor_tensor(B_lo[:, h, :], bias8[:, h, :], B_hi[:, h, :].bitcast(F32), ALU.subtract)\
                        .then_inc(sub_lo, 1)

            def gates(tag, half):
                g = L.base[f"proj_{tag}{half}"]
                for j in range(4):
                    n = 4 * half + j
                    wait_read(dve, L, L.base[f"gate_{tag}{half}"] + j)
                    wait_group(dve, L, g + j)
                    dst = merged[:, n, :] if tag == "a" else s_buf[:, j, :]
                    dve.tensor_tensor(dst, bank(L, g + j)[:, :], sg[:, j, :], ALU.mult).then_inc(l_free["v"], 1)
                    if tag == "b":
                        wait_read(dve, L, g + j)
                        dve.tensor_tensor(merged[:, n, :], merged[:, n, :], s_buf[:, j, :], ALU.add)\
                            .then_inc(m_ready, 1)

            gates("a", 0)
            gates("a", 1)

            def plain_norm(name, exp_done, buf, width, h, i):
                u = TT * h + i
                exp_done(h, i)
                a = u % 8
                step(dve.reciprocal(rl[:, a:a + 1], ls[:, a:a + 1]))
                sync()
                dve.tensor_scalar(buf[:, i, 0:width(i)], buf[:, i, 0:width(i)], rl[:, a:a + 1], None, ALU.mult)\
                    .then_inc(u_p, 1)

            def walk(name, heads, scores, exp_done, buf, width, values, keys=None):
                ev, at = plan.events[name]
                for kind, h, i in ev:
                    g = at[kind, h, i]
                    if kind == "K":
                        keys(g, h)
                    if kind == "S":
                        scores(g, h, i)
                        if h or i:
                            plain_norm(name, exp_done, buf, width, *divmod(TT * h + i - 1, TT))
                        if (h, i) == (heads - 1, TT - 1):
                            plain_norm(name, exp_done, buf, width, h, i)
                    if kind == "P":
                        values(g, h)

            at_fox = plan.events["fox"][1]

            def fox_keys(g, h):
                wait_group(dve, S, g)
                dve.tensor_copy(nck[:, h % 2, :], bank(S, g)[:, :]).then_inc(s_free["v"], 1)
                wait_read(dve, S, g)

            def fox_scores(g, h, i):
                n, u = P * (i + 1), TT * h + i
                wait_group(dve, S, g)
                if h:
                    wait_group(dve, L, at_fox["T", h - 1, i])
                dve.scalar_tensor_tensor(out=s_buf[:, i, 0:n], in0=bank(S, g)[:, 0:n],
                                         scalar=ck8[:, 8 * i + h:8 * i + h + 1], in1=nck[:, h % 2, 0:n],
                                         op0=ALU.add, op1=ALU.add).then_inc(s_free["v"], 1)
                wait_read(dve, S, g)
                step(dve.reduce_max(mx[:, u % 8:u % 8 + 1], s_buf[:, i, 0:n], AX_X))
                sync()
                dve.tensor_scalar(nm[:, u % 8:u % 8 + 1], mx[:, u % 8:u % 8 + 1], -0.125, None, ALU.mult)\
                    .then_inc(u_nm, 1)

            def half_values(name, hi_t, lo_t):
                def values(g, h):
                    r = slice(64 * (h % 2), 64 * (h % 2) + 64)
                    wait_group(dve, L, g)
                    dve.wait_ge(o_hi, OH[name] + h + 1)
                    dve.tensor_tensor(lo_t[r, h // 2, :], bank(L, g)[r, :], hi_t[r, h // 2, :].bitcast(F32),
                                      ALU.subtract).then_inc(l_free["v"], 1)
                return values

            walk("fox", FOX_HEADS, fox_scores, lambda h, i: dve.wait_ge(u_exp, 32 + TT * h + i + 1),
                 s_buf, lambda i: P * (i + 1), half_values("fox", B_hi, B_lo), keys=fox_keys)

            gates("b", 0)
            gates("b", 1)
            for n in range(KD):
                dve.wait_ge(m_hi, n + 1)
                dve.tensor_tensor(A_lo[:, n, :], merged[:, n, :], A_hi[:, n, :].bitcast(F32), ALU.subtract)\
                    .then_inc(m_lo, 1)

            r = slice(64, 96)

            def angle_steps():
                dve.wait_ge(ld_pos, 16)
                step(dve.tensor_copy(ang[r, :], posi[r, :]))
                sync()
                yield
                step(dve.tensor_scalar(ang[r, :], ang[r, :], keep[r, P + 64:P + 65], None, ALU.mult))
                sync()
                yield
                for dst, quarter, shift in ((sinT, 0.0, 0.0), (cosT, 0.25, float(np.pi / 2))):
                    step(dve.tensor_scalar(nrn[r, :], ang[r, :], float(np.float32(1 / (2 * np.pi))), quarter,
                                           ALU.mult, ALU.add))
                    sync()
                    step(dve.tensor_scalar(nrn[r, :], nrn[r, :], ROUND, None, ALU.add))
                    sync()
                    yield
                    step(dve.tensor_scalar(nrn[r, :], nrn[r, :], -ROUND, None, ALU.add))
                    sync()
                    src = ang
                    for part in TWO_PI:
                        step(dve.scalar_tensor_tensor(out=dst[r, :], in0=nrn[r, :], scalar=-float(part),
                                                      in1=src[r, :], op0=ALU.mult, op1=ALU.add))
                        sync()
                        src = dst
                        if part != TWO_PI[1]:
                            yield
                    step(dve.tensor_scalar(dst[r, :], dst[r, :], shift, PI32, ALU.add, ALU.min))
                    sync()
                    dve.tensor_scalar(dst[r, :], dst[r, :], -PI32, None, ALU.max).then_inc(ang_r, 1)

            def residual(g, k, fill=iter(())):
                def add(n):
                    if n:
                        next(fill, None)
                    wait_group(dve, L, g + n)
                    dve.tensor_tensor(x[:, n, :], bank(L, g + n)[:, :], x[:, n, :], ALU.add).then_inc(l_free["v"], 1)
                wait_read(dve, L, g - 1)
                with_acc(k, add)
                for _ in fill:
                    pass

            def mem_keys(c):
                g = L.base[f"memT{c}"]
                for n in range(KD):
                    wait_group(dve, L, g + n // 2)
                    dve.wait_ge(mem_hi, 8 * c + 2 * (n // 2) + 2)
                    o = slice(MEM * (n % 2), MEM * (n % 2) + MEM)
                    ins = dve.scalar_tensor_tensor(
                        out=B_lo[:, n // 2, o], in0=bank(L, g + n // 2)[:, o],
                        scalar=cols[:, GKV[c] + n:GKV[c] + n + 1], in1=B_hi[:, n // 2, o].bitcast(F32),
                        op0=ALU.mult, op1=ALU.subtract)
                    if n % 2:
                        ins.then_inc(l_free["v"], 1)

            def cross(c, k_norm, after):
                b = plan.block_base[f"xv{c}2"]
                if c == 1:
                    low_part(dve, b)
                    norm_h(k_norm, lows=[(1, b + 1)])
                else:
                    mem_keys(c)
                    for early in range(4):
                        low_part(dve, b - 4 + early)
                    norm_h(k_norm, lows=[(3, b), (6, b + 1)])
                name = f"xa{c}"
                at = plan.events[name][1]

                def scores(g, h, i):
                    u = TT * h + i
                    wait_group(dve, S, g)
                    step(dve.reduce_max(mx[:, u % 8:u % 8 + 1], bank(S, g)[:, 0:MEM], AX_X))
                    sync()
                    dve.tensor_scalar(nm[:, u % 8:u % 8 + 1], mx[:, u % 8:u % 8 + 1], -1 / 16, None, ALU.mult)\
                        .then_inc(u_nm, 1)

                def values(g, h):
                    for d in (0, 1):
                        wait_group(dve, L, g + d)
                        dve.wait_ge(o_hi, OH[name] + 2 * h + d + 1)
                        dve.tensor_tensor(A_lo[:, 2 * h + d, :], bank(L, g + d)[:, :],
                                          A_hi[:, 2 * h + d, :].bitcast(F32), ALU.subtract).then_inc(l_free["v"], 1)

                walk(name, XA_HEADS, scores, lambda h, i: wait_read(dve, S, at["S", h, i]), p_x, lambda i: MEM, values)
                residual(L.base[f"xo{c}"], after, *([angle_steps()] if c == 1 else []))

            residual(L.base["w_o"], 1)
            cross(0, 1, 2)

            def mlp():
                b = L.base["mlp"]
                nf, ub = FF1 // 256, UPB["mlp"]

                def up(f, g, i=None):
                    for c in (0, 1):
                        wait_read(dve, L, g + c, i, 20)
                        if f or i is not None:
                            dve.wait_ge(up_lo, lin(lambda r: ub + 2 * f + c - 1 + 4 * r, i))
                        dve.tensor_tensor(f32[:, c, :], r32[:, c, :], r32[:, c, :], ALU.mult).then_inc(up_f, 1)
                    for c in (0, 1):
                        dve.wait_ge(up_f, lin(lambda r: ub + 2 * f + c + 1 + 4 * r, i))
                        dve.wait_ge(up_hi, lin(lambda r: ub + 2 * f + c + 1 + 4 * r, i))
                        dve.tensor_tensor(B_lo[:, 2 * (f % 2) + c, :], f32[:, c, :],
                                          B_hi[:, 2 * (f % 2) + c, :].bitcast(F32), ALU.subtract).then_inc(up_lo, 1)

                norm_h(2)
                up(0, b)
                pairs = (nf - 1) // 2

                def body(i):
                    for f in (0, 1):
                        g = b + 2 + 10 * f
                        up(f + 1, g, i)
                        residual_loop(g + 2, i, 20)

                def residual_loop(g, i, dg):
                    for n in range(KD):
                        wait_group(dve, L, g + n, i, dg)
                        dve.tensor_tensor(x[:, n, :], bank(L, g + n)[:, :], x[:, n, :], ALU.add)\
                            .then_inc(l_free["v"], 1)
                    wait_read(dve, L, g + 7, i, dg)
                rep(dve, pairs, body)
                for f in range(2 * pairs, nf):
                    g = b + 2 + 10 * f
                    if f + 1 < nf:
                        up(f + 1, g)
                        residual_loop(g + 2, None, 0)
                    else:
                        residual(g, 3)

            mlp()
            norm_h(3, split=False, into_x=True)
            dve.wait_ge(n_h, 8 * 4)
            norm_h(4)
            step(dve.memset(gl[:, :, 0:CONV_K - 1], 0.0))
            step(dve.memset(up_[:, :, 0:16], 0.0))
            sync()

            def glu(pair):
                for c in (0, 1):
                    q = 2 * pair + c
                    wait_read(dve, L, L.base["glu"] + 4 * pair + 2 + c)
                    dve.tensor_tensor(gl[:, q, CONV_K - 1:GW], gl[:, q, CONV_K - 1:GW], sgb[:, c, :], ALU.mult)\
                        .then_inc(glu_r, 1)
                dve.wait_ge(glu_r, 2 * pair + 2)

            tap_n = [0]

            def taps(count):
                for k in range(tap_n[0], min(tap_n[0] + count, TAPS)):
                    j, c = divmod(k % (2 * CONV_K), 2)
                    q = 2 * (k // (2 * CONV_K)) + c
                    w = col("conv_dw_w_2", 4 * j + q)
                    if j == 0:
                        ins = dve.tensor_scalar(cvt[:, q, :], gl[:, q, 0:T], w, col("conv_dw_b_2", q), ALU.mult, ALU.add)
                    else:
                        dve.wait_ge(tap, k - 1)
                        ins = dve.scalar_tensor_tensor(out=cvt[:, q, :], in0=gl[:, q, j:j + T], scalar=w,
                                                       in1=cvt[:, q, :], op0=ALU.mult, op1=ALU.add)
                    ins.then_inc(tap, 1)
                tap_n[0] = min(tap_n[0] + count, TAPS)

            glu(0)
            taps(CONV_K)
            glu(1)
            mem_keys(1)
            taps(CONV_K - 3)
            for q, w in enumerate(WINDOWS):
                wait_read(dve, L, L.base["pool_u"] + q)
                src, st, d = up_[:, q, :], 0, 1
                for n in range(q + 1):
                    st += d
                    dst = (pw_a, pw_b)[n % 2]
                    step(dve.tensor_tensor(dst[:, st:UW], src[:, st:UW], src[:, st - d:UW - d], ALU.add))
                    sync()
                    src, d = dst, 2 * d
                step(dve.scalar_tensor_tensor(out=pooled[:, q, :], in0=src[:, 16:UW], scalar=1.0 / w,
                                              in1=up_[:, q, 16:UW], op0=ALU.mult, op1=ALU.subtract))
                step(dve.tensor_tensor(ptmp, src[:, 16:32], keep[:, P + 16 * q:P + 16 * q + 16], ALU.mult))
                sync()
                dve.tensor_tensor(pooled[:, q, 0:16], ptmp, up_[:, q, 16:32], ALU.subtract).then_inc(pool_r, 1)
                dve.wait_ge(pool_r, q + 1)
            taps(26)
            for q in range(4):
                g = L.base["pool_w"] + q
                wait_group(dve, L, g)
                dve.wait_ge(ya_hi, q + 1)
                dve.scalar_tensor_tensor(out=A_lo[:, 4 + q, :], in0=bank(L, g)[:, :], scalar=col("pool_scale_2", q),
                                         in1=A_hi[:, 4 + q, :].bitcast(F32), op0=ALU.mult, op1=ALU.subtract)\
                    .then_inc(l_free["v"], 1)
            for n in range(KD):
                taps(5)
                g = L.base["pc_out_a"] + n
                wait_group(dve, L, g)
                dve.tensor_tensor(x[:, n, :], bank(L, g)[:, :], x[:, n, :], ALU.add).then_inc(l_free["v"], 1)
            taps(TAPS)
            g = S.base["ln_mean"]
            wait_group(dve, S, g)
            dve.tensor_copy(lmu, bank(S, g)[:, :]).then_inc(s_free["v"], 1)
            wait_read(dve, S, g)
            for q in range(4):
                dve.tensor_tensor(cvt[:, q, :], cvt[:, q, :], lmu, ALU.subtract).then_inc(ln_v, 1)
            dve.wait_ge(ln_v, 4)
            dve.wait_ge(ln_rs, 1)
            for q in range(4):
                dve.scalar_tensor_tensor(out=cvt[:, q, :], in0=cvt[:, q, :], scalar=col("conv_ln_g_2", q), in1=lrs,
                                         op0=ALU.mult, op1=ALU.mult).then_inc(ln_y, 1)
            for q in range(4):
                dve.wait_ge(yb_hi, q + 1)
                dve.tensor_tensor(A_lo[:, q, :], ly[:, q, :], A_hi[:, q, :].bitcast(F32), ALU.subtract)\
                    .then_inc(yb_lo, 1)
            wait_read(dve, L, L.base["pc_out_a"] + 7)
            residual(L.base["pc_out_b"], 5)
            cross(1, 5, 6)

            def ffn(name, layer, k_norm, after):
                b, cb, ub = L.base[name], CB[name], UPB[name]
                cw, cbias = COL["ffn_conv_w_2"] + 66 * layer, COL["ffn_conv_b_2"] + 22 * layer

                def wcol(base, n, i):
                    if i is None or isinstance(i, int):
                        n += 4 * (i or 0)
                        return cols[:, base + n:base + n + 1]
                    return cols[:, bass.ds(base + n + 4 * i, 1)]

                def up(f, g, i=None):
                    for c in (0, 1):
                        k = 2 * f + c
                        wait_read(dve, L, g + c, i, 24)
                        if cb + k > 1:
                            dve.wait_ge(up_act, lin(lambda r: cb + k - 1 + 4 * r, i))
                        dve.tensor_scalar(cv[:, c, :], gp[:, c, 2:T + 2], wcol(cw + 44, k, i), wcol(cbias, k, i),
                                          ALU.mult, ALU.add).then_inc(g_conv, 1)
                        for j in (1, 0):
                            dve.wait_ge(g_conv, lin(lambda r: 3 * (cb + k + 4 * r) + 2 - j, i))
                            dve.scalar_tensor_tensor(out=cv[:, c, :], in0=gp[:, c, j:T + j],
                                                     scalar=wcol(cw + 22 * j, k, i), in1=cv[:, c, :],
                                                     op0=ALU.mult, op1=ALU.add).then_inc(g_conv, 1)
                    for c in (0, 1):
                        k = 2 * f + c
                        wait_group(dve, L, g + 2 + c, i, 24)
                        dve.wait_ge(up_act, lin(lambda r: cb + k + 1 + 4 * r, i))
                        if k > 1:
                            dve.wait_ge(up_lo, lin(lambda r: ub + k - 1 + 4 * r, i))
                        dve.tensor_tensor(f32[:, c, :], bank(L, g + 2 + c)[:, :], sl[:, c, :], ALU.mult)\
                            .then_inc(l_free["v"], 1)
                    for c in (0, 1):
                        k = 2 * f + c
                        wait_read(dve, L, g + 2 + c, i, 24)
                        dve.wait_ge(up_hi, lin(lambda r: ub + k + 1 + 4 * r, i))
                        dve.tensor_tensor(B_lo[:, 2 * (f % 2) + c, :], f32[:, c, :],
                                          B_hi[:, 2 * (f % 2) + c, :].bitcast(F32), ALU.subtract).then_inc(up_lo, 1)

                def down(g, i=None):
                    for n in range(KD):
                        wait_group(dve, L, g + n, i, 24)
                        dve.tensor_tensor(x[:, n, :], bank(L, g + n)[:, :], x[:, n, :], ALU.add)\
                            .then_inc(l_free["v"], 1)
                    wait_read(dve, L, g + 7, i, 24)

                norm_h(k_norm)
                step(dve.memset(gp[:, :, 0:2], 0.0))
                sync()
                up(0, b)
                nf = FF2 // 256

                def body(i):
                    for f in (0, 1):
                        g = b + 4 + 12 * f
                        up(f + 1, g, i)
                        down(g + 4, i)
                rep(dve, (nf - 1) // 2, body)
                residual(b + 4 + 12 * (nf - 1), after)

            ffn("ffn0", 0, 6, 7)
            norm_h(7)

            def latent(n):
                wait_group(dve, L, L.base["dq"] + n)
                dve.tensor_copy(cc[:, n, :], bank(L, L.base["dq"] + n)[:, :]).then_inc(l_free["v"], 1)
                if n in (1, 2, 4):
                    dve.wait_ge(c_sq, n + 1)
                    if n == 2:
                        dve.wait_ge(c_acc, 1)
                    a = n // 4
                    dve.tensor_tensor(cacc[:, a, :], cacc[:, a, :] if n == 2 else h32[:, (n - 1) % 2, :],
                                      h32[:, n % 2, :], ALU.add).then_inc(c_acc, 1)

            def latent_h(j, ns):
                dve.wait_ge(c_rs, j + 1)
                for n in ns:
                    gcol = col("mla_kv_norm_g_2", n - 3) if j else col("mla_q_norm_g_2", n)
                    dve.scalar_tensor_tensor(out=cc[:, n, :], in0=cc[:, n, :], scalar=gcol, in1=crst[:, j, :],
                                             op0=ALU.mult, op1=ALU.mult).then_inc(c_h, 1)

            for n in range(4):
                latent(n)
            latent_h(0, range(3))
            latent(4)
            g = L.base["dq2"] + 1
            wait_group(dve, L, g)
            dve.tensor_copy(kpe[r, :], bank(L, g)[0:32, :]).then_inc(l_free["v"], 1)
            latent_h(1, (3, 4))
            dve.wait_ge(sincos, 2)
            step(dve.tensor_scalar(sinT[r, :], sinT[r, :], keep[r, P + 65:P + 66], None, ALU.mult))
            SWAP = [16 + q for q in range(16)] + list(range(16))

            def rope(v, n, done):
                turned = rsh[r, 0:n, :]
                cos, sin = (t[r, :].unsqueeze(1).broadcast_to((32, n, T)) for t in (cosT, sinT))
                step(dve.stream_shuffle(turned, v, SWAP))
                sync()
                step(dve.tensor_tensor(v, v, cos, ALU.mult))
                step(dve.tensor_tensor(turned, turned, sin, ALU.mult))
                sync()
                dve.tensor_tensor(v, v, turned, ALU.add).then_inc(done, 1)

            wait_read(dve, L, g)
            for n in range(5):
                dve.wait_ge(c_hi, n + 1)
                dve.tensor_tensor(A_lo[:, n, :], cc[:, n, :], A_hi[:, n, :].bitcast(F32), ALU.subtract)\
                    .then_inc(c_lo, 1)
            rope(kpe[r, :].unsqueeze(1), 1, rope_k)
            for half in (0, 1):
                for j in (0, 1):
                    wait_read(dve, L, L.base[f"uq{half}{j}"] + 3)
                    if j or half:
                        dve.wait_ge(rope_q, 2 * half + j)
                    else:
                        dve.wait_ge(rope_k, 1)
                    rope(qh[r, 4 * j:4 * j + 4, :], 4, rope_q)
                name = f"mla{half}"
                at = plan.events[name][1]

                def scores(g, h, i):
                    u, n = TT * h + i, P * (i + 1)
                    wait_group(dve, S, g)
                    step(dve.reduce_max(mx[:, u % 8:u % 8 + 1], bank(S, g)[:, 0:n], AX_X))
                    sync()
                    dve.tensor_scalar(nm[:, u % 8:u % 8 + 1], mx[:, u % 8:u % 8 + 1], -96.0 ** -0.5, None, ALU.mult)\
                        .then_inc(u_nm, 1)

                walk(name, 8, scores, lambda h, i, at=at: wait_read(dve, S, at["S", h, i]), s_buf,
                     lambda i: P * (i + 1), half_values(name, *((A_hi, A_lo) if half else (B_hi, B_lo))))
            residual(L.base["mla_o"], 8)
            cross(2, 8, 9)
            ffn("ffn1", 1, 9, 10)
            norm_h(10, split=False)


_INS = [
    "x", "mem", "w_in", "b_forget", "lambda_q1", "lambda_k1", "lambda_q2", "lambda_k2", "g_subln", "rel_bias",
    "w_diff_out", "w_fox_out", "w_o", "g_mix", "g_mem_q", "g_mem_kv", "w_q_mem", "w_kv_mem", "w_o_mem", "g_mlp",
    "w1", "w2", "g_final", "mem_2", "positions_2", "norm_mix_g_2", "norm_xa_g_2", "norm_mem_g_2", "xa_wq_2",
    "xa_wkv_2", "xa_wo_2", "norm_ffn_g_2", "ffn_w_up_2", "ffn_conv_w_2", "ffn_conv_b_2", "ffn_w_down_2",
    "pc_w_in_2", "pool_w_2", "pool_scale_2", "conv_dw_w_2", "conv_dw_b_2", "conv_ln_g_2", "conv_ln_b_2",
    "pc_w_out_2", "mla_w_dq_dkv_2", "mla_q_norm_g_2", "mla_w_uq_2", "mla_kv_norm_g_2", "mla_w_ukv_2",
    "mla_w_o_2", "final_norm_g_2",
]


def kernel(**inputs):
    import numpy as _np
    import concourse.bacc as _bacc
    from concourse import mybir as _mybir
    from concourse.bass_utils import run_bass_kernel_spmd as _run

    nc = _bacc.Bacc("TRN2", target_bir_lowering=False, num_devices=1)
    arrays, aps = {}, {}
    for name in _INS:
        a = _np.ascontiguousarray(inputs[name])
        arrays[f"in_{name}_dram"] = a
        aps[name] = nc.dram_tensor(f"in_{name}_dram", a.shape, _mybir.dt.from_np(a.dtype), kind="ExternalInput").ap()
    out = nc.dram_tensor("out_0_dram", (1, T, D), _mybir.dt.float32, kind="ExternalOutput").ap()
    build(nc, aps, out)
    r = _run(nc, [arrays], core_ids=[0])
    return r.results[0]["out_0_dram"]
```
